# Optimizing a Trainium2 kernel written in Bass

```python
import math
import jax, jax.numpy as jnp
from jax import lax
import numpy as np

D_MODEL = 1024
BATCH = 1
SEQ = 512
DEPTH = 1

D_MIX = D_MODEL
HGRN_W = D_MIX // 2
CONV_W = D_MIX - HGRN_W
HGRN_HEADS = 4
HGRN_DV = HGRN_W // HGRN_HEADS
HGRN_DK = 128
HGRN_F = HGRN_HEADS * HGRN_DK
CONV_GROUPS = 8
CONV_K = 3
CHUNK = 64
MEM_LEN = 256
MEM_HEADS = 4
MEM_HD = D_MODEL // MEM_HEADS
D_FF = int(math.ceil(8 * D_MODEL / 3 / 256) * 256)
EPS = 1e-6
IN_COLS = 3 * HGRN_F // HGRN_F * 0 + HGRN_F + HGRN_F + HGRN_W + HGRN_W + 3 * CONV_W


def rms_norm(x, g):
    xf = x.astype(jnp.float32)
    y = xf * lax.rsqrt(jnp.mean(xf * xf, axis=-1, keepdims=True) + EPS)
    return (y * g.astype(jnp.float32)).astype(x.dtype)

def swiglu(h, w_gate, w_up, w_down):
    return (jax.nn.silu(h @ w_gate) * (h @ w_up)) @ w_down

def hgrn2_chunkwise(q, k, v, logf):
    b_, s_, h_, dk = q.shape
    dv = v.shape[-1]
    n = s_ // CHUNK

    def to_chunks(t):
        return t.astype(jnp.float32).reshape(b_, n, CHUNK, h_, t.shape[-1]).transpose(1, 0, 3, 2, 4)

    qc, kc, vc, lc = to_chunks(q), to_chunks(k), to_chunks(v), to_chunks(logf)
    bc = jnp.cumsum(lc, axis=-2)
    causal = jnp.tril(jnp.ones((CHUNK, CHUNK), dtype=bool))[None, None, :, :, None]

    def step(state, inp):
        qi, ki, vi, bi = inp
        diff = bi[:, :, :, None, :] - bi[:, :, None, :, :]
        decay = jnp.exp(jnp.where(causal, diff, -jnp.inf))
        scores = jnp.einsum('bhtk,bhsk,bhtsk->bhts', qi, ki, decay)
        o = jnp.einsum('bhts,bhsv->bhtv', scores, vi) + \
            jnp.einsum('bhtk,bhkv->bhtv', qi * jnp.exp(bi), state)
        b_last = bi[:, :, -1:, :]
        new_state = jnp.exp(b_last[:, :, 0, :])[..., None] * state + \
            jnp.einsum('bhsk,bhsv->bhkv', ki * jnp.exp(b_last - bi), vi)
        return new_state, o

    s0 = jnp.zeros((b_, h_, dk, dv), jnp.float32)
    _, o = lax.scan(step, s0, (qc, kc, vc, bc))
    return o.transpose(1, 0, 3, 2, 4).reshape(b_, s_, h_, dv)

def causal_depthwise_conv(u, w):
    s_ = u.shape[1]
    up = jnp.pad(u, ((0, 0), (CONV_K - 1, 0), (0, 0)))
    return sum(w[:, j] * up[:, j:j + s_, :] for j in range(CONV_K))

def first_inputs(seed: int = 0) -> dict:
    key = jax.random.key(seed)
    ks = jax.random.split(key, 24)
    L = DEPTH

    def w(k, shape, fan_in):
        return jax.random.normal(k, shape, jnp.float32) * fan_in ** -0.5

    def gain(k, shape):
        return 1.0 + 0.02 * jax.random.normal(k, shape, jnp.float32)

    return {
        "x": jax.random.normal(ks[0], (BATCH, SEQ, D_MODEL), jnp.float32),
        "mem": jax.random.normal(ks[1], (BATCH, MEM_LEN, D_MODEL), jnp.float32),
        "ffn1_norm": gain(ks[2], (L, D_MODEL)),
        "ffn1_gate": w(ks[3], (L, D_MODEL, D_FF), D_MODEL),
        "ffn1_up": w(ks[4], (L, D_MODEL, D_FF), D_MODEL),
        "ffn1_down": w(ks[5], (L, D_FF, D_MODEL), D_FF),
        "mix_norm": gain(ks[6], (L, D_MODEL)),
        "w_in": w(ks[7], (L, D_MODEL, IN_COLS), D_MODEL),
        "lb_param": 0.1 * jax.random.normal(ks[8], (L + 1, HGRN_F), jnp.float32),
        "hgrn_out_norm": gain(ks[9], (L, HGRN_W)),
        "conv_w": w(ks[10], (L, CONV_W, CONV_K), CONV_K),
        "w_out": w(ks[11], (L, D_MIX, D_MODEL), D_MIX),
        "xattn_norm": gain(ks[12], (L, D_MODEL)),
        "mem_norm": gain(ks[13], (L, D_MODEL)),
        "w_q_mem": w(ks[14], (L, D_MODEL, D_MODEL), D_MODEL),
        "w_kv_mem": w(ks[15], (L, D_MODEL, 2 * D_MODEL), D_MODEL),
        "w_o_mem": w(ks[16], (L, D_MODEL, D_MODEL), D_MODEL),
        "ffn2_norm": gain(ks[17], (L, D_MODEL)),
        "ffn2_gate": w(ks[18], (L, D_MODEL, D_FF), D_MODEL),
        "ffn2_up": w(ks[19], (L, D_MODEL, D_FF), D_MODEL),
        "ffn2_down": w(ks[20], (L, D_FF, D_MODEL), D_FF),
        "final_norm": gain(ks[21], (D_MODEL,)),
    }

def first_block(x, mem, ffn1_norm, ffn1_gate, ffn1_up, ffn1_down, mix_norm, w_in,
              lb_param, hgrn_out_norm, conv_w, w_out, xattn_norm, mem_norm,
              w_q_mem, w_kv_mem, w_o_mem, ffn2_norm, ffn2_gate, ffn2_up,
              ffn2_down, final_norm):
    b_, s_, _ = x.shape
    lb_all = jnp.cumsum(jax.nn.softmax(lb_param.astype(jnp.float32), axis=0), axis=0)

    for l in range(DEPTH):
        x = x + 0.5 * swiglu(rms_norm(x, ffn1_norm[l]), ffn1_gate[l], ffn1_up[l], ffn1_down[l])

        h = rms_norm(x, mix_norm[l])
        z = h @ w_in[l]
        o1 = HGRN_F; o2 = o1 + HGRN_F; o3 = o2 + HGRN_W; o4 = o3 + HGRN_W
        o5 = o4 + CONV_W; o6 = o5 + CONV_W
        zq, zf, zi, zg = z[..., :o1], z[..., o1:o2], z[..., o2:o3], z[..., o3:o4]
        zb, zc, zu = z[..., o4:o5], z[..., o5:o6], z[..., o6:]

        lb = lb_all[l]
        f = lb + (1.0 - lb) * jax.nn.sigmoid(zf.astype(jnp.float32))
        logf = jnp.log(f)
        kk = 1.0 - f
        q = jax.nn.silu(zq.astype(jnp.float32)) * HGRN_DK ** -0.5
        shp_k = (b_, s_, HGRN_HEADS, HGRN_DK)
        o_h = hgrn2_chunkwise(q.reshape(shp_k), kk.reshape(shp_k),
                              zi.reshape(b_, s_, HGRN_HEADS, HGRN_DV), logf.reshape(shp_k))
        g_h = hgrn_out_norm[l].astype(jnp.float32).reshape(HGRN_HEADS, HGRN_DV)
        o_h = o_h * lax.rsqrt(jnp.mean(o_h * o_h, axis=-1, keepdims=True) + EPS) * g_h
        y_hgrn = (o_h.reshape(b_, s_, HGRN_W) * jax.nn.silu(zg.astype(jnp.float32))).astype(x.dtype)

        y_conv = zb * causal_depthwise_conv(zc * zu, conv_w[l])

        x = x + jnp.concatenate([y_hgrn, y_conv.astype(x.dtype)], axis=-1) @ w_out[l]

        hq = rms_norm(x, xattn_norm[l])
        mn = rms_norm(mem, mem_norm[l])
        qm = (hq @ w_q_mem[l]).reshape(b_, s_, MEM_HEADS, MEM_HD)
        kv = mn @ w_kv_mem[l]
        km = kv[..., :D_MODEL].reshape(b_, MEM_LEN, MEM_HEADS, MEM_HD)
        vm = kv[..., D_MODEL:].reshape(b_, MEM_LEN, MEM_HEADS, MEM_HD)
        sc = jnp.einsum('bshd,bmhd->bhsm', qm.astype(jnp.float32), km.astype(jnp.float32)) * MEM_HD ** -0.5
        p = jax.nn.softmax(sc, axis=-1)
        att = jnp.einsum('bhsm,bmhd->bshd', p, vm.astype(jnp.float32)).astype(x.dtype)
        x = x + att.reshape(b_, s_, D_MODEL) @ w_o_mem[l]

        x = x + 0.5 * swiglu(rms_norm(x, ffn2_norm[l]), ffn2_gate[l], ffn2_up[l], ffn2_down[l])

    return rms_norm(x, final_norm)


MOBA_HEADS = 8
MOBA_HEAD_DIM = 64
MOBA_BLOCK = 256
MOBA_TOPK = 3
MOBA_Q_CHUNK = 16
MOBA_WIDTH = MOBA_HEADS * MOBA_HEAD_DIM
DIFF_HEADS = 4
DIFF_HEAD_DIM = 64
DIFF_Q_BLOCK = 128
DIFF_WIDTH = DIFF_HEADS * 2 * DIFF_HEAD_DIM
N_BRANCHES = 2
IN_COLS_2 = 3 * MOBA_WIDTH + 3 * DIFF_WIDTH + N_BRANCHES * D_MODEL
D_FF_2 = -(-8 * D_MODEL // (3 * 256)) * 256
NORM_EPS = 1e-6
SUBLN_EPS = 1e-5
ALIBI_MAX_BIAS = 8.0
NEG = -1e30


def rms_norm_2(x, g, eps=NORM_EPS):
    x32 = x.astype(jnp.float32)
    y = x32 * lax.rsqrt(jnp.mean(x32 * x32, axis=-1, keepdims=True) + eps)
    return (y * g.astype(jnp.float32)).astype(x.dtype)

def alibi_slopes():
    n = MOBA_HEADS + DIFF_HEADS
    slopes = 2.0 ** (-ALIBI_MAX_BIAS * np.arange(1, n + 1) / n)
    stride = n // DIFF_HEADS
    diff_idx = np.arange(DIFF_HEADS) * stride + (stride - 1)
    moba_idx = np.setdiff1d(np.arange(n), diff_idx)
    return (jnp.asarray(slopes[moba_idx], dtype=jnp.float32),
            jnp.asarray(slopes[diff_idx], dtype=jnp.float32))

def moba_attention(q, k, v, slopes):
    B, H, S, Dh = q.shape
    BS = MOBA_BLOCK
    nb = -(-S // BS)
    s_pad = nb * BS
    scale = Dh ** -0.5
    pad = ((0, 0), (0, 0), (0, s_pad - S), (0, 0))
    k_pad = jnp.pad(k, pad)
    v_pad = jnp.pad(v, pad)
    k_blocks = k_pad.reshape(B, H, nb, BS, Dh)
    v_blocks = v_pad.reshape(B, H, nb, BS, Dh)
    k_mean = jnp.mean(k_blocks.astype(jnp.float32), axis=3).astype(q.dtype)
    pos = jnp.arange(S)
    q_blk = pos // BS
    gate = jnp.einsum('bhtd,bhnd->bhtn', q, k_mean).astype(jnp.float32)
    is_past = jnp.arange(nb)[None, :] < q_blk[:, None]
    gate = jnp.where(is_past, gate, NEG)
    n_sel = max(1, min(MOBA_TOPK, nb - 1))
    _, sel = lax.top_k(gate, n_sel)
    sel_valid = jnp.arange(n_sel)[None, :] < q_blk[:, None]
    b_ix = jnp.arange(B)[:, None, None, None]
    h_ix = jnp.arange(H)[None, :, None, None]
    C = MOBA_Q_CHUNK
    sl = slopes[None, :, None, None, None]

    def chunk(c):
        t0 = c * C
        qc = lax.dynamic_slice_in_dim(q, t0, C, axis=2)
        sc = lax.dynamic_slice_in_dim(sel, t0, C, axis=2)
        vc = lax.dynamic_slice_in_dim(sel_valid, t0, C, axis=0)
        tq = t0 + jnp.arange(C)
        kg = k_blocks[b_ix, h_ix, sc]
        s_pos = sc[..., None] * BS + jnp.arange(BS)
        lp = jnp.einsum('bhcd,bhcnkd->bhcnk', qc, kg).astype(jnp.float32) * scale
        lp = lp - sl * (tq[:, None, None] - s_pos).astype(jnp.float32)
        lp = jnp.where(vc[:, :, None], lp, NEG).reshape(B, H, C, n_sel * BS)
        own0 = (t0 // BS) * BS
        ko = lax.dynamic_slice_in_dim(k_pad, own0, BS, axis=2)
        vo = lax.dynamic_slice_in_dim(v_pad, own0, BS, axis=2)
        so = own0 + jnp.arange(BS)
        dist_o = (tq[:, None] - so[None, :]).astype(jnp.float32)
        lo = jnp.einsum('bhcd,bhkd->bhck', qc, ko).astype(jnp.float32) * scale
        lo = lo - slopes[None, :, None, None] * dist_o
        lo = jnp.where(so[None, :] <= tq[:, None], lo, NEG)
        p = jax.nn.softmax(jnp.concatenate([lp, lo], axis=-1), axis=-1).astype(v.dtype)
        pp = p[..., :n_sel * BS].reshape(B, H, C, n_sel, BS)
        po = p[..., n_sel * BS:]
        vg = v_blocks[b_ix, h_ix, sc]
        return (jnp.einsum('bhcnk,bhcnkd->bhcd', pp, vg)
                + jnp.einsum('bhck,bhkd->bhcd', po, vo))

    outs = lax.map(chunk, jnp.arange(S // C))
    return outs.transpose(1, 2, 0, 3, 4).reshape(B, H, S, Dh)

def diff_attention(q1, q2, k1, k2, v, lam, slopes):
    B, H, S, d = q1.shape
    scale = d ** -0.5
    QB = DIFF_Q_BLOCK
    kpos = jnp.arange(S)

    def block(c):
        t0 = c * QB
        tq = t0 + jnp.arange(QB)
        bias = -slopes[:, None, None] * (tq[:, None] - kpos[None, :]).astype(jnp.float32)
        causal = kpos[None, :] <= tq[:, None]

        def probs(q, k):
            qc = lax.dynamic_slice_in_dim(q, t0, QB, axis=2)
            logits = jnp.einsum('bhqd,bhkd->bhqk', qc, k).astype(jnp.float32) * scale + bias[None]
            return jax.nn.softmax(jnp.where(causal, logits, NEG), axis=-1)

        a = probs(q1, k1) - lam * probs(q2, k2)
        return jnp.einsum('bhqk,bhke->bhqe', a.astype(v.dtype), v)

    outs = lax.map(block, jnp.arange(S // QB))
    return outs.transpose(1, 2, 0, 3, 4).reshape(B, H, S, 2 * d)

def second_inputs(seed: int = 0) -> dict:
    key = jax.random.key(seed)
    ks = jax.random.split(key, 17)
    L, D = DEPTH, D_MODEL

    def normal(k, shape, scale):
        return jax.random.normal(k, shape, dtype=jnp.float32) * scale

    def gain(k, n):
        return 1.0 + normal(k, (L, n), 0.05)

    return {
        'x': normal(ks[0], (BATCH, SEQ, D), 1.0),
        'norm_mix_pre_g': gain(ks[1], D),
        'w_in': normal(ks[2], (L, D, IN_COLS_2), D ** -0.5),
        'w_branch_a': normal(ks[3], (L, MOBA_WIDTH, D), MOBA_WIDTH ** -0.5),
        'w_branch_b': normal(ks[4], (L, DIFF_WIDTH, D), DIFF_WIDTH ** -0.5),
        'lam_q1': normal(ks[5], (L, DIFF_HEAD_DIM), 0.1),
        'lam_k1': normal(ks[6], (L, DIFF_HEAD_DIM), 0.1),
        'lam_q2': normal(ks[7], (L, DIFF_HEAD_DIM), 0.1),
        'lam_k2': normal(ks[8], (L, DIFF_HEAD_DIM), 0.1),
        'diff_subln_g': gain(ks[9], 2 * DIFF_HEAD_DIM),
        'w_out': normal(ks[10], (L, D, D), D ** -0.5),
        'norm_mix_post_g': gain(ks[11], D),
        'norm_ffn_pre_g': gain(ks[12], D),
        'w_gate': normal(ks[13], (L, D, D_FF_2), D ** -0.5),
        'w_up': normal(ks[14], (L, D, D_FF_2), D ** -0.5),
        'w_down': normal(ks[15], (L, D_FF_2, D), D_FF_2 ** -0.5),
        'norm_ffn_post_g': gain(ks[16], D),
    }

def second_block(x, norm_mix_pre_g, w_in, w_branch_a, w_branch_b, lam_q1, lam_k1, lam_q2, lam_k2,
              diff_subln_g, w_out, norm_mix_post_g, norm_ffn_pre_g, w_gate, w_up, w_down,
              norm_ffn_post_g):
    B, S, D = x.shape
    moba_slopes, diff_slopes = alibi_slopes()
    sizes = [MOBA_WIDTH] * 3 + [DIFF_WIDTH] * 3 + [D_MODEL] * N_BRANCHES
    split_at = [int(v) for v in np.cumsum(sizes)[:-1]]
    for l in range(DEPTH):
        lam_init = 0.8 - 0.6 * math.exp(-0.3 * l)
        h = rms_norm_2(x, norm_mix_pre_g[l])
        proj = h @ w_in[l]
        mq, mk, mv, dq, dk, dv, ga, gb = jnp.split(proj, split_at, axis=-1)

        def moba_heads(t):
            return t.reshape(B, S, MOBA_HEADS, MOBA_HEAD_DIM).transpose(0, 2, 1, 3)

        ya = moba_attention(moba_heads(mq), moba_heads(mk), moba_heads(mv), moba_slopes)
        ya = ya.transpose(0, 2, 1, 3).reshape(B, S, MOBA_WIDTH)

        dq = dq.reshape(B, S, DIFF_HEADS, 2, DIFF_HEAD_DIM).transpose(0, 2, 3, 1, 4)
        dk = dk.reshape(B, S, DIFF_HEADS, 2, DIFF_HEAD_DIM).transpose(0, 2, 3, 1, 4)
        dv = dv.reshape(B, S, DIFF_HEADS, 2 * DIFF_HEAD_DIM).transpose(0, 2, 1, 3)
        lam = (jnp.exp(jnp.sum(lam_q1[l].astype(jnp.float32) * lam_k1[l].astype(jnp.float32)))
               - jnp.exp(jnp.sum(lam_q2[l].astype(jnp.float32) * lam_k2[l].astype(jnp.float32)))
               + lam_init)
        yb = diff_attention(dq[:, :, 0], dq[:, :, 1], dk[:, :, 0], dk[:, :, 1], dv, lam, diff_slopes)
        yb = rms_norm_2(yb, diff_subln_g[l], SUBLN_EPS) * (1.0 - lam_init)
        yb = yb.transpose(0, 2, 1, 3).reshape(B, S, DIFF_WIDTH)

        merged = (jax.nn.sigmoid(ga) * (ya @ w_branch_a[l])
                  + jax.nn.sigmoid(gb) * (yb @ w_branch_b[l]))
        x = x + rms_norm_2(merged @ w_out[l], norm_mix_post_g[l])
        h = rms_norm_2(x, norm_ffn_pre_g[l])
        f = (jax.nn.silu(h @ w_gate[l]) * (h @ w_up[l])) @ w_down[l]
        x = x + rms_norm_2(f, norm_ffn_post_g[l])
    return x


def setup_inputs(seed=0):
    out = dict(first_inputs(seed))
    for name, value in second_inputs(seed + 1).items():
        if name != "x":
            out[name + "_2"] = value
    return out


def reference(
    x, mem, ffn1_norm, ffn1_gate, ffn1_up, ffn1_down, mix_norm, w_in, lb_param, hgrn_out_norm,
    conv_w, w_out, xattn_norm, mem_norm, w_q_mem, w_kv_mem, w_o_mem, ffn2_norm, ffn2_gate,
    ffn2_up, ffn2_down, final_norm, norm_mix_pre_g_2, w_in_2, w_branch_a_2, w_branch_b_2,
    lam_q1_2, lam_k1_2, lam_q2_2, lam_k2_2, diff_subln_g_2, w_out_2, norm_mix_post_g_2,
    norm_ffn_pre_g_2, w_gate_2, w_up_2, w_down_2, norm_ffn_post_g_2,
):
    x = first_block(
        x, mem, ffn1_norm, ffn1_gate, ffn1_up, ffn1_down, mix_norm, w_in, lb_param,
        hgrn_out_norm, conv_w, w_out, xattn_norm, mem_norm, w_q_mem, w_kv_mem, w_o_mem,
        ffn2_norm, ffn2_gate, ffn2_up, ffn2_down, final_norm,
    )
    return second_block(
        x, norm_mix_pre_g_2, w_in_2, w_branch_a_2, w_branch_b_2, lam_q1_2, lam_k1_2, lam_q2_2,
        lam_k2_2, diff_subln_g_2, w_out_2, norm_mix_post_g_2, norm_ffn_pre_g_2, w_gate_2,
        w_up_2, w_down_2, norm_ffn_post_g_2,
    )


_drawn_inputs = setup_inputs


def setup_inputs(seed=0):
    import zlib

    import numpy as np

    out = dict(_drawn_inputs(seed))
    spreads = {}
    factors = {'ffn1_norm': 3.141,
     'lb_param': 8.0,
     'hgrn_out_norm': 5.346,
     'xattn_norm': 8.0,
     'mem_norm': 8.0,
     'ffn2_norm': 5.593,
     'lam_q1_2': 4.186,
     'lam_k1_2': 3.546}
    for name, (base, spread) in spreads.items():
        noise = np.random.default_rng([zlib.crc32(name.encode()), seed]).standard_normal(out[name].shape)
        drawn = base * np.exp(spread * noise) if base else spread * noise
        out[name] = __import__('jax').numpy.asarray(drawn.astype(out[name].dtype))
    for name, factor in factors.items():
        out[name] = (out[name] * factor).astype(out[name].dtype)
    return out
```

```python
import math
from contextlib import ExitStack

import concourse.bass as bass
from concourse import mybir

F32 = mybir.dt.float32
F32R = mybir.dt.float32r
I32 = mybir.dt.int32
ACT = mybir.ActivationFunctionType
ALU = mybir.AluOpType
AX_X = mybir.AxisListType.X

P = 128
T = 512
D = 1024
C = D // P
TT = T // P
MEM = 256
FF = 2816
FC = FF // P
HEADS = 4
EPS = 1e-6
EPS_SUBLN = 1e-5
LAM_INIT = 0.8 - 0.6 * math.exp(0.0)
MASKED = 1e33
SLOPES = [2.0 ** (-8.0 * n / 12) for n in range(1, 13)]
DIFF_SLOPES = SLOPES[2::3]
MOBA_SLOPES = [s for n, s in enumerate(SLOPES) if n % 3 != 2]
LEVELS = 9
W = 2048

GAIN_ROWS = [("ffn1_norm", 8), ("mix_norm", 8), ("xattn_norm", 8), ("mem_norm", 8), ("ffn2_norm", 8),
             ("final_norm", 8), ("norm_mix_pre_g_2", 8), ("norm_mix_post_g_2", 8), ("norm_ffn_pre_g_2", 8),
             ("norm_ffn_post_g_2", 8), ("hgrn_out_norm", 4), ("diff_subln_g_2", 1), ("lb_param", 8)]
GAIN_AT = {}
for _name, _rows in GAIN_ROWS:
    GAIN_AT[_name] = sum(r for n, r in GAIN_ROWS[:len(GAIN_AT)])
GAINS = sum(r for _, r in GAIN_ROWS)

GATE_UNITS, DOWN_UNITS = FC, FC // 2
FFN_UNITS = GATE_UNITS + DOWN_UNITS
MIX1_UNITS, KV_UNITS, SQUARE_UNITS, MIX2_UNITS, BRANCH_UNITS = 14, 8, 4, 20, 4
U_FFN1 = 0
U_MIX1 = U_FFN1 + FFN_UNITS
U_OUT1 = U_MIX1 + MIX1_UNITS + KV_UNITS
U_Q = U_OUT1 + SQUARE_UNITS
U_O = U_Q + SQUARE_UNITS
U_FFN2 = U_O + SQUARE_UNITS
U_MIX2 = U_FFN2 + FFN_UNITS
U_BRANCH = U_MIX2 + MIX2_UNITS
U_OUT2 = U_BRANCH + BRANCH_UNITS
U_FFN3 = U_OUT2 + SQUARE_UNITS
UNITS = U_FFN3 + FFN_UNITS

ZQ, ZF, ZI, ZG, ZB, ZC, ZU = range(0, 3584, 512)
MIX1_COLS = [z + 256 * j for z in (ZQ, ZG, ZF, ZI, ZC, ZU, ZB) for j in range(2)]
MIX2_COLS = [256 * j for j in range(MIX2_UNITS)]

X_LOAD, X_FFN1, X_MIX1, X_ATT, X_FFN2, X_FINAL, X_MIX2, X_FFN3 = range(8)
N_FFN1, N_MIX1, N_ATT, N_FFN2, N_FINAL, N_MIX2, N_POST2, N_FFN3, N_POST3 = range(9)

TILE_AT = {3: 0, 2: 512, 0: 896, 1: 1024}
KEYS_AT = {0: 0, 1: 512, 3: 896, 2: 1024}
MAPS = 16


def two_blocks(nc, a, out):
    with ExitStack() as ctx:
        def sem(name):
            return ctx.enter_context(nc.semaphore(name))

        cursor = [-(-nc.sbuf_base // 32) * 32]

        def at(name, shape, dt, offset):
            return nc.alloc_sbuf_tensor_at(name, shape, dt, offset=offset)

        def sb(name, shape, dt):
            size = 4 * math.prod(shape[1:])
            t = at(name, shape, dt, cursor[0])
            cursor[0] += -(-size // 32) * 32
            return t

        raw = [sb(f"w_raw{s}", [P, W], F32) for s in range(2)]
        whi = [sb(f"w_hi{s}", [P, W], F32R) for s in range(2)]
        wlo = [sb(f"w_lo{s}", [P, W], F32R) for s in range(2)]
        x = sb("x", [P, C, T], F32)
        n_at = cursor[0]
        nhi = sb("n_hi", [P, C, T], F32R)
        nlo = sb("n_lo", [P, C, T], F32R)
        ypost = at("y_post", [P, C, T], F32, n_at)
        sq = [sb(f"sq{s}", [P, T], F32) for s in range(2)]
        tmp = [sb(f"tmp{s}", [P, T], F32) for s in range(2)]
        lnt = sb("ln_mean_square", [P, T], F32)
        rstd = sb("rstd", [P, T], F32)
        ident = sb("ident", [P, P], F32)
        ones = sb("ones", [P, P], F32)
        gains = sb("gains", [P, GAINS], F32)
        small = sb("small", [P, 64], F32)
        convw = sb("conv_taps", [P, HEADS, 3], F32)
        masks = sb("level_masks", [P, 6, 32], I32)
        maskt = sb("mask_tmp", [P, 3, 32], I32)
        arena = cursor[0]
        arena_size = nc.sbuf_usable_end - arena
        KB = 1024

        hhi = at("h_hi", [P, FC, T], F32R, arena)
        hlo = at("h_lo", [P, FC, T], F32R, arena + 44 * KB)
        x_tok = at("x_tok", [P, TT, D], F32, arena)
        gain_rows = at("gain_rows", [GAINS, P], F32, arena + 16 * KB)
        out_tok = at("out_tok", [P, TT, D], F32, arena)
        hq = at("hgrn_q", [P, HEADS, T], F32, arena)
        hk = at("hgrn_k", [P, HEADS, T], F32, arena + 8 * KB)
        hf = at("hgrn_prefix", [P, HEADS, T], F32, arena + 16 * KB)
        hv = at("hgrn_v", [P, TT, T], F32, arena + 24 * KB)
        hg = at("hgrn_gate", [P, HEADS, T], F32, arena + 32 * KB)
        cv = at("conv_out", [P, HEADS, T], F32, arena + 40 * KB)
        cu = at("conv_in", [P, HEADS, T + 2], F32, arena + 48 * KB)
        mnhi = at("mem_hi", [P, C, MEM], F32R, arena + 57 * KB)
        mnlo = at("mem_lo", [P, C, MEM], F32R, arena + 65 * KB)
        hsuf = at("hgrn_suffix", [P, T], F32, arena + 73 * KB)
        qk = [at(f"hgrn_qk{s}", [P, T], F32, arena + (75 + 2 * s) * KB) for s in range(2)]
        pt = at("hgrn_scores", [P, TT * 640], F32, arena + 79 * KB)
        s32 = at("hgrn_diag", [P, TT, 32], F32, arena + 89 * KB)
        osb = at("hgrn_o", [P, T], F32, arena + 89 * KB + 512)
        osq = at("hgrn_o_sq", [P, T], F32, arena + 91 * KB + 512)
        orstd = at("hgrn_o_rstd", [P, T], F32, arena + 93 * KB + 512)
        mem_tok = at("mem_tok", [P, 2, D], F32, arena + 79 * KB)
        memt = at("mem_t", [P, C, MEM], F32, arena + 48 * KB)
        memsq = at("mem_sq", [P, C, MEM], F32, arena + 40 * KB)
        km = at("mem_k", [P, C, MEM], F32, arena + 16 * KB)
        vm = at("mem_v", [P, 2, D], F32, arena + 8 * KB)
        qx = at("att_q", [P, C, T], F32, arena + 24 * KB)
        px = at("att_p", [P, TT, MEM], F32, arena + 40 * KB)
        ptx = at("att_pt", [P, 2, T], F32, arena + 44 * KB)
        ga = at("gate_a", [P, C, T], F32, arena)
        mq = at("moba_q", [P, HEADS, T], F32, arena + 16 * KB)
        dq = at("diff_q", [P, HEADS, T], F32, arena + 24 * KB)
        dk = at("diff_k", [P, HEADS, T], F32, arena + 32 * KB)
        dv = at("diff_v", [P, TT, T], F32, arena + 40 * KB)
        mk = at("moba_k", [P, HEADS, T], F32, arena + 48 * KB)
        mv = at("moba_v", [P, TT, T], F32, arena + 56 * KB)
        gb = at("gate_b", [P, C, T], F32, arena + 48 * KB)
        mhi = at("merged_hi", [P, C, T], F32R, arena + 16 * KB)
        mlo = at("merged_lo", [P, C, T], F32R, arena + 32 * KB)
        pm = [at(f"map_p{s}", [P, 1280], F32, arena + (64 + 5 * s) * KB) for s in range(2)]
        ptm = at("map_pt", [P, 1280], F32, arena + 74 * KB)
        dist = at("distance", [P, T], F32, arena + 79 * KB)
        bias = [at(f"alibi{s}", [P, T], F32, arena + (81 + 2 * s) * KB) for s in range(2)]
        ysq = at("diff_y_sq", [P, T], F32, arena + 85 * KB)
        yrstd = at("diff_y_rstd", [P, T], F32, arena + 87 * KB)
        stat = at("map_stats", [P, 2, 4, 4], F32, arena + 89 * KB)
        lamv = at("lam_vectors", [P, 4, 64], F32, arena + 90 * KB)
        lams = at("lam_tmp", [P, 64], F32, arena + 91 * KB)
        assert arena_size >= 96 * KB

        def gain(name, c):
            return gains[:, GAIN_AT[name] + c:GAIN_AT[name] + c + 1]

        LB, OMLB, SUBG, NLAM, LSUM, LEXP = 0, 8, 12, 13, 16, 18
        LBE = 24

        bank = [ctx.enter_context(nc.psum_tensor(f"bank{b}", [P, 512], F32)) for b in range(8)]

        w_loaded = [sem("w_loaded0"), sem("w_loaded1")]
        w_hi_ready, w_lo_ready = sem("w_hi_ready"), sem("w_lo_ready")
        unit_done = sem("unit_done")
        x_loaded, gains_loaded, taps_loaded = sem("x_loaded"), sem("gains_loaded"), sem("taps_loaded")
        mem_loaded, lam_loaded, stored = sem("mem_loaded"), sem("lam_loaded"), sem("stored")
        ident_steps, dist_steps = sem("ident_steps"), sem("dist_steps")
        gains_t, gains_ready, small_steps, lb_exp = sem("gains_t"), sem("gains_ready"), sem("small_steps"), sem("lb_exp")
        mask_iota, mask_steps = sem("mask_iota"), sem("mask_steps")
        x_turned, x_ready = sem("x_turned"), sem("x_ready")
        sq_ready, sq_summed, ln_done, rstd_ready = sem("sq_ready"), sem("sq_summed"), sem("ln_done"), sem("rstd_ready")
        scaled, n_hi_ready, n_ready = sem("scaled"), sem("n_hi_ready"), sem("n_ready")
        ffn = [{k: sem(f"{k}_{f}") for k in ("silu_ready", "h_product", "h_hi_ready", "h_ready", "down_done")}
               for f in range(3)]
        m1_act, m1_dve = sem("m1_act"), sem("m1_dve")
        q_scaled, f_steps, logf_ready = sem("q_scaled"), sem("f_steps"), sem("logf_ready")
        conv_pad, conv_steps = sem("conv_pad"), sem("conv_steps")
        mem_turned, memt_ready, memsq_ready, mem_summed = sem("mem_turned"), sem("memt_ready"), sem("memsq_ready"), sem("mem_summed")
        mem_rstd, mem_scaled, mem_hi_ready, mem_ready = sem("mem_rstd"), sem("mem_scaled"), sem("mem_hi_ready"), sem("mem_ready")
        sums_ready, decay_ready, qk_ready, qk_used = sem("sums_ready"), sem("decay_ready"), sem("qk_ready"), sem("qk_used")
        diag_done = sem("diag_done")
        s32_steps, scores_dve, scores_act = sem("s32_steps"), sem("scores_dve"), sem("scores_act")
        o_done, o_copied, o_summed, o_rstd, y_steps = sem("o_done"), sem("o_copied"), sem("o_summed"), sem("o_rstd"), sem("y_steps")
        y1_hi, y1_ready, pt_zero = sem("y1_hi"), sem("y1_ready"), sem("pt_zero")
        qx_ready, sx_done, mx_ready, px_ready, px_norm = sem("qx_ready"), sem("sx_done"), sem("mx_ready"), sem("px_ready"), sem("px_norm")
        px_inv = sem("px_inv")
        tx_done, ptx_ready, ax_done, ax_copied, ax_hi, ax_ready = sem("tx_done"), sem("ptx_ready"), sem("ax_done"), sem("ax_copied"), sem("ax_hi"), sem("ax_ready")
        m2_act, lam_steps, lam_exp, bias_ready = sem("m2_act"), sem("lam_steps"), sem("lam_exp"), sem("bias_ready")
        map_scores, map_max, map_neg, map_exp = sem("map_scores"), sem("map_max"), sem("map_neg"), sem("map_exp")
        map_inv, map_norm, map_turned, map_pt = sem("map_inv"), sem("map_norm"), sem("map_turned"), sem("map_pt")
        av_done, yb_sq, yb_summed, yb_rstd, y2_steps = sem("av_done"), sem("yb_sq"), sem("yb_summed"), sem("yb_rstd"), sem("y2_steps")
        ya_copied, yb_copied, y2_hi, y2_ready = sem("ya_copied"), sem("yb_copied"), sem("y2_hi"), sem("y2_ready")
        br_a, br_b, br_sum, br_hi, br_ready = sem("br_a"), sem("br_b"), sem("br_sum"), sem("br_hi"), sem("br_ready")
        ypost_ready, out_turned, out_ready = sem("ypost_ready"), sem("out_turned"), sem("out_ready")

        block = ctx.enter_context(nc.Block())

        def k_major(w):
            return w.rearrange("(k p) n -> p k n", p=P)

        def y1_order(v):
            order = {14: (4, 5, 0, 1), 15: (6, 7, 2), 17: (3,)}.get(v, ())
            first = {14: 0, 15: 4, 17: 7}.get(v, 0)
            return [(first + n, c) for n, c in enumerate(order)]

        @block.sync
        def _(sp):
            def slot_free(par, half):
                sp.wait_ge(w_lo_ready, 2 * half + par - 1)

            def load(par, pieces):
                for (lo, hi, form), src in pieces:
                    dst = raw[par][:, lo:hi].rearrange("p (k n) -> p k n", k=form)
                    sp.dma_start(dst, src).then_inc(w_loaded[par], 16)

            def load_square(u, w, k0, c0):
                if u >= 2:
                    slot_free(u % 2, u // 2)
                v = k_major(w)[:, k0:k0 + C, c0:c0 + 256]
                load(u % 2, [((0, W // 2, 4), v[:, 0:4]), ((W // 2, W, 4), v[:, 4:8])])

            def load_ffn(base, gate, up, down):
                g, p_, d = k_major(gate), k_major(up), k_major(down)

                def gate_up(par, half, n, free):
                    if free:
                        slot_free(par, half)
                    cols = bass.ds(n * P, P)
                    load(par, [((0, W // 2, C), g[:, :, cols]), ((W // 2, W, C), p_[:, :, cols])])

                def down_pair(par, half, n):
                    slot_free(par, half)
                    load(par, [((0, W // 2, 1), d[:, bass.ds(2 * n, 1), :]),
                               ((W // 2, W, 1), d[:, bass.ds(2 * n + 1, 1), :])])

                for j in range(2):
                    gate_up((base + j) % 2, (base + j) // 2, j, base > 0)
                with sp.Fori(1, GATE_UNITS // 2) as i:
                    for j in range(2):
                        gate_up((base + j) % 2, i + (base + j) // 2, 2 * i + j, True)
                b = base + GATE_UNITS
                with sp.Fori(0, DOWN_UNITS // 2) as i:
                    for j in range(2):
                        down_pair((b + j) % 2, i + (b + j) // 2, 2 * i + j)
                u = b + DOWN_UNITS - 1
                down_pair(u % 2, u // 2, DOWN_UNITS - 1)

            xv = a["x"].rearrange("b (i p) d -> p (b i) d", p=P)
            for i in range(TT):
                sp.dma_start(x_tok[:, i, :], xv[:, i, :]).then_inc(x_loaded, 16)
            for name, rows in GAIN_ROWS:
                src = a[name]
                if len(src.shape) == 2:
                    src = src.rearrange("a d -> (a d)")
                sp.dma_start(gain_rows[GAIN_AT[name]:GAIN_AT[name] + rows, :],
                             src.rearrange("(c p) -> c p", p=P)).then_inc(gains_loaded, 16)
            sp.dma_start(convw[:, :, :], a["conv_w"][0].rearrange("(c p) j -> p c j", p=P)).then_inc(taps_loaded, 16)
            load_ffn(U_FFN1, a["ffn1_gate"][0], a["ffn1_up"][0], a["ffn1_down"][0])
            for j, c0 in enumerate(MIX1_COLS):
                load_square(U_MIX1 + j, a["w_in"][0], 0, c0)
                if j == 0:
                    sp.wait_ge(unit_done, U_MIX1)
                    sp.dma_start(mem_tok[:, :, :], a["mem"].rearrange("b (i p) d -> p (b i) d", p=P)).then_inc(mem_loaded, 16)
            for j in range(KV_UNITS):
                load_square(U_MIX1 + MIX1_UNITS + j, a["w_kv_mem"][0], 0, 256 * j)
            for base, name in ((U_OUT1, "w_out"), (U_Q, "w_q_mem"), (U_O, "w_o_mem")):
                for j in range(SQUARE_UNITS):
                    load_square(base + j, a[name][0], 0, 256 * j)
            load_ffn(U_FFN2, a["ffn2_gate"][0], a["ffn2_up"][0], a["ffn2_down"][0])
            for j, c0 in enumerate(MIX2_COLS):
                load_square(U_MIX2 + j, a["w_in_2"][0], 0, c0)
                if j == 0:
                    sp.wait_ge(unit_done, U_MIX2)
                    for n, name in enumerate(("lam_q1_2", "lam_k1_2", "lam_q2_2", "lam_k2_2")):
                        sp.dma_start(lamv[:, n, :], a[name].to_broadcast([P, 64])).then_inc(lam_loaded, 16)
            for j in range(BRANCH_UNITS):
                u = U_BRANCH + j
                slot_free(u % 2, u // 2)
                v = k_major(a["w_branch_b_2" if j % 2 else "w_branch_a_2"][0])[:, :, 512 * (j // 2):512 * (j // 2) + 512]
                load(u % 2, [((0, W // 2, 2), v[:, 0:2]), ((W // 2, W, 2), v[:, 2:4])])
            for j in range(SQUARE_UNITS):
                load_square(U_OUT2 + j, a["w_out_2"][0], 0, 256 * j)
            load_ffn(U_FFN3, a["w_gate_2"][0], a["w_up_2"][0], a["w_down_2"][0])
            ov = out.rearrange("b (i p) d -> p (b i) d", p=P)
            for i in range(TT):
                sp.wait_ge(out_ready, 2 * i + 2)
                sp.dma_start(ov[:, i, :], out_tok[:, i, :]).then_inc(stored, 16)
            sp.wait_ge(stored, 16 * TT)

        @block.gpsimd
        def _(pool):
            pool.memset(ones[:, :], 1.0).then_inc(ident_steps, 1)
            pool.wait_ge(ident_steps, 1)
            pool.affine_select(ident[:, :], ones[:, :], [[-1, P]], ALU.is_equal, 0.0, base=0,
                               channel_multiplier=1).then_inc(ident_steps, 1)
            pool.iota(maskt[:, 0, :], [[0, 32]], base=0, channel_multiplier=1).then_inc(mask_iota, 1)
            pool.iota(maskt[:, 1, :], [[1, 32]], base=0, channel_multiplier=0).then_inc(mask_iota, 1)
            pool.wait_ge(unit_done, U_MIX2)
            pool.iota(dist[:, :], [[-1, T]], base=T - P, channel_multiplier=1,
                      allow_small_or_imprecise_dtypes=True).then_inc(dist_steps, 1)
            pool.wait_ge(dist_steps, 1)
            pool.affine_select(dist[:, :], dist[:, :], [[-1, T]], ALU.is_ge, MASKED, base=T - P,
                               channel_multiplier=1).then_inc(dist_steps, 1)
            pool.wait_ge(dist_steps, 2)
            for m in range(MAPS):
                if m >= 2:
                    pool.wait_ge(map_max, 4 * (m - 1))
                slope = MOBA_SLOPES[m] if m < 8 else DIFF_SLOPES[(m - 8) // 2]
                pool.tensor_scalar(bias[m % 2][:, :], dist[:, :], -slope, None, ALU.mult).then_inc(bias_ready, 1)

        @block.tensor
        def _(pe):
            def products(acc, w_hi, w_lo, x_hi, x_lo, start, stop):
                pe.matmul(acc, w_hi, x_hi, start=start, stop=False)
                pe.matmul(acc, w_hi, x_lo, start=False, stop=False)
                return pe.matmul(acc, w_lo, x_hi, start=False, stop=stop)

            def unit_split(u):
                pe.wait_ge(w_lo_ready, u + 1)

            def dense(u, pair, xh, xl, wait_x=None, width=T, hooks=None):
                unit_split(u)
                s = u % 2
                for k in range(C):
                    if wait_x is not None:
                        wait_x(k)
                    for m in range(2):
                        w0 = k * 256 + m * P
                        mm = products(bank[pair + m][:, 0:width], whi[s][:, w0:w0 + P], wlo[s][:, w0:w0 + P],
                                      xh[:, k, :], xl[:, k, :], k == 0, k == C - 1)
                    if k == C - 1:
                        mm.then_inc(unit_done, 1)
                    if hooks and k in hooks:
                        hooks[k]()

            def dense_tokens(u, pair, xh, xl, tiles, hooks=None):
                unit_split(u)
                s = u % 2
                per = tiles // 2
                for i in range(tiles):
                    acc = bank[pair + i // per][:, (i % per) * 256:(i % per) * 256 + 256]
                    for k in range(C):
                        t0 = slice(i * P, i * P + P)
                        w0 = slice(k * 256, k * 256 + 256)
                        pe.matmul(acc, xh[:, k, t0], whi[s][:, w0], start=(k == 0), stop=False)
                        pe.matmul(acc, xl[:, k, t0], whi[s][:, w0], start=False, stop=False)
                        mm = pe.matmul(acc, xh[:, k, t0], wlo[s][:, w0], start=False, stop=(k == C - 1))
                        if i == tiles - 1 and k == C - 1:
                            mm.then_inc(unit_done, 1)
                        if hooks and k % 2 and (2 * i + k // 4) in hooks and k % 4 == 3:
                            hooks[2 * i + k // 4]()

            def sum_squares(norm, b):
                for c in range(C):
                    pe.wait_ge(sq_ready, C * norm + c + 1)
                    pe.matmul(bank[b][:, :], ones[:, :], sq[c % 2][:, :], start=(c == 0),
                              stop=(c == C - 1)).then_inc(sq_summed, 1)

            def after_norm(index):
                return lambda k: pe.wait_ge(n_ready, C * index + k + 1)

            def ffn_products(f, base, index):
                s_ = ffn[f]

                def gate_up(u, j, par, jj, first):
                    pe.wait_ge(w_lo_ready, u + 1)
                    if not first:
                        pe.wait_ge(s_["h_product"], j - 1)
                    for k in range(C):
                        if first and jj == 0:
                            pe.wait_ge(n_ready, C * index + k + 1)
                        for g in range(2):
                            w0 = (g * C + k) * P
                            mm = products(bank[2 * jj + g][:, :], whi[par][:, w0:w0 + P], wlo[par][:, w0:w0 + P],
                                          nhi[:, k, :], nlo[:, k, :], k == 0, k == C - 1)
                    mm.then_inc(unit_done, 1)

                for j in range(2):
                    gate_up(base + j, j, (base + j) % 2, j, True)
                with pe.Fori(1, GATE_UNITS // 2) as i:
                    for j in range(2):
                        gate_up(2 * i + (base + j), 2 * i + j, (base + j) % 2, j, False)

                def down(u, n, par, first=False, last=False):
                    pe.wait_ge(w_lo_ready, u + 1)
                    pe.wait_ge(s_["h_ready"], 2 * n + 2)
                    for d in ([4, 5, 6, 7, 0, 1, 2, 3] if first else range(C)):
                        if first and d == 0:
                            pe.wait_ge(s_["h_product"], FC)
                        for kk in range(2):
                            w0 = kk * D + d * P
                            if isinstance(n, int):
                                xh, xl = hhi[:, 2 * n + kk, :], hlo[:, 2 * n + kk, :]
                            else:
                                xh = hhi[:, bass.ds(2 * n + kk, 1), :].rearrange("p o t -> p (o t)")
                                xl = hlo[:, bass.ds(2 * n + kk, 1), :].rearrange("p o t -> p (o t)")
                            mm = products(bank[d][:, :], whi[par][:, w0:w0 + P], wlo[par][:, w0:w0 + P],
                                          xh, xl, first and kk == 0, last and kk == 1)
                        if last and d < C - 1:
                            mm.then_inc(s_["down_done"], 1)
                    mm.then_inc(unit_done, 1)

                b = base + GATE_UNITS
                down(b, 0, b % 2, first=True)
                with pe.Fori(0, (DOWN_UNITS - 3) // 2) as i:
                    for j in range(2):
                        down(2 * i + (b + 1 + j), 2 * i + (1 + j), (b + 1 + j) % 2)
                for n in (DOWN_UNITS - 2, DOWN_UNITS - 1):
                    down(b + n, n, (b + n) % 2, last=(n == DOWN_UNITS - 1))

            pe.wait_ge(ident_steps, 2)
            pe.wait_ge(x_loaded, 16 * TT)
            for c in range(C):
                for i in range(TT):
                    mm = pe.transpose(bank[c][:, i * P:(i + 1) * P], x_tok[:, i, c * P:(c + 1) * P], ident[:, :])
                mm.then_inc(x_turned, 1)
            sum_squares(N_FFN1, 0)
            pe.wait_ge(gains_loaded, 16 * len(GAIN_ROWS))
            pe.wait_ge(x_ready, 2)
            pe.transpose(bank[1][:, 0:GAINS], gain_rows[:, :], ident[0:GAINS, 0:GAINS]).then_inc(gains_t, 1)
            pe.wait_ge(gains_ready, 1)
            ffn_products(0, U_FFN1, N_FFN1)
            sum_squares(N_MIX1, 0)

            def hgrn_level(h, l):
                g = LEVELS * h + l
                pe.wait_ge(qk_ready, 2 * g + 2)
                L, z = 1 << l, qk[g % 2]
                if L < 32:
                    b, slot = (bank[4], l + 1) if l < 3 else (bank[5], l - 3)
                    for j in range(TT):
                        for m in range(4):
                            t0 = slice(P * j + 32 * m, P * j + 32 * m + 32)
                            mm = pe.matmul(b[32 * m:32 * m + 32, slot * P + 32 * j:slot * P + 32 * j + 32],
                                           z[:, t0], z[:, t0], start=True, stop=True)
                elif L == 32:
                    for j in range(TT):
                        for m in range(2):
                            s0 = P * j + 64 * m
                            mm = pe.matmul(bank[5][64 * m:64 * m + 32, 256 + 32 * j:288 + 32 * j],
                                           z[:, s0:s0 + 32], z[:, s0 + 32:s0 + 64], start=True, stop=True)
                elif L == 64:
                    for j in range(TT):
                        mm = pe.matmul(bank[6][0:64, 64 * j:64 * j + 64], z[:, P * j:P * j + 64],
                                       z[:, P * j + 64:P * j + P], start=True, stop=True)
                elif L == 128:
                    for j in range(2):
                        mm = pe.matmul(bank[6][:, 256 + P * j:256 + P * j + P], z[:, 256 * j:256 * j + P],
                                       z[:, 256 * j + P:256 * j + 256], start=True, stop=True)
                else:
                    for j in range(2):
                        mm = pe.matmul(bank[7][:, 256 * j:256 * j + 256], z[:, P * j:P * j + P],
                                       z[:, 256:512], start=True, stop=True)
                mm.then_inc(qk_used, 1)

            def hgrn_first(h):
                if h:
                    pe.wait_ge(scores_dve, 6 * h)
                else:
                    pe.wait_ge(mem_rstd, 2)
                pe.wait_ge(q_scaled, h + 1)
                pe.wait_ge(f_steps, 2 * h + 2)
                for j in range(TT):
                    for m in range(4):
                        t0 = slice(P * j + 32 * m, P * j + 32 * m + 32)
                        mm = pe.matmul(bank[4][32 * m:32 * m + 32, 32 * j:32 * j + 32], hk[:, h, t0], hq[:, h, t0],
                                       start=True, stop=True)
                mm.then_inc(diag_done, 1)
                hgrn_level(h, 0)

            def hgrn_rest(h):
                if h:
                    pe.wait_ge(o_copied, 2 * h)
                    pe.wait_ge(o_rstd, 2 * h - 1)
                hgrn_level(h, 5)

            def hgrn_out(h):
                pe.wait_ge(scores_dve, 6 * h + 6)
                pe.wait_ge(scores_act, 3 * h + 3)
                pe.wait_ge(m1_act, 16)
                for j in range(TT):
                    mm = pe.matmul(bank[7][:, P * j:T], hv[:, j, h * P:(h + 1) * P],
                                   pt[:, T * j + P * j:T * j + T], start=(j == 0), stop=(j == TT - 1))
                mm.then_inc(o_done, 1)

            def hgrn_sum(h):
                pe.wait_ge(o_copied, 2 * h + 2)
                pe.matmul(bank[6][:, :], ones[:, :], osq[:, :], start=True, stop=True).then_inc(o_summed, 1)

            def hgrn_hooks(v):
                def then(what, *args):
                    return lambda: what(*args)

                hooks = {}
                for h in range(HEADS):
                    if v == 7 + 2 * h:
                        hooks[3] = then(hgrn_first, h)
                        for l in range(1, 5):
                            hooks[3 + l] = then(hgrn_level, h, l)
                    if v == 8 + 2 * h:
                        hooks[4] = then(hgrn_rest, h)
                        for l in range(6, LEVELS):
                            hooks[l - 1] = then(hgrn_level, h, l)
                    if v == 10 + 2 * h:
                        hooks[2] = then(hgrn_sum, h)
                for h in range(HEADS):
                    if v == 9 + 2 * h:
                        before = hooks.get(7)
                        hooks[7] = (lambda h, before: lambda: (before() if before else None, hgrn_out(h)))(h, before)
                return hooks

            for v in range(MIX1_UNITS + KV_UNITS):
                u, pair = U_MIX1 + v, 2 * (v % 2)
                if 2 <= v < 12:
                    pe.wait_ge(m1_act, 2 * (v - 1))
                elif 12 <= v < 16:
                    pe.wait_ge(m1_dve, 2 * (v - 11))
                elif v >= 16:
                    pe.wait_ge(m1_act, 20 + 2 * (v - 15))
                hooks = hgrn_hooks(v)
                if v in (6, 7):
                    dense_tokens(u, pair, nhi, nlo, TT, hooks)
                elif v < MIX1_UNITS:
                    dense(u, pair, nhi, nlo, after_norm(N_MIX1) if v == 0 else None, hooks=hooks)
                elif v < MIX1_UNITS + 4:
                    if v == MIX1_UNITS:
                        pe.wait_ge(mem_ready, 1)
                    dense(u, pair, mnhi, mnlo, width=MEM, hooks=hooks)
                else:
                    dense_tokens(u, pair, mnhi, mnlo, 2)
                if v == 1:
                    pe.wait_ge(mem_loaded, 16)
                    for c in range(C):
                        for i in range(2):
                            col = (c % 2) * MEM + i * P
                            mm = pe.transpose(bank[4 + c // 2][:, col:col + P], mem_tok[:, i, c * P:(c + 1) * P], ident[:, :])
                        if c % 2:
                            mm.then_inc(mem_turned, 1)
                if v == 3:
                    pe.wait_ge(memsq_ready, 1)
                    for c in range(C):
                        mm = pe.matmul(bank[4][:, 0:MEM], ones[:, :], memsq[:, c, :], start=(c == 0), stop=(c == C - 1))
                    mm.then_inc(mem_summed, 1)
            for j in range(SQUARE_UNITS):
                if j == 0:
                    pe.wait_ge(y1_ready, C)
                if j < 2:
                    pe.wait_ge(m1_act, 34 + 2 * j)
                else:
                    pe.wait_ge(x_ready, C * X_MIX1 + 2 * (j - 1))
                dense(U_OUT1 + j, 2 * (j % 2), nhi, nlo)
            sum_squares(N_ATT, 7)

            def att_scores(h):
                pe.wait_ge(qx_ready, 2 * h + 2)
                if h:
                    pe.wait_ge(ax_copied, 2 * h)
                for i in range(TT):
                    for c in range(2):
                        mm = pe.matmul(bank[4 + i // 2][:, (i % 2) * MEM:(i % 2) * MEM + MEM],
                                       qx[:, 2 * h + c, i * P:(i + 1) * P], km[:, 2 * h + c, :], start=(c == 0), stop=(c == 1))
                    if i % 2:
                        mm.then_inc(sx_done, 1)

            def att_turn(h):
                for i in range(TT):
                    pe.wait_ge(px_norm, TT * h + i + 1)
                    for m in range(2):
                        mm = pe.transpose(bank[6 + m][:, i * P:(i + 1) * P], px[:, i, m * P:(m + 1) * P], ident[:, :])
                mm.then_inc(tx_done, 1)

            def att_out(h):
                pe.wait_ge(ptx_ready, 2 * h + 2)
                for c in range(2):
                    for m in range(2):
                        mm = pe.matmul(bank[4 + c][:, :], vm[:, m, h * 256 + c * P:h * 256 + c * P + P], ptx[:, m, :],
                                       start=(m == 0), stop=(m == 1))
                    mm.then_inc(ax_done, 1)

            for j in range(SQUARE_UNITS):
                if j >= 2:
                    pe.wait_ge(qx_ready, 2 * (j - 1))
                dense(U_Q + j, 2 * (j % 2), nhi, nlo, after_norm(N_ATT) if j == 0 else None)
                if j >= 2:
                    att_turn(j - 2)
                    att_out(j - 2)
                if j >= 1:
                    att_scores(j - 1)
            for h in (2, 3):
                att_turn(h)
                att_out(h)
                if h == 2:
                    att_scores(3)
            for j in range(SQUARE_UNITS):
                if j == 0:
                    pe.wait_ge(ax_ready, C)
                if j >= 2:
                    pe.wait_ge(x_ready, C * X_ATT + 2 * (j - 1))
                dense(U_O + j, 2 * (j % 2), nhi, nlo)
            sum_squares(N_FFN2, 7)
            ffn_products(1, U_FFN2, N_FFN2)
            sum_squares(N_FINAL, 0)
            sum_squares(N_MIX2, 1)

            def map_qk(m, part):
                q_, k_ = (mq, mk) if m < 8 else (dq, dk)
                c, rows = (m % 8) // 2, slice(64 * (m % 2), 64 * (m % 2) + 64)
                if part == 0:
                    pe.wait_ge(m2_act, (4 + 2 * (c // 2 + 1)) if m < 8 else (12 + 4 + 2 * (c // 2 + 1)))
                    if m:
                        pe.wait_ge(map_max, 4 * m)
                if part == 2 and m >= 2:
                    if m <= 10:
                        pe.wait_ge(ya_copied, min(m - 1, 8))
                    else:
                        pe.wait_ge(yb_sq, (m - 11) // 2 + 1)
                for i in ((3,), (2, 0), (1,))[part]:
                    b = bank[4 + part]
                    col = 384 if i == 0 else 0
                    pe.matmul(b[:, col:col + P * (i + 1)], q_[rows, c, i * P:(i + 1) * P], k_[rows, c, 0:P * (i + 1)],
                              start=True, stop=True).then_inc(map_scores, 1)

            def map_turn(m, r):
                n = m if m < 8 else 8 + (m - 8) // 2
                if r == 0:
                    pe.wait_ge(map_norm, 4 * m + 4)
                if n or r:
                    pe.wait_ge(map_pt, 3 * n + r)
                if m > 8 and r == 0 and m >= 11:
                    pe.wait_ge(yb_rstd, 2 * ((m - 9) // 2) - 1)
                for j in ((0,), (1, 3), (2,))[r]:
                    col0 = 384 if j == 3 else 0
                    for i in range(j, TT):
                        mm = pe.transpose(bank[7][:, col0 + (i - j) * P:col0 + (i - j + 1) * P],
                                          pm[m % 2][:, TILE_AT[i] + j * P:TILE_AT[i] + (j + 1) * P], ident[:, :])
                mm.then_inc(map_turned, 1)

            def map_out(m):
                n = m if m < 8 else 8 + (m - 8) // 2
                pe.wait_ge(map_pt, 3 * n + 3)
                pe.wait_ge(map_max, 4 * min(m + 2, MAPS))
                pe.wait_ge(m2_act, 12 if m < 8 else 24)
                for j in range(TT):
                    if m < 8:
                        lhs, rows = mv[:, j, 64 * m:64 * m + 64], slice(64 * (m % 2), 64 * (m % 2) + 64)
                    else:
                        h = (m - 8) // 2
                        lhs, rows = dv[:, j, P * h:P * h + P], slice(0, P)
                    mm = pe.matmul(bank[6][rows, P * j:T], lhs, ptm[:, KEYS_AT[j]:KEYS_AT[j] + T - P * j],
                                   start=(j == 0), stop=(j == TT - 1))
                mm.then_inc(av_done, 1)

            def map_sum(h):
                pe.wait_ge(yb_sq, h + 1)
                n = 8 + h
                pe.wait_ge(map_pt, 3 * n + 3)
                pe.matmul(bank[7][:, :], ones[:, :], ysq[:, :], start=True, stop=True).then_inc(yb_summed, 1)

            def has_out(m):
                return 0 <= m < 8 or (8 <= m < MAPS and m % 2 == 1)

            def map_hooks(v):
                hooks = {}
                m = v - 5
                if 0 <= m < MAPS:
                    for part in range(3):
                        hooks[part] = (lambda m, part: lambda: map_qk(m, part))(m, part)
                o = v - 6
                if has_out(o):
                    for r in range(3):
                        hooks[3 + r] = (lambda o, r: lambda: map_turn(o, r))(o, r)
                    hooks[7] = (lambda o: lambda: map_out(o))(o)
                s_ = v - 7
                if 8 <= s_ < MAPS and s_ % 2:
                    hooks[6] = (lambda h: lambda: map_sum(h))((s_ - 9) // 2)
                return hooks

            for v in range(MIX2_UNITS):
                if v >= 2:
                    pe.wait_ge(m2_act, 2 * (v - 1))
                if v in (4, 5, 10, 11):
                    dense_tokens(U_MIX2 + v, 2 * (v % 2), nhi, nlo, TT, map_hooks(v))
                else:
                    dense(U_MIX2 + v, 2 * (v % 2), nhi, nlo, after_norm(N_MIX2 - 1) if v == 0 else None, hooks=map_hooks(v))
            for v in range(MIX2_UNITS, MIX2_UNITS + 3):
                hooks = map_hooks(v)
                for k in sorted(hooks):
                    hooks[k]()

            for j in range(BRANCH_UNITS):
                u = U_BRANCH + j
                unit_split(u)
                if j == 0:
                    pe.wait_ge(m2_act, 2 * MIX2_UNITS)
                    pe.wait_ge(y2_ready, C)
                if j == 1:
                    pe.wait_ge(yb_rstd, 7)
                if j == 2:
                    pe.wait_ge(br_a, 4)
                if j == 3:
                    pe.wait_ge(br_b, 4)
                for m in range(4):
                    for k in range(4):
                        w0 = k * 512 + m * P
                        mm = products(bank[4 * (j % 2) + m][:, :], whi[u % 2][:, w0:w0 + P], wlo[u % 2][:, w0:w0 + P],
                                      nhi[:, 4 * (j % 2) + k, :], nlo[:, 4 * (j % 2) + k, :], k == 0, k == 3)
                mm.then_inc(unit_done, 1)
            for j in range(SQUARE_UNITS):
                if j == 0:
                    pe.wait_ge(br_a, C)
                if j >= 2:
                    pe.wait_ge(ypost_ready, 2 * (j - 1))
                dense(U_OUT2 + j, 2 * (j % 2), mhi, mlo,
                      (lambda k: pe.wait_ge(br_ready, k + 1)) if j == 0 else None)
            sum_squares(N_POST2, 6)
            sum_squares(N_FFN3, 7)
            ffn_products(2, U_FFN3, N_FFN3 - 2)
            sum_squares(N_POST3, 0)
            for c in range(C):
                pe.wait_ge(x_ready, C * X_FFN3 + c + 1)
            for i in range(TT):
                for half in range(2):
                    for c in range(4):
                        mm = pe.transpose(bank[2 * i + half][:, c * P:(c + 1) * P],
                                          x[:, 4 * half + c, i * P:(i + 1) * P], ident[:, :])
                    mm.then_inc(out_turned, 1)

        @block.scalar
        def _(act):
            def split(par, half, first=False):
                act.wait_ge(w_loaded[par], 32 * half + 32)
                if not first:
                    act.wait_ge(unit_done, 2 * half + (par - 1))
                act.copy(whi[par][:, :], raw[par][:, :]).then_inc(w_hi_ready, 1)

            def split_unit(u):
                if u < UNITS:
                    split(u % 2, u // 2, first=(u < 2))

            def squares(norm, source, wait):
                for c in range(C):
                    wait(c)
                    if norm or c >= 2:
                        act.wait_ge(sq_summed, C * norm + c - 1)
                    act.activation(sq[c % 2][:, :], source[:, c, :], ACT.Square).then_inc(sq_ready, 1)

            def inverse_root(norm, b):
                act.wait_ge(sq_summed, C * norm + C)
                act.activation(lnt[:, :], bank[b][:, :], ACT.Ln, scale=1.0 / D, bias=EPS).then_inc(ln_done, 1)
                act.wait_ge(ln_done, norm + 1)
                act.activation(rstd[:, :], lnt[:, :], ACT.Exp, scale=-0.5).then_inc(rstd_ready, 1)

            def norm_hi(norm, use):
                for c in range(C):
                    act.wait_ge(scaled, C * use + c + 1)
                    act.copy(nhi[:, c, :], tmp[c % 2][:, :]).then_inc(n_hi_ready, 1)

            def x_at(version):
                return lambda c: act.wait_ge(x_ready, C * version + c + 1)

            def ffn_steps(f, base):
                s_ = ffn[f]

                def gate_up(par, half, j, jj, first):
                    split(par, half)
                    act.wait_ge(unit_done, 2 * half + (par - 1))
                    if not first:
                        act.wait_ge(s_["h_product"], j - 1)
                    act.activation(sq[jj][:, :], bank[2 * jj][:, :], ACT.Silu).then_inc(s_["silu_ready"], 1)
                    act.wait_ge(s_["h_product"], j + 1)
                    if isinstance(j, int):
                        dst = hhi[:, j, :]
                    else:
                        dst = hhi[:, bass.ds(j, 1), :].rearrange("p o t -> p (o t)")
                    act.copy(dst, tmp[jj][:, :]).then_inc(s_["h_hi_ready"], 1)

                b = base + 2
                for j in range(2):
                    gate_up((b + j) % 2, (b + j) // 2, j, j, True)
                with act.Fori(1, GATE_UNITS // 2) as i:
                    for j in range(2):
                        gate_up((b + j) % 2, i + (b + j) // 2, 2 * i + j, j, False)
                b = base + GATE_UNITS + 2
                with act.Fori(0, (DOWN_UNITS - 3) // 2) as i:
                    for j in range(2):
                        split((b + j) % 2, i + (b + j) // 2)
                for n in (DOWN_UNITS - 3, DOWN_UNITS - 2):
                    split_unit(b + n)

            split_unit(0)
            for c in range(C):
                act.wait_ge(x_turned, c + 1)
                act.copy(x[:, c, :], bank[c][:, :]).then_inc(x_ready, 1)
                if c >= 1:
                    pass
            squares(N_FFN1, x, x_at(X_LOAD))
            split_unit(1)
            inverse_root(N_FFN1, 0)
            norm_hi(N_FFN1, 0)
            act.wait_ge(small_steps, 4)
            act.activation(small[:, LBE:LBE + 8], small[:, LBE:LBE + 8], ACT.Exp).then_inc(lb_exp, 1)
            ffn_steps(0, U_FFN1)
            squares(N_MIX1, x, x_at(X_FFN1))
            inverse_root(N_MIX1, 0)
            norm_hi(N_MIX1, 1)
            split_unit(U_MIX1 + 1)

            def pairs(t, L, which):
                return t.rearrange("p (n two l) -> p n two l", two=2, l=L)[:, :, which, :]

            def hgrn_decays(h, levels):
                for l in levels:
                    g, L = LEVELS * h + l, 1 << l
                    if l == 0:
                        act.wait_ge(logf_ready, h + 1)
                    act.wait_ge(sums_ready, 17 * h + 1 + 2 * l)
                    if g >= 2:
                        act.wait_ge(qk_used, g - 1)
                    act.activation(pairs(qk[g % 2][:, :], L, 1), pairs(hf[:, h, :], L, 1), ACT.Exp).then_inc(decay_ready, 1)
                    act.activation(pairs(qk[g % 2][:, :], L, 0), pairs(hsuf[:, :], L, 0), ACT.Exp).then_inc(decay_ready, 1)

            def far_scores(h):
                act.wait_ge(qk_used, LEVELS * (h + 1))
                if h:
                    act.wait_ge(o_done, h)
                else:
                    act.wait_ge(pt_zero, 1)
                tile = pt[:, :].rearrange("p (j c) -> p j c", c=640)
                act.copy(tile[0:64, :, 64:128], bank[6][0:64, 0:256].rearrange("p (j c) -> p j c", j=TT)).then_inc(scores_act, 1)
                act.copy(tile[:, 0:3:2, 128:256], bank[6][:, 256:512].rearrange("p (j c) -> p j c", j=2)).then_inc(scores_act, 1)
                half = pt[:, 0:1024].rearrange("p (j c) -> p j c", c=512)
                act.copy(half[:, :, 256:512], bank[7][:, :].rearrange("p (j c) -> p j c", j=2)).then_inc(scores_act, 1)

            for v in range(MIX1_UNITS + KV_UNITS):
                u, pair = U_MIX1 + v, 2 * (v % 2)
                split_unit(u + 2)
                act.wait_ge(unit_done, u + 1)
                for b in range(2):
                    src = bank[pair + b][:, :]
                    ch = 2 * (v % 2) + b
                    if v < 2:
                        act.activation(hq[:, ch, :], src, ACT.Silu).then_inc(m1_act, 1)
                    elif v < 4:
                        act.activation(hg[:, ch, :], src, ACT.Silu).then_inc(m1_act, 1)
                    elif v < 6:
                        act.activation(hf[:, ch, :], src, ACT.Sigmoid).then_inc(m1_act, 1)
                    elif v < 8:
                        act.copy(hv[:, 2 * b:2 * b + 2, 256 * (v % 2):256 * (v % 2) + 256],
                                 src.rearrange("p (i n) -> p i n", i=2)).then_inc(m1_act, 1)
                    elif v < 10:
                        if b == 0 and v == 8:
                            act.wait_ge(mem_hi_ready, 1)
                            act.wait_ge(mem_ready, 1)
                        act.copy(cu[:, ch, 2:T + 2], src).then_inc(m1_act, 1)
                    elif 14 <= v < 18:
                        if v == 14 and b == 0:
                            act.wait_ge(qk_ready, 2 * LEVELS * HEADS)
                        act.copy(km[:, 2 * (v - 14) + b, :], bank[pair + b][:, 0:MEM]).then_inc(m1_act, 1)
                    elif v >= 18:
                        if v == 18 and b == 0:
                            act.wait_ge(diag_done, HEADS)
                            act.wait_ge(qk_used, LEVELS * HEADS)
                        act.copy(vm[:, b, 256 * (v - 18):256 * (v - 18) + 256], bank[pair + b][:, 0:256]).then_inc(m1_act, 1)
                if v in (4, 5):
                    for h in range(2 * (v - 4), 2 * (v - 4) + 2):
                        act.wait_ge(f_steps, 2 * h + 2)
                        act.activation(hf[:, h, :], hf[:, h, :], ACT.Ln).then_inc(logf_ready, 1)
                if v == 1:
                    for b in range(4):
                        act.wait_ge(mem_turned, b + 1)
                        act.copy(memt[:, 2 * b:2 * b + 2, :], bank[4 + b][:, :].rearrange("p (c t) -> p c t", c=2)).then_inc(memt_ready, 1)
                    act.wait_ge(memt_ready, 4)
                    act.activation(memsq[:, :, :], memt[:, :, :], ACT.Square).then_inc(memsq_ready, 1)
                if v == 3:
                    act.wait_ge(mem_summed, 1)
                    act.activation(lnt[:, 0:MEM], bank[4][:, 0:MEM], ACT.Ln, scale=1.0 / D, bias=EPS).then_inc(mem_rstd, 1)
                    act.wait_ge(mem_rstd, 1)
                    act.activation(rstd[:, 0:MEM], lnt[:, 0:MEM], ACT.Exp, scale=-0.5).then_inc(mem_rstd, 1)
                if v == 5:
                    act.wait_ge(mem_scaled, C)
                    act.copy(mnhi[:, :, :], memt[:, :, :]).then_inc(mem_hi_ready, 1)
                for h in range(HEADS):
                    if v == 8 + 2 * h:
                        far_scores(h)
                    if v == 9 + 2 * h:
                        act.wait_ge(o_done, h + 1)
                        if h:
                            act.wait_ge(y_steps, 2 * h)
                        act.copy(osb[:, :], bank[7][:, :]).then_inc(o_copied, 1)
                        act.activation(osq[:, :], bank[7][:, :], ACT.Square).then_inc(o_copied, 1)
                        act.wait_ge(o_summed, h + 1)
                        act.activation(orstd[:, :], bank[6][:, :], ACT.Ln, scale=1.0 / P, bias=EPS).then_inc(o_rstd, 1)
                        act.wait_ge(o_rstd, 2 * h + 1)
                        act.activation(orstd[:, :], orstd[:, :], ACT.Exp, scale=-0.5).then_inc(o_rstd, 1)
                for h in range(HEADS):
                    if v == 6 + 2 * h:
                        hgrn_decays(h, range(5))
                    if v == 7 + 2 * h:
                        hgrn_decays(h, range(5, LEVELS))
                for n, c in y1_order(v):
                    act.wait_ge(y_steps if c < 4 else m1_dve, 2 * c + 2 if c < 4 else c + 1)
                    src = hq[:, c, :] if c < 4 else cv[:, c - 4, :]
                    act.copy(nhi[:, c, :], src).then_inc(y1_hi, 1)
            for j in range(SQUARE_UNITS):
                if j < 3:
                    split_unit(U_OUT1 + j + 2)
            squares(N_ATT, x, x_at(X_MIX1))
            inverse_root(N_ATT, 7)
            norm_hi(N_ATT, 2)
            split_unit(U_Q + 1)

            def att_exp(h):
                for i in range(TT):
                    if i % 2 == 0:
                        act.wait_ge(mx_ready, 2 * h + i // 2 + 1)
                    if i == 0 and h:
                        act.wait_ge(tx_done, h)
                    act.activation(px[:, i, :], bank[4 + i // 2][:, (i % 2) * MEM:(i % 2) * MEM + MEM], ACT.Exp,
                                   bias=small[:, 32 + i:33 + i], accum_out=small[:, 36 + i:37 + i]).then_inc(px_ready, 1)

            def att_copies(h):
                act.wait_ge(tx_done, h + 1)
                if h:
                    act.wait_ge(ax_done, 2 * h)
                for m in range(2):
                    act.copy(ptx[:, m, :], bank[6 + m][:, :]).then_inc(ptx_ready, 1)
                for c in range(2):
                    act.wait_ge(ax_done, 2 * h + c + 1)
                    act.copy(qx[:, 2 * h + c, :], bank[4 + c][:, :]).then_inc(ax_copied, 1)

            for j in range(SQUARE_UNITS):
                split_unit(U_Q + j + 2)
                act.wait_ge(unit_done, U_Q + j + 1)
                for b in range(2):
                    act.activation(qx[:, 2 * j + b, :], bank[2 * (j % 2) + b][:, :], ACT.Copy, scale=256.0 ** -0.5).then_inc(qx_ready, 1)
                if j >= 2:
                    att_copies(j - 2)
                if j >= 1:
                    att_exp(j - 1)
            att_copies(2)
            att_exp(3)
            att_copies(3)
            for c in range(C):
                act.wait_ge(ax_copied, c + 1)
                act.copy(nhi[:, c, :], qx[:, c, :]).then_inc(ax_hi, 1)
            for j in range(SQUARE_UNITS):
                if j < 3:
                    split_unit(U_O + j + 2)
            squares(N_FFN2, x, x_at(X_ATT))
            inverse_root(N_FFN2, 7)
            norm_hi(N_FFN2, 3)
            split_unit(U_FFN2 + 1)
            ffn_steps(1, U_FFN2)
            squares(N_FINAL, x, x_at(X_FFN2))
            inverse_root(N_FINAL, 0)
            squares(N_MIX2, x, x_at(X_FINAL))
            inverse_root(N_MIX2, 1)
            norm_hi(N_MIX2, 4)
            split_unit(U_MIX2 + 1)

            act.wait_ge(lam_steps, 2)
            act.activation(small[:, LEXP:LEXP + 2], small[:, LSUM:LSUM + 2], ACT.Exp).then_inc(lam_exp, 1)

            def map_exps(m):
                for n, i in enumerate((3, 2, 0, 1)):
                    act.wait_ge(map_neg, m + 1)
                    w = P * (i + 1)
                    p_ = pm[m % 2][:, TILE_AT[i]:TILE_AT[i] + w]
                    act.activation(p_, p_, ACT.Exp, bias=stat[:, m % 2, 1, i:i + 1],
                                   accum_out=stat[:, m % 2, 2, i:i + 1]).then_inc(map_exp, 1)

            def map_copies(m):
                n = m if m < 8 else 8 + (m - 8) // 2
                if n:
                    act.wait_ge(av_done, n)
                for r, (lo, hi) in enumerate(((0, 512), (512, 1024), (1024, 1280))):
                    act.wait_ge(map_turned, 3 * n + r + 1)
                    act.copy(ptm[:, lo:hi], bank[7][:, 0:hi - lo]).then_inc(map_pt, 1)

            def map_y(m):
                if m < 8:
                    act.wait_ge(av_done, m + 1)
                    rows = slice(64 * (m % 2), 64 * (m % 2) + 64)
                    act.copy(mq[rows, m // 2, :], bank[6][rows, :]).then_inc(ya_copied, 1)
                else:
                    h = (m - 8) // 2
                    act.wait_ge(av_done, 8 + h + 1)
                    if h:
                        act.wait_ge(yb_summed, h)
                    act.copy(dq[:, h, :], bank[6][:, :]).then_inc(yb_copied, 1)
                    act.activation(ysq[:, :], bank[6][:, :], ACT.Square).then_inc(yb_sq, 1)

            def map_root(h):
                act.wait_ge(yb_summed, h + 1)
                if h:
                    act.wait_ge(y2_steps, h)
                act.activation(yrstd[:, :], bank[7][:, :], ACT.Ln, scale=1.0 / P, bias=EPS_SUBLN).then_inc(yb_rstd, 1)
                act.wait_ge(yb_rstd, 2 * h + 1)
                act.activation(yrstd[:, :], yrstd[:, :], ACT.Exp, scale=-0.5).then_inc(yb_rstd, 1)

            def has_out(m):
                return 0 <= m < 8 or (8 <= m < MAPS and m % 2 == 1)

            for v in range(MIX2_UNITS + 3):
                if has_out(v - 6):
                    map_y(v - 6)
                if v < MIX2_UNITS:
                    split_unit(U_MIX2 + v + 2)
                    act.wait_ge(unit_done, U_MIX2 + v + 1)
                    for b in range(2):
                        src = bank[2 * (v % 2) + b][:, :]
                        if v in (4, 5, 10, 11):
                            dst = (mv if v < 6 else dv)[:, 2 * b:2 * b + 2, 256 * (v % 2):256 * (v % 2) + 256]
                            act.copy(dst, src.rearrange("p (i n) -> p i n", i=2)).then_inc(m2_act, 1)
                        elif v < 12:
                            dst = {0: mq, 1: mk, 3: dq, 4: dk}[v // 2][:, 2 * (v % 2) + b, :]
                            act.activation(dst, src, ACT.Copy, scale=64.0 ** -0.5 if v // 2 in (0, 3) else 1.0).then_inc(m2_act, 1)
                        else:
                            if v == 16 and b == 0:
                                act.wait_ge(av_done, 8)
                            dst = (ga if v < 16 else gb)[:, 2 * (v % 4) + b, :]
                            act.activation(dst, src, ACT.Tanh, scale=0.5).then_inc(m2_act, 1)
                if 8 < v - 6 < MAPS + 1 and (v - 6) % 2 == 0:
                    map_root((v - 6 - 10) // 2)
                if has_out(v - 5):
                    map_copies(v - 5)
                if 0 <= v - 4 < MAPS:
                    map_exps(v - 4)
            for c in range(C):
                if c < 4:
                    act.wait_ge(ya_copied, 8)
                else:
                    act.wait_ge(y2_steps, c - 3)
                src = mq[:, c, :] if c < 4 else dq[:, c - 4, :]
                act.copy(nhi[:, c, :], src).then_inc(y2_hi, 1)
            for j in range(BRANCH_UNITS):
                split_unit(U_BRANCH + j + 2)
                if j % 2:
                    for c in range(4 * (j // 2), 4 * (j // 2) + 4):
                        act.wait_ge(br_sum, c + 1)
                        act.copy(mhi[:, c, :], tmp[c % 2][:, :]).then_inc(br_hi, 1)
            for j in range(SQUARE_UNITS):
                split_unit(U_OUT2 + j + 2) if j < 3 else None
                act.wait_ge(unit_done, U_OUT2 + j + 1)
                for b in range(2):
                    act.activation(ypost[:, 2 * j + b, :], bank[2 * (j % 2) + b][:, :], ACT.Copy, scale=0.5).then_inc(ypost_ready, 1)
            squares(N_POST2, ypost, lambda c: act.wait_ge(ypost_ready, c + 1))
            inverse_root(N_POST2, 6)
            squares(N_FFN3, x, x_at(X_MIX2))
            inverse_root(N_FFN3, 7)
            norm_hi(N_FFN3, 6)
            split_unit(U_FFN3 + 1)
            ffn_steps(2, U_FFN3)
            for c in range(C):
                if c < C - 1:
                    act.wait_ge(ffn[2]["down_done"], c + 1)
                else:
                    act.wait_ge(unit_done, UNITS)
                act.copy(ypost[:, c, :], bank[c][:, :]).then_inc(ypost_ready, 1)
            squares(N_POST3, ypost, lambda c: act.wait_ge(ypost_ready, C + c + 1))
            inverse_root(N_POST3, 0)

        @block.vector
        def _(dve):
            def split(par, half):
                dve.wait_ge(w_hi_ready, 2 * half + (par + 1))
                dve.tensor_tensor(wlo[par][:, :], raw[par][:, :], whi[par][:, :].bitcast(F32), ALU.subtract).then_inc(w_lo_ready, 1)

            def split_unit(u):
                if u < UNITS:
                    split(u % 2, u // 2)

            def norm_chunks(norm, use, name):
                def lo(c):
                    dve.wait_ge(n_hi_ready, C * use + c + 1)
                    dve.tensor_tensor(nlo[:, c, :], tmp[c % 2][:, :], nhi[:, c, :].bitcast(F32), ALU.subtract).then_inc(n_ready, 1)

                dve.wait_ge(rstd_ready, norm + 1)
                for c in range(C):
                    if c >= 2:
                        dve.wait_ge(n_ready, C * use + c - 1)
                    dve.scalar_tensor_tensor(tmp[c % 2][:, :], x[:, c, :], gain(name, c), rstd[:, :],
                                             ALU.mult, ALU.mult).then_inc(scaled, 1)
                    if c:
                        lo(c - 1)
                lo(C - 1)

            def add_down(f, version, base):
                for c in range(C):
                    if c < C - 1:
                        dve.wait_ge(ffn[f]["down_done"], c + 1)
                    else:
                        dve.wait_ge(unit_done, base + FFN_UNITS)
                    dve.scalar_tensor_tensor(x[:, c, :], bank[c][:, :], 0.5, x[:, c, :], ALU.mult, ALU.add).then_inc(x_ready, 1)

            def add_square(base, last):
                for j in range(SQUARE_UNITS):
                    if j < 3:
                        split_unit(base + j + 2)
                    dve.wait_ge(unit_done, base + j + 1)
                    for b in range(2):
                        c = 2 * j + b
                        dve.tensor_tensor(x[:, c, :], bank[2 * (j % 2) + b][:, :], x[:, c, :], ALU.add).then_inc(x_ready, 1)

            def post_norm(norm, name, use, version):
                dve.wait_ge(rstd_ready, norm + 1)
                for c in range(C):
                    dve.scalar_tensor_tensor(tmp[c % 2][:, :], ypost[:, c, :], gain(name, c), rstd[:, :],
                                             ALU.mult, ALU.mult).then_inc(scaled, 1)
                    dve.wait_ge(scaled, C * use + c + 1)
                    dve.tensor_tensor(x[:, c, :], tmp[c % 2][:, :], x[:, c, :], ALU.add).then_inc(x_ready, 1)

            def ffn_steps(f, base):
                s_ = ffn[f]

                def gate_up(par, half, j, jj):
                    split(par, half)
                    dve.wait_ge(s_["silu_ready"], j + 1)
                    dve.tensor_tensor(tmp[jj][:, :], sq[jj][:, :], bank[2 * jj + 1][:, :], ALU.mult).then_inc(s_["h_product"], 1)
                    dve.wait_ge(s_["h_hi_ready"], j + 1)
                    if isinstance(j, int):
                        dst, hi = hlo[:, j, :], hhi[:, j, :].bitcast(F32)
                    else:
                        dst = hlo[:, bass.ds(j, 1), :].rearrange("p o t -> p (o t)")
                        hi = hhi[:, :, :].bitcast(F32)[:, bass.ds(j, 1), :].rearrange("p o t -> p (o t)")
                    dve.tensor_tensor(dst, tmp[jj][:, :], hi, ALU.subtract).then_inc(s_["h_ready"], 1)

                b = base + 2
                for j in range(2):
                    gate_up((b + j) % 2, (b + j) // 2, j, j)
                with dve.Fori(1, GATE_UNITS // 2) as i:
                    for j in range(2):
                        gate_up((b + j) % 2, i + (b + j) // 2, 2 * i + j, j)
                b = base + GATE_UNITS + 2
                with dve.Fori(0, (DOWN_UNITS - 3) // 2) as i:
                    for j in range(2):
                        split((b + j) % 2, i + (b + j) // 2)
                for n in (DOWN_UNITS - 3, DOWN_UNITS - 2):
                    split_unit(b + n)

            dve.wait_ge(mask_iota, 2)
            dve.tensor_scalar(maskt[:, 0, :], maskt[:, 0, :], 31, None, ALU.bitwise_and).then_inc(mask_steps, 1)
            dve.wait_ge(mask_steps, 1)
            dve.tensor_tensor(maskt[:, 2, :], maskt[:, 1, :], maskt[:, 0, :], ALU.is_gt).then_inc(mask_steps, 1)
            dve.tensor_tensor(masks[:, 0, :], maskt[:, 1, :], maskt[:, 0, :], ALU.bitwise_xor).then_inc(mask_steps, 1)
            dve.wait_ge(mask_steps, 3)
            for l in range(5):
                dve.scalar_tensor_tensor(masks[:, 1 + l, :], masks[:, 0, :], float(1 << l), maskt[:, 2, :],
                                         ALU.is_ge, ALU.mult).then_inc(mask_steps, 1)
            dve.wait_ge(mask_steps, 8)
            dve.tensor_scalar(masks[:, 0, :], masks[:, 0, :], 0.0, None, ALU.is_equal).then_inc(mask_steps, 1)
            split_unit(0)
            split_unit(1)
            dve.wait_ge(gains_t, 1)
            dve.tensor_copy(gains[:, :], bank[1][:, 0:GAINS]).then_inc(gains_ready, 1)
            dve.wait_ge(gains_ready, 1)
            norm_chunks(N_FFN1, 0, "ffn1_norm")
            g0 = GAIN_AT["lb_param"]
            r0, r1 = gains[:, g0:g0 + 4], gains[:, g0 + 4:g0 + 8]
            dve.tensor_tensor(small[:, LB:LB + 4], r0, r1, ALU.max).then_inc(small_steps, 1)
            dve.wait_ge(small_steps, 1)
            dve.tensor_tensor(small[:, LBE:LBE + 4], r0, small[:, LB:LB + 4], ALU.subtract).then_inc(small_steps, 1)
            dve.tensor_tensor(small[:, LBE + 4:LBE + 8], r1, small[:, LB:LB + 4], ALU.subtract).then_inc(small_steps, 1)
            dve.tensor_scalar(small[:, SUBG:SUBG + 1], gain("diff_subln_g_2", 0), 1.0 - LAM_INIT, None, ALU.mult).then_inc(small_steps, 1)
            dve.wait_ge(lb_exp, 1)
            dve.tensor_tensor(small[:, LB:LB + 4], small[:, LBE:LBE + 4], small[:, LBE + 4:LBE + 8], ALU.add).then_inc(small_steps, 1)
            dve.wait_ge(small_steps, 5)
            dve.reciprocal(small[:, LB + 4:LB + 8], small[:, LB:LB + 4]).then_inc(small_steps, 1)
            dve.wait_ge(small_steps, 6)
            dve.tensor_tensor(small[:, LB:LB + 4], small[:, LBE:LBE + 4], small[:, LB + 4:LB + 8], ALU.mult).then_inc(small_steps, 1)
            dve.wait_ge(small_steps, 7)
            dve.tensor_scalar(small[:, OMLB:OMLB + 4], small[:, LB:LB + 4], -1.0, 1.0, ALU.mult, ALU.add).then_inc(small_steps, 1)
            dve.wait_ge(small_steps, 8)
            ffn_steps(0, U_FFN1)
            add_down(0, X_FFN1, U_FFN1)
            norm_chunks(N_MIX1, 1, "mix_norm")
            split_unit(U_MIX1 + 1)

            def pairs(t, L, which):
                return t.rearrange("p (n two l) -> p n two l", two=2, l=L)[:, :, which, :]

            def hgrn_levels(h, levels):
                for l in levels:
                    g, L = LEVELS * h + l, 1 << l
                    n = T // (2 * L)
                    if l == 0:
                        if g:
                            dve.wait_ge(decay_ready, 2 * g)
                        dve.memset(hsuf[:, :], 0.0).then_inc(sums_ready, 1)
                    dve.wait_ge(decay_ready, 2 * g + 2)
                    pre = hf[:, h, :]
                    dve.wait_ge(sums_ready, 17 * h + 1 + 2 * l)
                    if l < LEVELS - 1:
                        whole_odd = pairs(pre, L, 1)[:, :, L - 1:L].to_broadcast([P, n, L])
                        whole_even = pairs(pre, L, 0)[:, :, L - 1:L].to_broadcast([P, n, L])
                        dve.tensor_tensor(pairs(hsuf[:, :], L, 0), pairs(hsuf[:, :], L, 0), whole_odd, ALU.add).then_inc(sums_ready, 1)
                        dve.wait_ge(sums_ready, 17 * h + 2 + 2 * l)
                        dve.tensor_tensor(pairs(pre, L, 1), pairs(pre, L, 1), whole_even, ALU.add).then_inc(sums_ready, 1)
                    z = qk[g % 2][:, :]
                    dve.tensor_tensor(pairs(z, L, 1), pairs(z, L, 1), pairs(hq[:, h, :], L, 1), ALU.mult).then_inc(qk_ready, 1)
                    dve.tensor_tensor(pairs(z, L, 0), pairs(z, L, 0), pairs(hk[:, h, :], L, 0), ALU.mult).then_inc(qk_ready, 1)

            def near_scores(h):
                dve.wait_ge(diag_done, h + 1)
                dve.wait_ge(qk_used, LEVELS * h + 6)
                if h:
                    dve.wait_ge(scores_dve, 6 * h)
                dve.memset(s32[:, :, :], 0.0).then_inc(s32_steps, 1)
                for l in range(6):
                    dve.wait_ge(s32_steps, 7 * h + l + 1)
                    b, slot = (bank[4], l) if l < 4 else (bank[5], l - 4)
                    dve.copy_predicated(s32[:, :, :], masks[:, l:l + 1, :].to_broadcast([P, TT, 32]),
                                        b[:, slot * P:slot * P + P].rearrange("p (j t) -> p j t", j=TT)).then_inc(s32_steps, 1)
                dve.wait_ge(s32_steps, 7 * h + 7)
                if h:
                    dve.wait_ge(o_done, h)
                else:
                    dve.wait_ge(pt_zero, 1)
                tile = pt[:, :].rearrange("p (j c) -> p j c", c=640)
                for m in range(4):
                    r = slice(32 * m, 32 * m + 32)
                    dve.tensor_copy(tile[r, :, 32 * m:32 * m + 32], s32[r, :, :]).then_inc(scores_dve, 1)
                for m in range(2):
                    r = slice(64 * m, 64 * m + 32)
                    dve.tensor_copy(tile[r, :, 64 * m + 32:64 * m + 64],
                                    bank[5][r, 256:384].rearrange("p (j c) -> p j c", j=TT)).then_inc(scores_dve, 1)

            for v in range(MIX1_UNITS + KV_UNITS):
                u, pair = U_MIX1 + v, 2 * (v % 2)
                split_unit(u + 2)
                if v < 2:
                    for h in (2 * v, 2 * v + 1):
                        dve.wait_ge(m1_act, h + 1)
                        dve.tensor_scalar(hq[:, h, :], hq[:, h, :], 128.0 ** -0.5, None, ALU.mult).then_inc(q_scaled, 1)
                if v in (4, 5):
                    for h in (2 * (v - 4), 2 * (v - 4) + 1):
                        dve.wait_ge(m1_act, 8 + h + 1)
                        dve.tensor_scalar(hf[:, h, :], hf[:, h, :], small[:, OMLB + h:OMLB + h + 1],
                                          small[:, LB + h:LB + h + 1], ALU.mult, ALU.add).then_inc(f_steps, 1)
                        dve.wait_ge(f_steps, 2 * h + 1)
                        dve.tensor_scalar(hk[:, h, :], hf[:, h, :], -1.0, 1.0, ALU.mult, ALU.add).then_inc(f_steps, 1)
                if v == 4:
                    dve.wait_ge(mem_rstd, 2)
                    for c in range(C):
                        dve.scalar_tensor_tensor(memt[:, c, :], memt[:, c, :], gain("mem_norm", c), rstd[:, 0:MEM],
                                                 ALU.mult, ALU.mult).then_inc(mem_scaled, 1)
                if v == 5:
                    dve.wait_ge(mem_hi_ready, 1)
                    dve.tensor_tensor(mnlo[:, :, :], memt[:, :, :], mnhi[:, :, :].bitcast(F32), ALU.subtract).then_inc(mem_ready, 1)
                    dve.memset(pt[:, :], 0.0).then_inc(pt_zero, 1)
                if v == 8:
                    dve.wait_ge(mem_ready, 1)
                    dve.memset(cu[:, :, 0:2], 0.0).then_inc(conv_pad, 1)
                if v in (10, 11):
                    for b in range(2):
                        c = 2 * (v % 2) + b
                        n = 4 * c
                        dve.wait_ge(unit_done, u + 1)
                        dve.wait_ge(m1_act, 16 + 4)
                        dve.tensor_tensor(cu[:, c, 2:T + 2], cu[:, c, 2:T + 2], bank[pair + b][:, :], ALU.mult).then_inc(m1_dve, 1)
                        dve.wait_ge(m1_dve, c + 1)
                        dve.wait_ge(conv_pad, 1)
                        dve.tensor_scalar(cv[:, c, :], cu[:, c, 0:T], convw[:, c, 0:1], None, ALU.mult).then_inc(conv_steps, 1)
                        for j in (1, 2):
                            dve.wait_ge(conv_steps, 3 * c + j)
                            dve.scalar_tensor_tensor(cv[:, c, :], cu[:, c, j:T + j], convw[:, c, j:j + 1], cv[:, c, :],
                                                     ALU.mult, ALU.add).then_inc(conv_steps, 1)
                if v in (12, 13):
                    for b in range(2):
                        c = 2 * (v % 2) + b
                        dve.wait_ge(unit_done, u + 1)
                        dve.wait_ge(conv_steps, 3 * c + 3)
                        dve.tensor_tensor(cv[:, c, :], cv[:, c, :], bank[pair + b][:, :], ALU.mult).then_inc(m1_dve, 1)
                for h in range(HEADS):
                    if v == 8 + 2 * h:
                        near_scores(h)
                    if v == 10 + 2 * h:
                        dve.wait_ge(o_rstd, 2 * h + 2)
                        dve.scalar_tensor_tensor(osb[:, :], osb[:, :], gain("hgrn_out_norm", h), orstd[:, :],
                                                 ALU.mult, ALU.mult).then_inc(y_steps, 1)
                        dve.wait_ge(y_steps, 2 * h + 1)
                        dve.tensor_tensor(hq[:, h, :], osb[:, :], hg[:, h, :], ALU.mult).then_inc(y_steps, 1)
                for h in range(HEADS):
                    if v == 6 + 2 * h:
                        hgrn_levels(h, range(5))
                    if v == 7 + 2 * h:
                        hgrn_levels(h, range(5, LEVELS))
                for n, c in y1_order(v):
                    dve.wait_ge(y1_hi, n + 1)
                    src = hq[:, c, :] if c < 4 else cv[:, c - 4, :]
                    dve.tensor_tensor(nlo[:, c, :], src, nhi[:, c, :].bitcast(F32), ALU.subtract).then_inc(y1_ready, 1)
            add_square(U_OUT1, X_MIX1)
            norm_chunks(N_ATT, 2, "xattn_norm")
            split_unit(U_Q + 1)

            def att_softmax(h):
                for b in range(2):
                    dve.wait_ge(sx_done, 2 * h + b + 1)
                    if h and b == 0:
                        dve.wait_ge(px_ready, TT * h)
                    dve.tensor_reduce(small[:, 32 + 2 * b:34 + 2 * b], bank[4 + b][:, :].rearrange("p (i m) -> p i m", i=2),
                                      AX_X, ALU.max, negate=True).then_inc(mx_ready, 1)
                dve.wait_ge(px_ready, TT * h + TT)
                dve.reciprocal(small[:, 40:44], small[:, 36:40]).then_inc(px_inv, 1)
                dve.wait_ge(px_inv, h + 1)
                for i in range(TT):
                    dve.tensor_scalar(px[:, i, :], px[:, i, :], small[:, 40 + i:41 + i], None, ALU.mult).then_inc(px_norm, 1)

            for j in range(SQUARE_UNITS):
                split_unit(U_Q + j + 2)
                if j >= 1:
                    att_softmax(j - 1)
            att_softmax(3)
            for c in range(C):
                dve.wait_ge(ax_hi, c + 1)
                dve.tensor_tensor(nlo[:, c, :], qx[:, c, :], nhi[:, c, :].bitcast(F32), ALU.subtract).then_inc(ax_ready, 1)
            add_square(U_O, X_ATT)
            norm_chunks(N_FFN2, 3, "ffn2_norm")
            split_unit(U_FFN2 + 1)
            ffn_steps(1, U_FFN2)
            add_down(1, X_FFN2, U_FFN2)
            dve.wait_ge(rstd_ready, N_FINAL + 1)
            for c in range(C):
                dve.scalar_tensor_tensor(x[:, c, :], x[:, c, :], gain("final_norm", c), rstd[:, :],
                                         ALU.mult, ALU.mult).then_inc(x_ready, 1)
            norm_chunks(N_MIX2, 4, "norm_mix_pre_g_2")
            split_unit(U_MIX2 + 1)

            dve.wait_ge(lam_loaded, 64)
            for n in range(2):
                dve.tensor_tensor_reduce(lams[:, :], lamv[:, 2 * n, :], lamv[:, 2 * n + 1, :], 1.0, 0.0, ALU.mult, ALU.add,
                                         small[:, LSUM + n:LSUM + n + 1]).then_inc(lam_steps, 1)
                dve.wait_ge(lam_steps, n + 1)
            dve.wait_ge(lam_exp, 1)
            dve.tensor_tensor(small[:, NLAM:NLAM + 1], small[:, LEXP + 1:LEXP + 2], small[:, LEXP:LEXP + 1], ALU.subtract).then_inc(lam_steps, 1)
            dve.wait_ge(lam_steps, 3)
            dve.tensor_scalar(small[:, NLAM:NLAM + 1], small[:, NLAM:NLAM + 1], -LAM_INIT, None, ALU.add).then_inc(lam_steps, 1)
            dve.wait_ge(lam_steps, 4)

            def map_softmax(m):
                st = stat[:, m % 2]
                dve.wait_ge(bias_ready, m + 1)
                if m >= 2:
                    dve.wait_ge(map_norm, 4 * (m - 1))
                    outs = m - 1 if m <= 9 else 8 + (m - 1 - 8) // 2
                    if m - 2 < 8 or (m - 2) % 2:
                        dve.wait_ge(map_turned, 3 * outs)
                for n, i in enumerate((3, 2, 0, 1)):
                    w = P * (i + 1)
                    b = bank[{3: 4, 2: 5, 0: 5, 1: 6}[i]]
                    col = 384 if i == 0 else 0
                    dve.wait_ge(map_scores, 4 * m + (1, 3, 3, 4)[n])
                    dve.tensor_tensor_reduce(pm[m % 2][:, TILE_AT[i]:TILE_AT[i] + w], b[:, col:col + w],
                                             bias[m % 2][:, (3 - i) * P:T], 1.0, -3.0e38, ALU.add, ALU.max,
                                             st[:, 0, i:i + 1]).then_inc(map_max, 1)
                dve.wait_ge(map_max, 4 * m + 4)
                dve.tensor_scalar(st[:, 1, :], st[:, 0, :], -1.0, None, ALU.mult).then_inc(map_neg, 1)
                dve.wait_ge(map_exp, 4 * m + 4)
                dve.reciprocal(st[:, 3, :], st[:, 2, :]).then_inc(map_inv, 1)
                inv = m + 1 + max(0, (m - 8 + 0) // 2 if m >= 8 else 0)
                dve.wait_ge(map_inv, inv)
                if m >= 8 and m % 2:
                    dve.tensor_scalar(st[:, 3, :], st[:, 3, :], small[:, NLAM:NLAM + 1], None, ALU.mult).then_inc(map_inv, 1)
                    dve.wait_ge(map_inv, inv + 1)
                for n, i in enumerate((3, 2, 0, 1)):
                    w = P * (i + 1)
                    p_ = pm[m % 2][:, TILE_AT[i]:TILE_AT[i] + w]
                    if m >= 8 and m % 2:
                        dve.scalar_tensor_tensor(p_, p_, st[:, 3, i:i + 1], pm[0][:, TILE_AT[i]:TILE_AT[i] + w],
                                                 ALU.mult, ALU.add).then_inc(map_norm, 1)
                    else:
                        dve.tensor_scalar(p_, p_, st[:, 3, i:i + 1], None, ALU.mult).then_inc(map_norm, 1)
                dve.wait_ge(map_norm, 4 * m + 4)

            for v in range(MIX2_UNITS + 3):
                if v < MIX2_UNITS:
                    split_unit(U_MIX2 + v + 2)
                if 8 < v - 6 < MAPS + 1 and (v - 6) % 2 == 0:
                    h = (v - 6 - 10) // 2
                    dve.wait_ge(yb_rstd, 2 * h + 2)
                    dve.wait_ge(yb_copied, h + 1)
                    dve.scalar_tensor_tensor(dq[:, h, :], dq[:, h, :], small[:, SUBG:SUBG + 1], yrstd[:, :],
                                             ALU.mult, ALU.mult).then_inc(y2_steps, 1)
                if 0 <= v - 4 < MAPS:
                    map_softmax(v - 4)
            for c in range(C):
                dve.wait_ge(y2_hi, c + 1)
                src = mq[:, c, :] if c < 4 else dq[:, c - 4, :]
                dve.tensor_tensor(nlo[:, c, :], src, nhi[:, c, :].bitcast(F32), ALU.subtract).then_inc(y2_ready, 1)
            for j in range(BRANCH_UNITS):
                split_unit(U_BRANCH + j + 2)
                dve.wait_ge(unit_done, U_BRANCH + j + 1)
                for m in range(4):
                    c = 4 * (j // 2) + m
                    if j % 2 == 0:
                        dve.scalar_tensor_tensor(ga[:, c, :], ga[:, c, :], 1.0, bank[m][:, :], ALU.add, ALU.mult).then_inc(br_a, 1)
                    else:
                        dve.scalar_tensor_tensor(gb[:, c, :], gb[:, c, :], 1.0, bank[4 + m][:, :], ALU.add, ALU.mult).then_inc(br_b, 1)
                        dve.wait_ge(br_b, c + 1)
                        dve.wait_ge(br_a, c + 1)
                        dve.tensor_tensor(tmp[c % 2][:, :], ga[:, c, :], gb[:, c, :], ALU.add).then_inc(br_sum, 1)
                        dve.wait_ge(br_hi, c + 1)
                        dve.tensor_tensor(mlo[:, c, :], tmp[c % 2][:, :], mhi[:, c, :].bitcast(F32), ALU.subtract).then_inc(br_ready, 1)
            for j in range(3):
                split_unit(U_OUT2 + j + 2)
            post_norm(N_POST2, "norm_mix_post_g_2", 5, X_MIX2)
            norm_chunks(N_FFN3, 5, "norm_ffn_pre_g_2")
            split_unit(U_FFN3 + 1)
            ffn_steps(2, U_FFN3)
            post_norm(N_POST3, "norm_ffn_post_g_2", 7, X_FFN3)
            for n in range(2 * TT):
                dve.wait_ge(out_turned, n + 1)
                i, half = divmod(n, 2)
                dve.tensor_copy(out_tok[:, i, 512 * half:512 * half + 512], bank[n][:, :]).then_inc(out_ready, 1)


INPUTS = ["x", "mem", "ffn1_norm", "ffn1_gate", "ffn1_up", "ffn1_down", "mix_norm", "w_in", "lb_param",
          "hgrn_out_norm", "conv_w", "w_out", "xattn_norm", "mem_norm", "w_q_mem", "w_kv_mem", "w_o_mem",
          "ffn2_norm", "ffn2_gate", "ffn2_up", "ffn2_down", "final_norm", "norm_mix_pre_g_2", "w_in_2",
          "w_branch_a_2", "w_branch_b_2", "lam_q1_2", "lam_k1_2", "lam_q2_2", "lam_k2_2", "diff_subln_g_2",
          "w_out_2", "norm_mix_post_g_2", "norm_ffn_pre_g_2", "w_gate_2", "w_up_2", "w_down_2",
          "norm_ffn_post_g_2"]


def kernel(**inputs):
    import numpy as np
    import concourse.bacc as bacc
    from concourse.bass_utils import run_bass_kernel_spmd

    nc = bacc.Bacc("TRN2", target_bir_lowering=False, num_devices=1)
    arrays, aps = {}, {}
    for name in INPUTS:
        v = np.ascontiguousarray(inputs[name])
        arrays[f"in_{name}"] = v
        aps[name] = nc.dram_tensor(f"in_{name}", v.shape, mybir.dt.from_np(v.dtype), kind="ExternalInput").ap()
    out = nc.dram_tensor("out_dram", (1, T, D), F32, kind="ExternalOutput").ap()
    two_blocks(nc, aps, out)
    r = run_bass_kernel_spmd(nc, [arrays], core_ids=[0])
    return r.results[0]["out_dram"]
```

```python
import math
from contextlib import ExitStack

import concourse.bass as bass
from concourse import mybir

F32 = mybir.dt.float32
F32R = mybir.dt.float32r
I32 = mybir.dt.int32
ACT = mybir.ActivationFunctionType
ALU = mybir.AluOpType
AX_X = mybir.AxisListType.X

P = 128
T = 512
D = 1024
C = D // P
TT = T // P
MEM = 256
FF = 2816
FC = FF // P
HEADS = 4
EPS = 1e-6
EPS_SUBLN = 1e-5
LAM_INIT = 0.8 - 0.6 * math.exp(0.0)
MASKED = 1e33
SLOPES = [2.0 ** (-8.0 * n / 12) for n in range(1, 13)]
DIFF_SLOPES = SLOPES[2::3]
MOBA_SLOPES = [s for n, s in enumerate(SLOPES) if n % 3 != 2]
LEVELS = 9
W = 2048

GAIN_ROWS = [("ffn1_norm", 8), ("mix_norm", 8), ("xattn_norm", 8), ("mem_norm", 8), ("ffn2_norm", 8),
             ("final_norm", 8), ("norm_mix_pre_g_2", 8), ("norm_mix_post_g_2", 8), ("norm_ffn_pre_g_2", 8),
             ("hgrn_out_norm", 4), ("diff_subln_g_2", 1), ("lb_param", 8)]
GAIN_AT = {}
for _name, _rows in GAIN_ROWS:
    GAIN_AT[_name] = sum(r for n, r in GAIN_ROWS[:len(GAIN_AT)])
GAINS = sum(r for _, r in GAIN_ROWS)

GATE_UNITS, DOWN_UNITS = FC, FC // 2
FFN_UNITS = GATE_UNITS + DOWN_UNITS
MIX1_UNITS, SQUARE_UNITS, MIX2_UNITS, BRANCH_UNITS = 14, 4, 20, 4
ATT_ORDER = (("q", 0), ("v", 0), ("q", 1), ("v", 1), ("q", 2), ("q", 3), ("v", 2), ("v", 3))
ATT_UNITS = len(ATT_ORDER)
U_FFN1 = 0
U_MIX1 = U_FFN1 + FFN_UNITS
U_K = U_MIX1 + MIX1_UNITS
U_OUT1 = U_K + SQUARE_UNITS
U_ATT = U_OUT1 + SQUARE_UNITS
U_O = U_ATT + ATT_UNITS
U_FFN2 = U_O + SQUARE_UNITS
U_MIX2 = U_FFN2 + FFN_UNITS
U_BRANCH = U_MIX2 + MIX2_UNITS
U_OUT2 = U_BRANCH + BRANCH_UNITS
U_FFN3 = U_OUT2 + SQUARE_UNITS
UNITS = U_FFN3 + FFN_UNITS

ZQ, ZF, ZI, ZG, ZB, ZC, ZU = range(0, 3584, 512)
MIX1_COLS = [z + 256 * j for z in (ZQ, ZF, ZI, ZG, ZC, ZU, ZB) for j in range(2)]
MIX2_COLS = [256 * j for j in range(MIX2_UNITS)]

X_LOAD, X_FFN1, X_MIX1, X_ATT, X_FFN2, X_FINAL, X_MIX2 = range(7)
N_FFN1, N_MIX1, N_ATT, N_FFN2, N_MIX2, N_FFN3 = range(6)
S_FFN1, S_MIX1, S_ATT, S_FFN2, S_FINAL, S_POST2, S_FFN3 = range(7)
STREAMS = [2 if g == S_FINAL else 1 for g in range(7)]
SUMS_BEFORE = [sum(STREAMS[:g]) for g in range(7)]
R_FFN1, R_MIX1, R_ATT, R_FFN2, R_FINAL, R_MIX2, R_POST2, R_FFN3 = range(8)


def square_count(g, c, w=0):
    return C * (SUMS_BEFORE[g] + w) + c + 1


def add_count(g, c, w=0):
    return (C - 1) * (SUMS_BEFORE[g] + w) + c - (g > S_POST2)


TILE_AT = {3: 0, 2: 512, 0: 896, 1: 1024}
KEYS_AT = {0: 0, 1: 512, 3: 896, 2: 1024}
MAPS = 16


def two_blocks(nc, a, out):
    with ExitStack() as ctx:
        def sem(name):
            return ctx.enter_context(nc.semaphore(name))

        cursor = [-(-nc.sbuf_base // 32) * 32]

        def at(name, shape, dt, offset):
            return nc.alloc_sbuf_tensor_at(name, shape, dt, offset=offset)

        def sb(name, shape, dt):
            size = 4 * math.prod(shape[1:])
            t = at(name, shape, dt, cursor[0])
            cursor[0] += -(-size // 32) * 32
            return t

        raw = [sb(f"w_raw{s}", [P, W], F32) for s in range(2)]
        whi = [sb(f"w_hi{s}", [P, W], F32R) for s in range(2)]
        wlo = [sb(f"w_lo{s}", [P, W], F32R) for s in range(2)]
        x_at_offset = cursor[0]
        x = sb("x", [P, C, T], F32)
        n_at = cursor[0]
        nhi = sb("n_hi", [P, C, T], F32R)
        nlo = sb("n_lo", [P, C, T], F32R)
        ypost = at("y_post", [P, C, T], F32, n_at)
        sq = [sb(f"sq{s}", [P, T], F32) for s in range(2)]
        tmp = [sb(f"tmp{s}", [P, T], F32) for s in range(2)]
        sumsq = sb("sum_squares", [P, T], F32)
        rstd = sb("rstd", [P, T], F32)
        ident = sb("ident", [P, P], F32)
        ones = sb("ones", [P, P], F32)
        gains = sb("gains", [P, GAINS], F32)
        small = sb("small", [P, 80], F32)
        convw = sb("conv_taps", [P, HEADS, 3], F32)
        masks = sb("level_masks", [P, 6, 32], I32)
        maskt = sb("mask_tmp", [P, 3, 32], I32)
        arena = cursor[0]
        arena_size = nc.sbuf_usable_end - arena
        KB = 1024

        hhi = at("h_hi", [P, FC, T], F32R, arena)
        hlo = at("h_lo", [P, FC, T], F32R, arena + 44 * KB)
        x_tok = at("x_tok", [P, TT, D], F32, arena)
        gain_rows = at("gain_rows", [GAINS, P], F32, arena + 16 * KB)
        x_tok_a = at("x_tok_a", [P, 2, D], F32, arena + 88 * KB)
        x_tok_b = at("x_tok_b", [P, 2, D], F32, x_at_offset)
        out_tok = at("out_tok", [P, TT, D], F32, n_at)
        post_gain = at("post_gain", [P, D], F32, n_at + 16 * KB)
        hq = at("hgrn_q", [P, HEADS, T], F32, arena)
        hk = at("hgrn_k", [P, HEADS, T], F32, arena + 8 * KB)
        hf = at("hgrn_prefix", [P, HEADS, T], F32, arena + 16 * KB)
        hv = at("hgrn_v", [P, TT, T], F32, arena + 24 * KB)
        hg = at("hgrn_gate", [P, HEADS, T], F32, arena + 32 * KB)
        cv = at("conv_out", [P, HEADS, T], F32, arena + 40 * KB)
        cu = at("conv_in", [P, HEADS, T + 2], F32, arena + 48 * KB)
        mnhi = at("mem_hi", [P, C, MEM], F32R, arena + 57 * KB)
        mnlo = at("mem_lo", [P, C, MEM], F32R, arena + 65 * KB)
        hsuf = at("hgrn_suffix", [P, T], F32, arena + 73 * KB)
        qk = [at(f"hgrn_qk{s}", [P, T], F32, arena + (75 + 2 * s) * KB) for s in range(2)]
        pt = at("hgrn_scores", [P, TT * 640], F32, arena + 79 * KB)
        s32 = at("hgrn_diag", [P, TT, 32], F32, arena + 89 * KB)
        osb = at("hgrn_o", [P, T], F32, arena + 89 * KB + 512)
        osq = at("hgrn_o_sq", [P, T], F32, arena + 91 * KB + 512)
        orstd = at("hgrn_o_rstd", [P, T], F32, arena + 93 * KB + 512)
        mem_tok = at("mem_tok", [P, 2, D], F32, arena + 79 * KB)
        memt = at("mem_t", [P, C, MEM], F32, arena + 48 * KB)
        memsq = at("mem_sq", [P, C, MEM], F32, arena + 40 * KB)
        km = at("mem_k", [P, C, MEM], F32, arena + 16 * KB)
        vm = at("mem_v", [P, 2, D], F32, arena + 8 * KB)
        qx = at("att_q", [P, C, T], F32, arena + 24 * KB)
        px = at("att_p", [P, TT, MEM], F32, arena + 40 * KB)
        ptx = at("att_pt", [P, 2, T], F32, arena + 44 * KB)
        ga = at("gate_a", [P, C, T], F32, arena)
        mq = at("moba_q", [P, HEADS, T], F32, arena + 16 * KB)
        dq = at("diff_q", [P, HEADS, T], F32, arena + 24 * KB)
        dk = at("diff_k", [P, HEADS, T], F32, arena + 32 * KB)
        dv = at("diff_v", [P, TT, T], F32, arena + 40 * KB)
        mk = at("moba_k", [P, HEADS, T], F32, arena + 48 * KB)
        mv = at("moba_v", [P, TT, T], F32, arena + 56 * KB)
        gb = at("gate_b", [P, C, T], F32, arena + 48 * KB)
        mhi = at("merged_hi", [P, C, T], F32R, arena + 16 * KB)
        mlo = at("merged_lo", [P, C, T], F32R, arena + 32 * KB)
        pm = [at(f"map_p{s}", [P, 1280], F32, arena + (64 + 5 * s) * KB) for s in range(2)]
        ptm = at("map_pt", [P, 1280], F32, arena + 74 * KB)
        dist = at("distance", [P, T], F32, arena + 79 * KB)
        bias = [at(f"alibi{s}", [P, T], F32, arena + (81 + 2 * s) * KB) for s in range(2)]
        ysq = at("diff_y_sq", [P, T], F32, arena + 85 * KB)
        yrstd = at("diff_y_rstd", [P, T], F32, arena + 87 * KB)
        stat = at("map_stats", [P, 2, 4, 4], F32, arena + 89 * KB)
        lamv = at("lam_vectors", [P, 4, 64], F32, arena + 90 * KB)
        lams = at("lam_tmp", [P, 64], F32, arena + 91 * KB)
        assert arena_size >= 96 * KB

        def gain(name, c):
            return gains[:, GAIN_AT[name] + c:GAIN_AT[name] + c + 1]

        LB, OMLB, SUBG, NLAM, LSUM, LEXP = 0, 8, 12, 13, 16, 18
        LBE = 24
        GG, RTOK, SS, RT3, PG = 48, 56, 32, 44, 64

        bank = [ctx.enter_context(nc.psum_tensor(f"bank{b}", [P, 512], F32)) for b in range(8)]

        w_loaded = [sem("w_loaded0"), sem("w_loaded1")]
        w_hi_ready, w_lo_ready = sem("w_hi_ready"), sem("w_lo_ready")
        unit_done = sem("unit_done")
        x_loaded = [sem(f"x_loaded{i}") for i in range(TT)]
        first_loaded, first_hi, first_lo = sem("first_loaded"), sem("first_hi"), sem("first_lo")
        gain1_loaded, gains_loaded, taps_loaded = sem("gain1_loaded"), sem("gains_loaded"), sem("taps_loaded")
        gain1_t, gain1_ready = sem("gain1_t"), sem("gain1_ready")
        mem_loaded, lam_loaded, stored = sem("mem_loaded"), sem("lam_loaded"), sem("stored")
        ident_steps, dist_steps = sem("ident_steps"), sem("dist_steps")
        gains_t, gains_ready, small_steps, lb_exp = sem("gains_t"), sem("gains_ready"), sem("small_steps"), sem("lb_exp")
        mask_iota, mask_steps = sem("mask_iota"), sem("mask_steps")
        x_turned, x_ready = sem("x_turned"), sem("x_ready")
        sq_ready, sq_added, sq_summed = sem("sq_ready"), sem("sq_added"), sem("sq_summed")
        ln_done, rstd_ready, final_steps = sem("ln_done"), sem("rstd_ready"), sem("final_steps")
        rstd_turned, rtok_ready = sem("rstd_turned"), sem("rtok_ready")
        n_hi_ready, n_ready, n_used = sem("n_hi_ready"), sem("n_ready"), sem("n_used")
        scaled, scaled_pool = sem("scaled"), sem("scaled_pool")
        ffn = [{k: sem(f"{k}_{f}") for k in ("gu_scaled", "silu_ready", "h_product", "h_hi_ready", "h_ready", "down_done")}
               for f in range(3)]
        m1_act, m1_dve, m1_fn = sem("m1_act"), sem("m1_dve"), sem("m1_fn")
        q_scaled, f_steps, logf_ready = sem("q_scaled"), sem("f_steps"), sem("logf_ready")
        conv_pad, conv_steps = sem("conv_pad"), sem("conv_steps")
        mem_turned, memt_ready, memsq_ready, mem_summed = sem("mem_turned"), sem("memt_ready"), sem("memsq_ready"), sem("mem_summed")
        mem_rstd, mem_scaled, mem_hi_ready, mem_ready = sem("mem_rstd"), sem("mem_scaled"), sem("mem_hi_ready"), sem("mem_ready")
        sums_ready, decay_ready, qk_ready, qk_used = sem("sums_ready"), sem("decay_ready"), sem("qk_ready"), sem("qk_used")
        diag_done = sem("diag_done")
        s32_steps, scores_dve, scores_act = sem("s32_steps"), sem("scores_dve"), sem("scores_act")
        o_done, o_copied, o_summed, o_rstd, y_steps = sem("o_done"), sem("o_copied"), sem("o_summed"), sem("o_rstd"), sem("y_steps")
        y1_hi, y1_ready, pt_zero = sem("y1_hi"), sem("y1_ready"), sem("pt_zero")
        qx_ready, sx_done, mx_ready, px_ready, px_norm = sem("qx_ready"), sem("sx_done"), sem("mx_ready"), sem("px_ready"), sem("px_norm")
        px_inv = sem("px_inv")
        tx_done, ptx_ready, ax_done, ax_read, ax_hi, ax_ready = sem("tx_done"), sem("ptx_ready"), sem("ax_done"), sem("ax_read"), sem("ax_hi"), sem("ax_ready")
        vm_ready = sem("vm_ready")
        m2_act, m2_dve, m2_tanh = sem("m2_act"), sem("m2_dve"), sem("m2_tanh")
        lam_steps, lam_exp, bias_ready = sem("lam_steps"), sem("lam_exp"), sem("bias_ready")
        map_scores, map_max, map_neg, map_exp = sem("map_scores"), sem("map_max"), sem("map_neg"), sem("map_exp")
        map_inv, map_norm, map_turned, map_pt = sem("map_inv"), sem("map_norm"), sem("map_turned"), sem("map_pt")
        av_done, yb_sq, yb_summed, yb_rstd, y2_steps = sem("av_done"), sem("yb_sq"), sem("yb_summed"), sem("yb_rstd"), sem("y2_steps")
        ya_copied, yb_copied, y2_hi, y2_ready = sem("ya_copied"), sem("yb_copied"), sem("y2_hi"), sem("y2_ready")
        br_done, br_a, br_b, br_sum, br_hi, br_ready = sem("br_done"), sem("br_a"), sem("br_b"), sem("br_sum"), sem("br_hi"), sem("br_ready")
        ypost_ready, out_ready = sem("ypost_ready"), sem("out_ready")
        xt_turned, xt_ready, post_loaded = sem("xt_turned"), sem("xt_ready"), sem("post_loaded")
        y3_sq, y3_sum, y3_root, y3_scaled = sem("y3_sq"), sem("y3_sum"), sem("y3_root"), sem("y3_scaled")

        block = ctx.enter_context(nc.Block())

        def k_major(w):
            return w.rearrange("(k p) n -> p k n", p=P)

        def pairs(t, L, which):
            return t.rearrange("p (n two l) -> p n two l", two=2, l=L)[:, :, which, :]

        def m1_emptied(v):
            if v < 4:
                return m1_dve, 2 * v + 2
            if v < 6:
                return m1_act, 4 * (v - 3)
            if v < MIX1_UNITS:
                return m1_dve, 8 + 2 * (v - 5)
            return m1_act, 8 + 2 * (v - MIX1_UNITS + 1)

        def m2_emptied(v):
            if v in (4, 5, 10, 11):
                return m2_act, 4 * (v - 3 if v < 6 else v - 7)
            return m2_dve, 2 * (v + 1 - 2 * (v > 5) - 2 * (v > 11))

        def y1_order(v):
            order = {14: (4, 5, 6, 7, 0), 15: (1, 2), 16: (3,)}.get(v, ())
            first = {14: 0, 15: 5, 16: 7}.get(v, 0)
            return [(first + n, c) for n, c in enumerate(order)]

        @block.sync
        def _(sp):
            def slot_free(par, half):
                sp.wait_ge(w_lo_ready, 2 * half + par - 1)

            def load(par, pieces, first_signal=None):
                for (lo, hi, form), src in pieces:
                    dst = raw[par][:, lo:hi].rearrange("p (k n) -> p k n", k=form)
                    sp.dma_start(dst, src).then_inc(first_signal or w_loaded[par], 16)
                    first_signal = None

            def load_square(u, w, k0, c0):
                if u >= 2:
                    slot_free(u % 2, u // 2)
                v = k_major(w)[:, k0:k0 + C, c0:c0 + 256]
                load(u % 2, [((0, W // 2, 4), v[:, 0:4]), ((W // 2, W, 4), v[:, 4:8])])

            def load_ffn(base, gate, up, down):
                g, p_, d = k_major(gate), k_major(up), k_major(down)

                def gate_up(par, half, n, free):
                    if free:
                        slot_free(par, half)
                    cols = bass.ds(n * P, P)
                    load(par, [((0, W // 2, C), g[:, :, cols]), ((W // 2, W, C), p_[:, :, cols])],
                         first_loaded if base == 0 and isinstance(n, int) and n == 0 else None)

                def down_pair(par, half, n):
                    slot_free(par, half)
                    load(par, [((0, W // 2, 1), d[:, bass.ds(2 * n, 1), :]),
                               ((W // 2, W, 1), d[:, bass.ds(2 * n + 1, 1), :])])

                for j in range(2):
                    gate_up((base + j) % 2, (base + j) // 2, j, base > 0)
                with sp.Fori(1, GATE_UNITS // 2) as i:
                    for j in range(2):
                        gate_up((base + j) % 2, i + (base + j) // 2, 2 * i + j, True)
                b = base + GATE_UNITS
                with sp.Fori(0, DOWN_UNITS // 2) as i:
                    for j in range(2):
                        down_pair((b + j) % 2, i + (b + j) // 2, 2 * i + j)
                u = b + DOWN_UNITS - 1
                down_pair(u % 2, u // 2, DOWN_UNITS - 1)

            xv = a["x"].rearrange("b (i p) d -> p (b i) d", p=P)
            for i in range(TT):
                sp.dma_start(x_tok[:, i, :], xv[:, i, :]).then_inc(x_loaded[i], 16)
            load_ffn(U_FFN1, a["ffn1_gate"][0], a["ffn1_up"][0], a["ffn1_down"][0])
            for j, c0 in enumerate(MIX1_COLS):
                load_square(U_MIX1 + j, a["w_in"][0], 0, c0)
                if j == 0:
                    sp.wait_ge(unit_done, U_MIX1)
                    sp.dma_start(mem_tok[:, :, :], a["mem"].rearrange("b (i p) d -> p (b i) d", p=P)).then_inc(mem_loaded, 16)
            for j in range(SQUARE_UNITS):
                load_square(U_K + j, a["w_kv_mem"][0], 0, 256 * j)
            for j in range(SQUARE_UNITS):
                load_square(U_OUT1 + j, a["w_out"][0], 0, 256 * j)
            for p, (what, h) in enumerate(ATT_ORDER):
                if what == "q":
                    load_square(U_ATT + p, a["w_q_mem"][0], 0, 256 * h)
                else:
                    load_square(U_ATT + p, a["w_kv_mem"][0], 0, D + 256 * h)
            for j in range(SQUARE_UNITS):
                load_square(U_O + j, a["w_o_mem"][0], 0, 256 * j)
            load_ffn(U_FFN2, a["ffn2_gate"][0], a["ffn2_up"][0], a["ffn2_down"][0])
            for j, c0 in enumerate(MIX2_COLS):
                load_square(U_MIX2 + j, a["w_in_2"][0], 0, c0)
                if j == 0:
                    sp.wait_ge(unit_done, U_MIX2)
                    for n, name in enumerate(("lam_q1_2", "lam_k1_2", "lam_q2_2", "lam_k2_2")):
                        sp.dma_start(lamv[:, n, :], a[name].to_broadcast([P, 64])).then_inc(lam_loaded, 16)
            for j in range(BRANCH_UNITS):
                u = U_BRANCH + j
                slot_free(u % 2, u // 2)
                v = k_major(a["w_branch_b_2" if j >= 2 else "w_branch_a_2"][0])[:, :, 512 * (j % 2):512 * (j % 2) + 512]
                load(u % 2, [((0, W // 2, 2), v[:, 0:2]), ((W // 2, W, 2), v[:, 2:4])])
            for j in range(SQUARE_UNITS):
                load_square(U_OUT2 + j, a["w_out_2"][0], 0, 256 * j)
            load_ffn(U_FFN3, a["w_gate_2"][0], a["w_up_2"][0], a["w_down_2"][0])
            ov = out.rearrange("b (i p) d -> p (b i) d", p=P)
            sp.wait_ge(unit_done, U_FFN3 + GATE_UNITS)
            sp.dma_start(post_gain[:, :], a["norm_ffn_post_g_2"].to_broadcast([P, D])).then_inc(post_loaded, 16)
            for n in range(2 * TT):
                i, cols = n // 2, slice(T * (n % 2), T * (n % 2) + T)
                sp.wait_ge(out_ready, n + 1)
                sp.dma_start(ov[:, i, cols], out_tok[:, i, cols]).then_inc(stored, 16)
            sp.wait_ge(stored, 16 * 2 * TT)

        @block.gpsimd
        def _(pool):
            pool.memset(ones[:, :], 1.0).then_inc(ident_steps, 1)
            pool.wait_ge(ident_steps, 1)
            pool.affine_select(ident[:, :], ones[:, :], [[-1, P]], ALU.is_equal, 0.0, base=0,
                               channel_multiplier=1).then_inc(ident_steps, 1)
            pool.iota(maskt[:, 0, :], [[0, 32]], base=0, channel_multiplier=1).then_inc(mask_iota, 1)
            pool.iota(maskt[:, 1, :], [[1, 32]], base=0, channel_multiplier=0).then_inc(mask_iota, 1)

            def add_squares(g, chunks=range(1, C)):
                for w in range(STREAMS[g]):
                    for c in chunks:
                        n = add_count(g, c, w)
                        acc = (sumsq, rstd)[w]
                        pool.wait_ge(sq_ready, square_count(g, c, w))
                        if n > 1:
                            pool.wait_ge(sq_added, n - 1)
                        pool.tensor_tensor(acc[:, :], acc[:, :], sq[n % 2][:, :], ALU.add).then_inc(sq_added, 1)

            def hgrn_sums(h):
                pre, suf = hf[:, h, :], hsuf[:, :]
                if h:
                    pool.wait_ge(decay_ready, 2 * LEVELS * h)
                pool.memset(suf, 0.0).then_inc(sums_ready, 1)
                pool.wait_ge(logf_ready, h + 1)
                for l in range(LEVELS - 1):
                    L = 1 << l
                    n = T // (2 * L)
                    whole_odd = pairs(pre, L, 1)[:, :, L - 1:L].to_broadcast([P, n, L])
                    whole_even = pairs(pre, L, 0)[:, :, L - 1:L].to_broadcast([P, n, L])
                    pool.wait_ge(decay_ready, 2 * (LEVELS * h + l) + 2)
                    pool.wait_ge(sums_ready, 17 * h + 1 + 2 * l)
                    pool.tensor_tensor(pairs(suf, L, 0), pairs(suf, L, 0), whole_odd, ALU.add).then_inc(sums_ready, 1)
                    pool.wait_ge(sums_ready, 17 * h + 2 + 2 * l)
                    pool.tensor_tensor(pairs(pre, L, 1), pairs(pre, L, 1), whole_even, ALU.add).then_inc(sums_ready, 1)

            add_squares(S_FFN1)
            add_squares(S_MIX1)
            for h in range(HEADS):
                hgrn_sums(h)
            for g in (S_ATT, S_FFN2, S_FINAL):
                add_squares(g)
            pool.wait_ge(unit_done, U_MIX2)
            pool.iota(dist[:, :], [[-1, T]], base=T - P, channel_multiplier=1,
                      allow_small_or_imprecise_dtypes=True).then_inc(dist_steps, 1)
            pool.wait_ge(dist_steps, 1)
            pool.affine_select(dist[:, :], dist[:, :], [[-1, T]], ALU.is_ge, MASKED, base=T - P,
                               channel_multiplier=1).then_inc(dist_steps, 1)
            pool.wait_ge(dist_steps, 2)
            for m in range(MAPS):
                if m >= 2:
                    pool.wait_ge(map_max, 4 * (m - 1))
                slope = MOBA_SLOPES[m] if m < 8 else DIFF_SLOPES[(m - 8) // 2]
                pool.tensor_scalar(bias[m % 2][:, :], dist[:, :], -slope, None, ALU.mult).then_inc(bias_ready, 1)
            pool.wait_ge(rstd_ready, R_POST2 + 1)
            for c in range(1, C, 2):
                if c > 1:
                    pool.wait_ge(x_ready, C * X_MIX2 + c - 1)
                pool.tensor_tensor(tmp[1][:, :], ypost[:, c, :], rstd[:, :], ALU.mult).then_inc(scaled_pool, 1)
                if c > 3:
                    add_squares(S_FFN3, range(c // 2 - 1, c // 2))
            add_squares(S_FFN3, range(3, C))

        @block.tensor
        def _(pe):
            def products(acc, w_hi, w_lo, x_hi, x_lo, start, stop):
                pe.matmul(acc, w_hi, x_hi, start=start, stop=False)
                pe.matmul(acc, w_hi, x_lo, start=False, stop=False)
                return pe.matmul(acc, w_lo, x_hi, start=False, stop=stop)

            def unit_split(u):
                pe.wait_ge(w_lo_ready, u + 1)

            def dense_released(u, pair, xh, xl):
                unit_split(u)
                s = u % 2
                for m in range(2):
                    for k in range(C):
                        w0 = k * 256 + m * P
                        mm = products(bank[pair + m][:, :], whi[s][:, w0:w0 + P], wlo[s][:, w0:w0 + P],
                                      xh[:, k, :], xl[:, k, :], k == 0, k == C - 1)
                        if k == C - 1 or m:
                            mm.then_inc(unit_done if m and k == C - 1 else n_used, 1)

            def dense(u, pair, xh, xl, wait_x=None, width=T, hooks=None, order=range(C), released=0):
                unit_split(u)
                s = u % 2
                for n, k in enumerate(order):
                    if wait_x is not None:
                        wait_x(k)
                    for m in range(2):
                        w0 = k * 256 + m * P
                        mm = products(bank[pair + m][:, 0:width], whi[s][:, w0:w0 + P], wlo[s][:, w0:w0 + P],
                                      xh[:, k, :], xl[:, k, :], n == 0, n == C - 1)
                    if n == C - 1:
                        mm.then_inc(unit_done, 1)
                    elif n < released:
                        mm.then_inc(n_used, 1)
                    if hooks and n in hooks:
                        hooks[n]()

            def dense_tokens(u, pair, xh, xl, tiles, hooks=None):
                unit_split(u)
                s = u % 2
                per = tiles // 2
                for i in range(tiles):
                    acc = bank[pair + i // per][:, (i % per) * 256:(i % per) * 256 + 256]
                    for k in range(C):
                        t0 = slice(i * P, i * P + P)
                        w0 = slice(k * 256, k * 256 + 256)
                        pe.matmul(acc, xh[:, k, t0], whi[s][:, w0], start=(k == 0), stop=False)
                        pe.matmul(acc, xl[:, k, t0], whi[s][:, w0], start=False, stop=False)
                        mm = pe.matmul(acc, xh[:, k, t0], wlo[s][:, w0], start=False, stop=(k == C - 1))
                        if i == tiles - 1 and k == C - 1:
                            mm.then_inc(unit_done, 1)
                        if hooks and k % 2 and (2 * i + k // 4) in hooks and k % 4 == 3:
                            hooks[2 * i + k // 4]()

            def sum_over_partitions(g, b=7, w=0):
                pe.wait_ge(sq_added, add_count(g, C - 1, w))
                pe.matmul(bank[b][:, :], ones[:, :], (sumsq, rstd)[w][:, :], start=True, stop=True).then_inc(sq_summed, 1)

            def turn_rstd(b):
                for i in range(TT):
                    mm = pe.matmul(bank[b][:, i:i + 1], rstd[:, i * P:(i + 1) * P], ident[:, 0:1], start=True, stop=True)
                mm.then_inc(rstd_turned, 1)

            def turn_x(i, b):
                for half in range(2):
                    for c in range(4):
                        mm = pe.transpose(bank[b + half][:, c * P:(c + 1) * P],
                                          x[:, 4 * half + c, i * P:(i + 1) * P], ident[:, :])
                mm.then_inc(xt_turned, 1)

            def after_norm(index):
                return lambda k: pe.wait_ge(n_ready, C * index + k + 1)

            def ffn_products(f, base, index, sums, tokens=False):
                s_ = ffn[f]

                def gate_up(u, j, par, jj, first, hooks=None):
                    pe.wait_ge(w_lo_ready, u + 1)
                    if not first:
                        pe.wait_ge(s_["gu_scaled"], 2 * (j - 1))
                    for k in range(C):
                        if first and jj == 0:
                            pe.wait_ge(n_ready, C * index + k + 1)
                        for g in range(2):
                            w0 = (g * C + k) * P
                            mm = products(bank[2 * jj + g][:, :], whi[par][:, w0:w0 + P], wlo[par][:, w0:w0 + P],
                                          nhi[:, k, :], nlo[:, k, :], k == 0, k == C - 1)
                        if k == C - 1:
                            mm.then_inc(unit_done, 1)
                        if hooks and k in hooks:
                            hooks[k]()

                def turn_middle():
                    pe.wait_ge(rstd_ready, R_FFN3 + 1)
                    turn_x(1, 6)

                def turn_rest():
                    for i in (2, 3):
                        pe.wait_ge(xt_ready, 2 * (i - 1))
                        turn_x(i, 4 + 2 * (i % 2))

                if f == 0:
                    for g in range(2):
                        if g == 0:
                            pe.wait_ge(first_lo, 1)
                        else:
                            pe.wait_ge(w_lo_ready, 1)
                        pe.wait_ge(x_ready, g + 1)
                        for k in range(C):
                            if g == 0:
                                pe.wait_ge(n_ready, k + 1)
                            w0 = (g * C + k) * P
                            mm = products(bank[g][:, :], whi[0][:, w0:w0 + P], wlo[0][:, w0:w0 + P],
                                          nhi[:, k, :], nlo[:, k, :], k == 0, k == C - 1)
                    mm.then_inc(unit_done, 1)
                    pe.wait_ge(gains_loaded, 16 * (len(GAIN_ROWS) - 1))
                    pe.wait_ge(x_ready, C)
                    pe.transpose(bank[6][:, 0:GAINS], gain_rows[:, :], ident[0:GAINS, 0:GAINS]).then_inc(gains_t, 1)
                else:
                    gate_up(base, 0, base % 2, 0, True)
                if tokens:
                    turn_x(0, 4)
                gate_up(base + 1, 1, (base + 1) % 2, 1, True,
                        {2: lambda: sum_over_partitions(sums), 5: turn_middle, 7: turn_rest} if tokens
                        else {1: lambda: sum_over_partitions(sums)})
                with pe.Fori(1, GATE_UNITS // 2) as i:
                    for j in range(2):
                        gate_up(2 * i + (base + j), 2 * i + j, (base + j) % 2, j, False)

                def chunk(n):
                    if isinstance(n, int):
                        return hhi[:, n, :], hlo[:, n, :]
                    return (hhi[:, bass.ds(n, 1), :].rearrange("p o t -> p (o t)"),
                            hlo[:, bass.ds(n, 1), :].rearrange("p o t -> p (o t)"))

                def down(u, n, par, first=False, last=False):
                    pe.wait_ge(w_lo_ready, u + 1)
                    pe.wait_ge(s_["h_ready"], 2 * n + 2)
                    for d in ([4, 5, 6, 7, 0, 1, 2, 3] if first else range(C)):
                        if first and d == 0:
                            pe.wait_ge(s_["gu_scaled"], 2 * FC)
                        for kk in range(2):
                            w0 = kk * D + d * P
                            xh, xl = chunk(2 * n + kk)
                            mm = products(bank[d][:, :], whi[par][:, w0:w0 + P], wlo[par][:, w0:w0 + P],
                                          xh, xl, first and kk == 0, last and kk == 1)
                        if last and d < C - 1:
                            mm.then_inc(s_["down_done"], 1)
                    mm.then_inc(unit_done, 1)

                def down_tokens(u, n, par, first=False, last=False):
                    pe.wait_ge(w_lo_ready, u + 1)
                    pe.wait_ge(s_["h_ready"], 2 * n + 2)
                    if first:
                        pe.wait_ge(xt_ready, 2 * TT)
                    for i in ((2, 3, 0, 1) if first else range(TT)):
                        if first and i == 0:
                            pe.wait_ge(s_["gu_scaled"], 2 * FC)
                        for kk in range(2):
                            xh, xl = [v[:, i * P:(i + 1) * P] for v in chunk(2 * n + kk)]
                            for x_part, w_part, begin, end in ((xh, whi, True, False), (xh, wlo, False, False),
                                                               (xl, whi, False, True)):
                                for half in range(2):
                                    w0 = kk * D + T * half
                                    mm = pe.matmul(bank[2 * i + half][:, :], x_part, w_part[par][:, w0:w0 + T],
                                                   start=first and kk == 0 and begin, stop=last and kk == 1 and end)
                        if last and i < TT - 1:
                            mm.then_inc(s_["down_done"], 1)
                    mm.then_inc(unit_done, 1)

                down = down_tokens if tokens else down
                b = base + GATE_UNITS
                down(b, 0, b % 2, first=True)
                if tokens:
                    for n in range(1, DOWN_UNITS - 2):
                        down(b + n, n, (b + n) % 2)
                else:
                    with pe.Fori(0, (DOWN_UNITS - 3) // 2) as i:
                        for j in range(2):
                            down(2 * i + (b + 1 + j), 2 * i + (1 + j), (b + 1 + j) % 2)
                for n in (DOWN_UNITS - 2, DOWN_UNITS - 1):
                    down(b + n, n, (b + n) % 2, last=(n == DOWN_UNITS - 1))

            pe.wait_ge(ident_steps, 2)
            pe.wait_ge(gain1_loaded, 16)
            pe.transpose(bank[7][:, 0:C], gain_rows[0:C, :], ident[0:C, 0:C]).then_inc(gain1_t, 1)
            for i in range(TT):
                pe.wait_ge(x_loaded[i], 16)
                for c in range(C):
                    if i == 0 and c == C - 1:
                        pe.wait_ge(gain1_ready, 1)
                    mm = pe.transpose(bank[c][:, i * P:(i + 1) * P], x_tok[:, i, c * P:(c + 1) * P], ident[:, :])
                    if i == TT - 1:
                        mm.then_inc(x_turned, 1)
            ffn_products(0, U_FFN1, N_FFN1, S_FFN1)

            def hgrn_level(h, l):
                g = LEVELS * h + l
                pe.wait_ge(qk_ready, 2 * g + 2)
                L, z = 1 << l, qk[g % 2]
                if h and l == 5:
                    pe.wait_ge(o_copied, 2 * h)
                if h and l == 6:
                    pe.wait_ge(o_rstd, 2 * h - 1)
                if L < 32:
                    b, slot = (bank[4], l + 1) if l < 3 else (bank[5], l - 3)
                    for j in range(TT):
                        for m in range(4):
                            t0 = slice(P * j + 32 * m, P * j + 32 * m + 32)
                            mm = pe.matmul(b[32 * m:32 * m + 32, slot * P + 32 * j:slot * P + 32 * j + 32],
                                           z[:, t0], z[:, t0], start=True, stop=True)
                elif L == 32:
                    for j in range(TT):
                        for m in range(2):
                            s0 = P * j + 64 * m
                            mm = pe.matmul(bank[5][64 * m:64 * m + 32, 256 + 32 * j:288 + 32 * j],
                                           z[:, s0:s0 + 32], z[:, s0 + 32:s0 + 64], start=True, stop=True)
                elif L == 64:
                    for j in range(TT):
                        mm = pe.matmul(bank[6][0:64, 64 * j:64 * j + 64], z[:, P * j:P * j + 64],
                                       z[:, P * j + 64:P * j + P], start=True, stop=True)
                elif L == 128:
                    for j in range(2):
                        mm = pe.matmul(bank[6][:, 256 + P * j:256 + P * j + P], z[:, 256 * j:256 * j + P],
                                       z[:, 256 * j + P:256 * j + 256], start=True, stop=True)
                else:
                    for j in range(2):
                        mm = pe.matmul(bank[7][:, 256 * j:256 * j + 256], z[:, P * j:P * j + P],
                                       z[:, 256:512], start=True, stop=True)
                mm.then_inc(qk_used, 1)

            def hgrn_first(h):
                if h:
                    pe.wait_ge(scores_dve, 6 * h)
                else:
                    pe.wait_ge(mem_rstd, 2)
                pe.wait_ge(q_scaled, h + 1)
                pe.wait_ge(f_steps, 2 * h + 2)
                for j in range(TT):
                    for m in range(4):
                        t0 = slice(P * j + 32 * m, P * j + 32 * m + 32)
                        mm = pe.matmul(bank[4][32 * m:32 * m + 32, 32 * j:32 * j + 32], hk[:, h, t0], hq[:, h, t0],
                                       start=True, stop=True)
                mm.then_inc(diag_done, 1)
                hgrn_level(h, 0)

            def hgrn_out(h):
                pe.wait_ge(scores_dve, 6 * h + 6)
                pe.wait_ge(scores_act, 3 * h + 3)
                pe.wait_ge(m1_act, 8)
                for j in range(TT):
                    mm = pe.matmul(bank[7][:, P * j:T], hv[:, j, h * P:(h + 1) * P],
                                   pt[:, T * j + P * j:T * j + T], start=(j == 0), stop=(j == TT - 1))
                mm.then_inc(o_done, 1)

            def hgrn_sum(h):
                pe.wait_ge(o_copied, 2 * h + 2)
                pe.matmul(bank[6][:, :], ones[:, :], osq[:, :], start=True, stop=True).then_inc(o_summed, 1)

            def hgrn_hooks(v):
                def then(what, *args):
                    return lambda: what(*args)

                hooks = {}
                for h in range(HEADS):
                    if v == 5 + 2 * h:
                        hooks[5] = then(hgrn_first, h)
                        hooks[6] = then(hgrn_level, h, 1)
                        hooks[7] = then(hgrn_level, h, 2)
                    if v == 6 + 2 * h:
                        for l, part in ((3, 0), (4, 1), (5, 6), (6, 7)):
                            hooks[part] = then(hgrn_level, h, l)
                    if v == 7 + 2 * h:
                        hooks[0] = then(hgrn_level, h, 7)
                        hooks[1] = then(hgrn_level, h, 8)
                    if v == 8 + 2 * h:
                        hooks[3] = then(hgrn_sum, h)
                for h in range(HEADS):
                    if v == 7 + 2 * h:
                        before = hooks.get(7)
                        hooks[7] = (lambda h, before: lambda: (before() if before else None, hgrn_out(h)))(h, before)
                return hooks

            for v in range(MIX1_UNITS + SQUARE_UNITS):
                u, pair = U_MIX1 + v, 2 * (v % 2)
                if v >= 2:
                    pe.wait_ge(*m1_emptied(v - 2))
                hooks = hgrn_hooks(v)
                if v in (4, 5):
                    dense_tokens(u, pair, nhi, nlo, TT, hooks)
                elif v < MIX1_UNITS:
                    dense(u, pair, nhi, nlo, after_norm(N_MIX1) if v == 0 else None, hooks=hooks)
                else:
                    if v == MIX1_UNITS:
                        pe.wait_ge(mem_ready, 1)
                    dense(u, pair, mnhi, mnlo, width=MEM, hooks=hooks)
                if v == 0:
                    sum_over_partitions(S_MIX1)
                if v == 2:
                    pe.wait_ge(memt_ready, 4)
                    turn_rstd(7)
                if v == 1:
                    pe.wait_ge(mem_loaded, 16)
                    pe.wait_ge(rstd_ready, R_MIX1 + 1)
                    for c in range(C):
                        for i in range(2):
                            col = (c % 2) * MEM + i * P
                            mm = pe.transpose(bank[4 + c // 2][:, col:col + P], mem_tok[:, i, c * P:(c + 1) * P], ident[:, :])
                        if c % 2:
                            mm.then_inc(mem_turned, 1)
                if v == 3:
                    pe.wait_ge(memsq_ready, 1)
                    for c in range(C):
                        mm = pe.matmul(bank[4][:, 0:MEM], ones[:, :], memsq[:, c, :], start=(c == 0), stop=(c == C - 1))
                    mm.then_inc(mem_summed, 1)
            for j in range(SQUARE_UNITS):
                if j < 2:
                    pe.wait_ge(*m1_emptied(MIX1_UNITS + SQUARE_UNITS - 2 + j))
                else:
                    pe.wait_ge(x_ready, C * X_MIX1 + 2 * (j - 1))
                if j == 0:
                    split_order = [c for v in range(MIX1_UNITS, MIX1_UNITS + SQUARE_UNITS) for _, c in y1_order(v)]
                    dense(U_OUT1, 0, nhi, nlo, lambda k: pe.wait_ge(y1_ready, split_order.index(k) + 1), order=split_order)
                elif j < SQUARE_UNITS - 1:
                    dense(U_OUT1 + j, 2 * (j % 2), nhi, nlo)
                else:
                    dense_released(U_OUT1 + j, 2 * (j % 2), nhi, nlo)

            def att_scores(h):
                pe.wait_ge(qx_ready, 2 * h + 2)
                if h:
                    pe.wait_ge(px_ready, TT * h)
                for i in range(TT):
                    for c in range(2):
                        mm = pe.matmul(bank[4 + i // 2][:, (i % 2) * MEM:(i % 2) * MEM + MEM],
                                       qx[:, 2 * h + c, i * P:(i + 1) * P], km[:, 2 * h + c, :], start=(c == 0), stop=(c == 1))
                    if i % 2:
                        mm.then_inc(sx_done, 1)

            def att_turn(h):
                if h == 3:
                    pe.wait_ge(ax_ready, 6)
                elif h:
                    pe.wait_ge(ax_read, 2 * h)
                for i in range(TT):
                    pe.wait_ge(px_norm, TT * h + i + 1)
                    for m in range(2):
                        mm = pe.transpose(bank[6 + m][:, i * P:(i + 1) * P], px[:, i, m * P:(m + 1) * P], ident[:, :])
                mm.then_inc(tx_done, 1)

            def att_out(h):
                pe.wait_ge(ptx_ready, 2 * h + 2)
                pe.wait_ge(vm_ready, 2 * h + 2)
                for c in range(2):
                    for m in range(2):
                        mm = pe.matmul(bank[6 + c][:, :], vm[:, m, h * 256 + c * P:h * 256 + c * P + P], ptx[:, m, :],
                                       start=(m == 0), stop=(m == 1))
                    mm.then_inc(ax_done, 1)

            scores, turn, output = att_scores, att_turn, att_out
            att_hooks = [{}, {}, {1: (scores, 0)}, {1: (turn, 0)}, {2: (output, 0), 3: (scores, 1)},
                         {1: (turn, 1), 3: (output, 1), 4: (scores, 2)}, {1: (turn, 2), 3: (scores, 3)},
                         {2: (output, 2)}, {1: (turn, 3), 3: (output, 3)}]

            def call(hooks):
                return {k: (lambda f, h: lambda: f(h))(*what) for k, what in hooks.items()}

            for p, (what, h) in enumerate(ATT_ORDER):
                if p >= 2:
                    last, lh = ATT_ORDER[p - 2]
                    pe.wait_ge(*((qx_ready, 2 * lh + 2) if last == "q" else (vm_ready, 2 * lh + 2)))
                if what == "q":
                    dense(U_ATT + p, 2 * (p % 2), nhi, nlo, after_norm(N_ATT) if p == 0 else None, hooks=call(att_hooks[p]))
                else:
                    dense_tokens(U_ATT + p, 2 * (p % 2), mnhi, mnlo, 2, call(att_hooks[p]))
                if p == 0:
                    sum_over_partitions(S_ATT)
            for j in range(SQUARE_UNITS):
                if j < 2:
                    pe.wait_ge(vm_ready, 6 + 2 * j)
                else:
                    pe.wait_ge(x_ready, C * X_ATT + 2 * (j - 1))
                if j < SQUARE_UNITS - 1:
                    dense(U_O + j, 2 * (j % 2), nhi, nlo, (lambda k: pe.wait_ge(ax_ready, k + 1)) if j == 0 else None,
                          hooks=call(att_hooks[ATT_UNITS]) if j == 0 else None)
                else:
                    dense_released(U_O + j, 2 * (j % 2), nhi, nlo)
            ffn_products(1, U_FFN2, N_FFN2, S_FFN2)

            def map_qk(m, part):
                q_, k_ = (mq, mk) if m < 8 else (dq, dk)
                c, rows = (m % 8) // 2, slice(64 * (m % 2), 64 * (m % 2) + 64)
                if part == 0:
                    pe.wait_ge(*m2_emptied((2 if m < 8 else 8) + c // 2))
                    pe.wait_ge(rtok_ready, 2)
                    if m:
                        pe.wait_ge(map_max, 4 * m)
                if part == 2 and m >= 2:
                    if m <= 10:
                        pe.wait_ge(ya_copied, min(m - 1, 8))
                    else:
                        pe.wait_ge(yb_sq, (m - 11) // 2 + 1)
                for i in ((3,), (2, 0), (1,))[part]:
                    b = bank[4 + part]
                    col = 384 if i == 0 else 0
                    pe.matmul(b[:, col:col + P * (i + 1)], q_[rows, c, i * P:(i + 1) * P], k_[rows, c, 0:P * (i + 1)],
                              start=True, stop=True).then_inc(map_scores, 1)

            def map_turn(m, r):
                n = m if m < 8 else 8 + (m - 8) // 2
                if r == 0:
                    pe.wait_ge(map_norm, 4 * m + 4)
                if n or r:
                    pe.wait_ge(map_pt, 3 * n + r)
                if m > 8 and r == 0 and m >= 11:
                    pe.wait_ge(yb_rstd, 2 * ((m - 9) // 2) - 1)
                for j in ((0,), (1, 3), (2,))[r]:
                    col0 = 384 if j == 3 else 0
                    for i in range(j, TT):
                        mm = pe.transpose(bank[7][:, col0 + (i - j) * P:col0 + (i - j + 1) * P],
                                          pm[m % 2][:, TILE_AT[i] + j * P:TILE_AT[i] + (j + 1) * P], ident[:, :])
                mm.then_inc(map_turned, 1)

            def map_out(m):
                n = m if m < 8 else 8 + (m - 8) // 2
                pe.wait_ge(map_pt, 3 * n + 3)
                pe.wait_ge(map_max, 4 * min(m + 2, MAPS))
                pe.wait_ge(*m2_emptied((4 if m < 4 else 5) if m < 8 else (10 if m < 12 else 11)))
                for j in range(TT):
                    if m < 8:
                        lhs, rows = mv[:, j, 64 * m:64 * m + 64], slice(64 * (m % 2), 64 * (m % 2) + 64)
                    else:
                        h = (m - 8) // 2
                        lhs, rows = dv[:, j, P * h:P * h + P], slice(0, P)
                    mm = pe.matmul(bank[6][rows, P * j:T], lhs, ptm[:, KEYS_AT[j]:KEYS_AT[j] + T - P * j],
                                   start=(j == 0), stop=(j == TT - 1))
                mm.then_inc(av_done, 1)

            def map_sum(h):
                pe.wait_ge(yb_sq, h + 1)
                n = 8 + h
                pe.wait_ge(map_pt, 3 * n + 3)
                pe.matmul(bank[7][:, :], ones[:, :], ysq[:, :], start=True, stop=True).then_inc(yb_summed, 1)

            def has_out(m):
                return 0 <= m < 8 or (8 <= m < MAPS and m % 2 == 1)

            def sum_both():
                sum_over_partitions(S_FINAL, 6)
                sum_over_partitions(S_FINAL, 7, 1)

            def turn_both():
                pe.wait_ge(final_steps, 3)
                turn_rstd(5)

            def map_hooks(v):
                if v < 4:
                    return {1: {3: sum_both}, 2: {5: turn_both}}.get(v)
                hooks = {}
                m, o = v - 4, v - 5
                if 0 <= m < MAPS:
                    for part in range(3):
                        hooks[part] = (lambda m, part: lambda: map_qk(m, part))(m, part)
                if has_out(o):
                    for r in range(3):
                        hooks[3 + r] = (lambda o, r: lambda: map_turn(o, r))(o, r)
                    hooks[7] = (lambda o: lambda: map_out(o))(o)
                if has_out(v - 6) and v - 6 >= 8:
                    scores = hooks.get(2)
                    hooks[2] = (lambda scores, h: lambda: (scores() if scores else None, map_sum(h)))(scores, (v - 6 - 9) // 2)
                return hooks

            for v in range(MIX2_UNITS):
                if v >= 2:
                    pe.wait_ge(*m2_emptied(v - 2))
                if v in (4, 5, 10, 11):
                    dense_tokens(U_MIX2 + v, 2 * (v % 2), nhi, nlo, TT, map_hooks(v))
                else:
                    dense(U_MIX2 + v, 2 * (v % 2), nhi, nlo, after_norm(N_MIX2) if v == 0 else None, hooks=map_hooks(v),
                          released=4 if v == MIX2_UNITS - 1 else 0)
            for j in range(BRANCH_UNITS):
                u = U_BRANCH + j
                hooks = map_hooks(MIX2_UNITS + j)
                unit_split(u)
                if j == 2:
                    pe.wait_ge(yb_rstd, 8)
                for m in range(4):
                    if j == 0 and m % 2 == 0:
                        pe.wait_ge(*m2_emptied(MIX2_UNITS - 2 + m // 2))
                    if j == 1 or j == 3:
                        pe.wait_ge(br_a, 4 * (j // 2) + m + 1)
                    for k in range(4):
                        if j % 2 == 0 and m == 0:
                            pe.wait_ge(y2_ready, 2 * j + k + 1)
                        w0 = k * 512 + m * P
                        mm = products(bank[(4 if j == 2 else 0) + m][:, :], whi[u % 2][:, w0:w0 + P], wlo[u % 2][:, w0:w0 + P],
                                      nhi[:, 4 * (j // 2) + k, :], nlo[:, 4 * (j // 2) + k, :], k == 0, k == 3)
                        if k == 3:
                            mm.then_inc(br_done if m < 3 else unit_done, 1)
                        part = (4 * m + k) // 2
                        if k % 2 and part in hooks:
                            hooks[part]()
            for j in range(SQUARE_UNITS):
                if j < 2:
                    pe.wait_ge(br_b, 6 + 2 * j)
                else:
                    pe.wait_ge(ypost_ready, 2 * (j - 1))
                if j < SQUARE_UNITS - 1:
                    dense(U_OUT2 + j, 2 * (j % 2), mhi, mlo,
                          (lambda k: pe.wait_ge(br_ready, k + 1)) if j == 0 else None)
                else:
                    dense_released(U_OUT2 + j, 2 * (j % 2), mhi, mlo)
            n = add_count(S_POST2, C - 1)
            pe.wait_ge(sq_added, n - 1)
            pe.matmul(bank[6][:, :], ones[:, :], sumsq[:, :], start=True, stop=False)
            pe.wait_ge(sq_ready, square_count(S_POST2, C - 1))
            pe.matmul(bank[6][:, :], ones[:, :], sq[n % 2][:, :], start=False, stop=True).then_inc(sq_summed, 1)
            ffn_products(2, U_FFN3, N_FFN3, S_FFN3, tokens=True)

        @block.scalar
        def _(act):
            def split(par, half, first=False):
                act.wait_ge(w_loaded[par], 32 * half + (32 if par else 16))
                if not first:
                    act.wait_ge(unit_done, 2 * half + (par - 1))
                act.copy(whi[par][:, :], raw[par][:, :]).then_inc(w_hi_ready, 1)

            def split_unit(u):
                if u < UNITS:
                    split(u % 2, u // 2, first=(u < 2))

            def square(g, c, source, w=0, scale=1.0):
                n = add_count(g, c, w)
                if c == 0:
                    dst = (sumsq, rstd)[w]
                else:
                    dst = sq[n % 2]
                    if n > 2:
                        act.wait_ge(sq_added, n - 2)
                act.activation(dst[:, :], source, ACT.Square, scale=scale).then_inc(sq_ready, 1)

            def feed(use, version, name, g, next_unit, released=None, last_unit=None, lag=0):
                for c in range(C + lag):
                    if c == C:
                        split_unit(next_unit)
                    if c >= C:
                        square(g, c - lag, x[:, c - lag, :])
                        continue
                    act.wait_ge(x_ready, C * version + c + 1)
                    if released is not None:
                        if c < C - 1:
                            act.wait_ge(n_used, C * released + 1 + c + 1)
                        else:
                            act.wait_ge(unit_done, last_unit + 1)
                    act.activation(nhi[:, c, :], x[:, c, :], ACT.Copy, scale=gain(name, c)).then_inc(n_hi_ready, 1)
                    if c >= lag:
                        square(g, c - lag, x[:, c - lag, :])
                if not lag:
                    split_unit(next_unit)

            def inverse_root(g, r, b=7):
                act.preload_act_table_set("natural_log_exp_and_others")
                act.wait_ge(sq_summed, SUMS_BEFORE[g] + 1)
                act.activation(sumsq[:, :], bank[b][:, :], ACT.Ln, scale=1.0 / D, bias=EPS).then_inc(ln_done, 1)
                act.wait_ge(ln_done, r + 1)
                act.activation(rstd[:, :], sumsq[:, :], ACT.Exp, scale=-0.5).then_inc(rstd_ready, 1)

            def ffn_steps(f, base):
                s_ = ffn[f]

                def gate_up(par, half, j, jj):
                    split(par, half)
                    act.wait_ge(s_["gu_scaled"], 2 * j + 1)
                    act.activation(sq[jj][:, :], sq[jj][:, :], ACT.Silu).then_inc(s_["silu_ready"], 1)
                    act.wait_ge(s_["h_product"], j + 1)
                    if isinstance(j, int):
                        dst = hhi[:, j, :]
                    else:
                        dst = hhi[:, bass.ds(j, 1), :].rearrange("p o t -> p (o t)")
                    act.copy(dst, tmp[jj][:, :]).then_inc(s_["h_hi_ready"], 1)

                def copy_turned(i, dst):
                    for half in range(2):
                        act.copy(dst[:, i % 2, T * half:T * half + T],
                                 bank[4 + 2 * (i % 2) + half][:, :]).then_inc(xt_ready, 1)

                b = base + 2
                if f == 2:
                    act.wait_ge(xt_turned, 1)
                    copy_turned(0, x_tok_a)
                for j in range(2):
                    gate_up((b + j) % 2, (b + j) // 2, j, j)
                    if f == 2 and j == 0:
                        act.wait_ge(xt_turned, 2)
                        copy_turned(1, x_tok_a)
                    if f == 2 and j == 1:
                        act.wait_ge(xt_turned, TT)
                        for i in (2, 3):
                            copy_turned(i, x_tok_b)
                with act.Fori(1, GATE_UNITS // 2) as i:
                    for j in range(2):
                        gate_up((b + j) % 2, i + (b + j) // 2, 2 * i + j, j)
                b = base + GATE_UNITS + 2
                with act.Fori(0, (DOWN_UNITS - 3) // 2) as i:
                    for j in range(2):
                        split((b + j) % 2, i + (b + j) // 2)
                for n in (DOWN_UNITS - 3, DOWN_UNITS - 2):
                    split_unit(b + n)

            act.preload_act_table_set("natural_log_exp_and_others")
            for name, rows in GAIN_ROWS:
                src = a[name]
                if len(src.shape) == 2:
                    src = src.rearrange("a d -> (a d)")
                act.dma_start(gain_rows[GAIN_AT[name]:GAIN_AT[name] + rows, :],
                              src.rearrange("(c p) -> c p", p=P)).then_inc(gain1_loaded if name == "ffn1_norm" else gains_loaded, 16)
            act.dma_start(convw[:, :, :], a["conv_w"][0].rearrange("(c p) j -> p c j", p=P)).then_inc(taps_loaded, 16)
            act.wait_ge(gain1_ready, 1)
            act.wait_ge(first_loaded, 16)
            act.copy(whi[0][:, 0:W // 2], raw[0][:, 0:W // 2]).then_inc(first_hi, 1)
            for c in range(C):
                act.wait_ge(x_turned, c + 1)
                act.activation(nhi[:, c, :], bank[c][:, :], ACT.Copy, scale=gain("ffn1_norm", c)).then_inc(n_hi_ready, 1)
            act.wait_ge(w_loaded[0], 16)
            act.copy(whi[0][:, W // 2:W], raw[0][:, W // 2:W]).then_inc(w_hi_ready, 1)
            split_unit(1)
            for c in range(C):
                act.wait_ge(x_ready, c + 1)
                square(S_FFN1, c, x[:, c, :])
            inverse_root(S_FFN1, R_FFN1)
            act.wait_ge(small_steps, 4)
            act.activation(small[:, LBE:LBE + 8], small[:, LBE:LBE + 8], ACT.Exp).then_inc(lb_exp, 1)
            ffn_steps(0, U_FFN1)
            feed(N_MIX1, X_FFN1, "mix_norm", S_MIX1, U_MIX1 + 1)
            inverse_root(S_MIX1, R_MIX1)

            def hgrn_decays(h, levels):
                for l in levels:
                    g, L = LEVELS * h + l, 1 << l
                    if l == 0:
                        act.wait_ge(logf_ready, h + 1)
                    act.wait_ge(sums_ready, 17 * h + 1 + 2 * l)
                    if g >= 2:
                        act.wait_ge(qk_used, g - 1)
                    act.activation(pairs(qk[g % 2][:, :], L, 1), pairs(hf[:, h, :], L, 1), ACT.Exp).then_inc(decay_ready, 1)
                    act.activation(pairs(qk[g % 2][:, :], L, 0), pairs(hsuf[:, :], L, 0), ACT.Exp).then_inc(decay_ready, 1)

            def far_scores(h):
                act.wait_ge(qk_used, LEVELS * (h + 1))
                if h:
                    act.wait_ge(o_done, h)
                else:
                    act.wait_ge(pt_zero, 1)
                tile = pt[:, :].rearrange("p (j c) -> p j c", c=640)
                act.copy(tile[0:64, :, 64:128], bank[6][0:64, 0:256].rearrange("p (j c) -> p j c", j=TT)).then_inc(scores_act, 1)
                act.copy(tile[:, 0:3:2, 128:256], bank[6][:, 256:512].rearrange("p (j c) -> p j c", j=2)).then_inc(scores_act, 1)
                half = pt[:, 0:1024].rearrange("p (j c) -> p j c", c=512)
                act.copy(half[:, :, 256:512], bank[7][:, :].rearrange("p (j c) -> p j c", j=2)).then_inc(scores_act, 1)

            for v in range(MIX1_UNITS + SQUARE_UNITS):
                u, pair = U_MIX1 + v, 2 * (v % 2)
                split_unit(u + 2)
                act.wait_ge(unit_done, u + 1)
                for b in range(2):
                    src = bank[pair + b][:, :]
                    ch = 2 * (v % 2) + b
                    if v < 4 or v in (6, 7):
                        if v < 4:
                            buf = (hq, hf)[v // 2][:, ch, :]
                            act.wait_ge(m1_dve, 2 * v + b + 1)
                            act.activation(buf, buf, ACT.Sigmoid if v in (2, 3) else ACT.Silu).then_inc(m1_fn, 1)
                    elif v < 6:
                        for i in (2 * b, 2 * b + 1):
                            act.activation(hv[:, i, 256 * (v % 2):256 * (v % 2) + 256], src[:, 256 * (i % 2):256 * (i % 2) + 256],
                                           ACT.Copy, scale=small[:, RTOK + i:RTOK + i + 1]).then_inc(m1_act, 1)
                    elif 14 <= v < 18:
                        if v == 14 and b == 0:
                            act.wait_ge(qk_ready, 2 * LEVELS * HEADS)
                        act.copy(km[:, 2 * (v - 14) + b, :], bank[pair + b][:, 0:MEM]).then_inc(m1_act, 1)
                if v in (2, 3):
                    for h in range(2 * (v - 2), 2 * (v - 2) + 2):
                        act.wait_ge(f_steps, 2 * h + 2)
                        act.activation(hf[:, h, :], hf[:, h, :], ACT.Ln).then_inc(logf_ready, 1)
                if v == 2:
                    act.wait_ge(rstd_turned, 1)
                    act.copy(small[:, RTOK:RTOK + TT], bank[7][:, 0:TT]).then_inc(rtok_ready, 1)
                    act.wait_ge(rtok_ready, 1)
                if v == 1:
                    for b in range(4):
                        act.wait_ge(mem_turned, b + 1)
                        act.copy(memt[:, 2 * b:2 * b + 2, :], bank[4 + b][:, :].rearrange("p (c t) -> p c t", c=2)).then_inc(memt_ready, 1)
                    act.wait_ge(memt_ready, 4)
                    act.activation(memsq[:, :, :], memt[:, :, :], ACT.Square).then_inc(memsq_ready, 1)
                if v == 3:
                    act.wait_ge(mem_summed, 1)
                    act.activation(orstd[:, 0:MEM], bank[4][:, 0:MEM], ACT.Ln, scale=1.0 / D, bias=EPS).then_inc(mem_rstd, 1)
                    act.wait_ge(mem_rstd, 1)
                    act.activation(orstd[:, 0:MEM], orstd[:, 0:MEM], ACT.Exp, scale=-0.5).then_inc(mem_rstd, 1)
                if v == 5:
                    act.wait_ge(mem_scaled, C)
                    act.copy(mnhi[:, :, :], memt[:, :, :]).then_inc(mem_hi_ready, 1)
                if v == 8:
                    act.preload_act_table_set("natural_log_exp_and_others")
                for h in range(HEADS):
                    if v == 7 + 2 * h:
                        act.wait_ge(o_done, h + 1)
                        if h:
                            act.wait_ge(y_steps, 2 * h)
                        act.copy(osb[:, :], bank[7][:, :]).then_inc(o_copied, 1)
                        act.activation(osq[:, :], bank[7][:, :], ACT.Square).then_inc(o_copied, 1)
                for h in range(HEADS):
                    if v == 6 + 2 * h:
                        far_scores(h)
                    if v == 4 + 2 * h:
                        hgrn_decays(h, range(5))
                    if v == 5 + 2 * h:
                        hgrn_decays(h, range(5, 6))
                for h in range(HEADS):
                    if v == 7 + 2 * h:
                        act.wait_ge(o_summed, h + 1)
                        act.activation(orstd[:, :], bank[6][:, :], ACT.Ln, scale=1.0 / P, bias=EPS).then_inc(o_rstd, 1)
                        act.wait_ge(o_rstd, 2 * h + 1)
                        act.activation(orstd[:, :], orstd[:, :], ACT.Exp, scale=-0.5).then_inc(o_rstd, 1)
                for h in range(HEADS):
                    if v == 5 + 2 * h:
                        hgrn_decays(h, range(6, LEVELS))
                if v == 7:
                    for ch in range(HEADS):
                        act.wait_ge(m1_dve, 8 + ch + 1)
                        act.activation(hg[:, ch, :], hg[:, ch, :], ACT.Silu).then_inc(m1_fn, 1)
                for n, c in y1_order(v):
                    if c < 4:
                        act.wait_ge(y_steps, 2 * c + 2)
                    else:
                        act.wait_ge(m1_dve, 20 + c - 4 + 1)
                    src = hq[:, c, :] if c < 4 else cv[:, c - 4, :]
                    act.copy(nhi[:, c, :], src).then_inc(y1_hi, 1)
            for j in range(SQUARE_UNITS):
                if j < 3:
                    split_unit(U_OUT1 + j + 2)
            feed(N_ATT, X_MIX1, "xattn_norm", S_ATT, U_ATT + 1, released=0, last_unit=U_ATT - 1)
            inverse_root(S_ATT, R_ATT)

            def att_exp(h):
                for i in range(TT):
                    if i % 2 == 0:
                        act.wait_ge(mx_ready, 2 * h + i // 2 + 1)
                    if i == 0 and h:
                        act.wait_ge(tx_done, h)
                    act.activation(px[:, i, :], bank[4 + i // 2][:, (i % 2) * MEM:(i % 2) * MEM + MEM], ACT.Exp,
                                   bias=small[:, 32 + i:33 + i], accum_out=small[:, 36 + i:37 + i]).then_inc(px_ready, 1)

            def att_pt(h):
                act.wait_ge(tx_done, h + 1)
                if h:
                    act.wait_ge(ax_done, 2 * h)
                for m in range(2):
                    act.copy(ptx[:, m, :], bank[6 + m][:, :]).then_inc(ptx_ready, 1)

            def att_values(h, p):
                act.wait_ge(unit_done, U_ATT + p + 1)
                for m in range(2):
                    act.copy(vm[:, m, 256 * h:256 * h + 256], bank[2 * (p % 2) + m][:, 0:256]).then_inc(vm_ready, 1)

            def att_keep(h):
                for c in range(2):
                    act.wait_ge(ax_done, 2 * h + c + 1)
                    act.copy(qx[:, 2 * h + c, :], bank[6 + c][:, :]).then_inc(ax_read, 1)

            def att_hi(c, source):
                act.copy(nhi[:, c, :], source).then_inc(ax_hi, 1)

            for p, (what, h) in enumerate(ATT_ORDER):
                if p in (3, 7):
                    att_values(h, p)
                    att_pt({3: 0, 7: 3}[p])
                split_unit(U_ATT + p + 2)
                if p == 3:
                    att_keep(0)
                    att_exp(1)
                elif p == 4:
                    att_pt(1)
                    att_keep(1)
                    att_exp(2)
                elif p == 5:
                    att_pt(2)
                    act.wait_ge(unit_done, U_ATT + 6)
                    for c in range(4):
                        att_hi(c, qx[:, c, :])
                elif p == 7:
                    for c in (6, 7):
                        act.wait_ge(ax_done, c + 1)
                        att_hi(c, bank[c][:, :])
                elif what == "v":
                    att_values(h, p)
                    att_exp({1: 0, 6: 3}[p])
                    if p == 6:
                        for c in (4, 5):
                            act.wait_ge(ax_done, c + 1)
                            att_hi(c, bank[2 + c][:, :])
            for j in range(SQUARE_UNITS):
                if j < 3:
                    split_unit(U_O + j + 2)
            feed(N_FFN2, X_ATT, "ffn2_norm", S_FFN2, U_FFN2 + 1, released=1, last_unit=U_FFN2 - 1)
            inverse_root(S_FFN2, R_FFN2)
            ffn_steps(1, U_FFN2)
            act.preload_act_table_set("natural_log_exp_and_others")
            for c in range(C):
                act.wait_ge(x_ready, C * X_FFN2 + c + 1)
                act.activation(nhi[:, c, :], x[:, c, :], ACT.Copy, scale=small[:, GG + c:GG + c + 1]).then_inc(n_hi_ready, 1)
                square(S_FINAL, c, x[:, c, :])
            for c in range(C):
                if c == 2:
                    split_unit(U_MIX2 + 1)
                square(S_FINAL, c, x[:, c, :], 1, gain("final_norm", c))
            split_unit(U_MIX2 + 2)
            act.wait_ge(sq_summed, SUMS_BEFORE[S_FINAL] + 1)
            act.activation(sumsq[:, :], bank[6][:, :], ACT.Ln, scale=1.0 / D, bias=EPS).then_inc(ln_done, 1)
            act.wait_ge(ln_done, R_FINAL + 1)
            act.activation(sumsq[:, :], sumsq[:, :], ACT.Exp, scale=-0.5).then_inc(rstd_ready, 1)
            act.wait_ge(final_steps, 2)
            act.activation(rstd[:, :], rstd[:, :], ACT.Ln, scale=1.0 / D, bias=EPS).then_inc(ln_done, 1)
            act.wait_ge(ln_done, R_MIX2 + 1)
            act.activation(rstd[:, :], rstd[:, :], ACT.Exp, scale=-0.5).then_inc(rstd_ready, 1)

            act.wait_ge(lam_steps, 2)
            act.activation(small[:, LEXP:LEXP + 2], small[:, LSUM:LSUM + 2], ACT.Exp).then_inc(lam_exp, 1)

            def map_exps(m):
                for n, i in enumerate((3, 2, 0, 1)):
                    act.wait_ge(map_neg, m + 1)
                    w = P * (i + 1)
                    p_ = pm[m % 2][:, TILE_AT[i]:TILE_AT[i] + w]
                    act.activation(p_, p_, ACT.Exp, bias=stat[:, m % 2, 1, i:i + 1],
                                   accum_out=stat[:, m % 2, 2, i:i + 1]).then_inc(map_exp, 1)

            def map_copies(m):
                n = m if m < 8 else 8 + (m - 8) // 2
                if n:
                    act.wait_ge(av_done, n)
                for r, (lo, hi) in enumerate(((0, 512), (512, 1024), (1024, 1280))):
                    act.wait_ge(map_turned, 3 * n + r + 1)
                    act.copy(ptm[:, lo:hi], bank[7][:, 0:hi - lo]).then_inc(map_pt, 1)

            def map_y(m):
                if m < 8:
                    act.wait_ge(av_done, m + 1)
                    rows = slice(64 * (m % 2), 64 * (m % 2) + 64)
                    act.copy(mq[rows, m // 2, :], bank[6][rows, :]).then_inc(ya_copied, 1)
                else:
                    h = (m - 8) // 2
                    act.wait_ge(av_done, 8 + h + 1)
                    if h:
                        act.wait_ge(yb_summed, h)
                    act.copy(dq[:, h, :], bank[6][:, :]).then_inc(yb_copied, 1)
                    act.activation(ysq[:, :], bank[6][:, :], ACT.Square).then_inc(yb_sq, 1)

            def map_root(h):
                act.wait_ge(yb_summed, h + 1)
                if h:
                    act.wait_ge(y2_steps, h)
                act.activation(yrstd[:, :], bank[7][:, :], ACT.Ln, scale=1.0 / P, bias=EPS_SUBLN).then_inc(yb_rstd, 1)
                act.wait_ge(yb_rstd, 2 * h + 1)
                act.activation(yrstd[:, :], yrstd[:, :], ACT.Exp, scale=-0.5).then_inc(yb_rstd, 1)

            def has_out(m):
                return 0 <= m < 8 or (8 <= m < MAPS and m % 2 == 1)

            def y2_hi_part(c):
                act.copy(nhi[:, c, :], (mq[:, c, :] if c < 4 else dq[:, c - 4, :])).then_inc(y2_hi, 1)

            for v in range(MIX2_UNITS + 2):
                if has_out(v - 5):
                    map_y(v - 5)
                if v:
                    split_unit(U_MIX2 + v + 2)
                if v < MIX2_UNITS:
                    act.wait_ge(unit_done, U_MIX2 + v + 1)
                    for b in range(2):
                        if v in (4, 5, 10, 11):
                            for i in (2 * b, 2 * b + 1):
                                act.activation((mv if v < 6 else dv)[:, i, 256 * (v % 2):256 * (v % 2) + 256],
                                               bank[2 * (v % 2) + b][:, 256 * (i % 2):256 * (i % 2) + 256],
                                               ACT.Copy, scale=small[:, RTOK + i:RTOK + i + 1]).then_inc(m2_act, 1)
                        elif v >= 12:
                            g_ = (ga if v < 16 else gb)[:, 2 * (v % 4) + b, :]
                            act.wait_ge(m2_dve, 16 + 2 * (v - 12) + b + 1)
                            act.activation(g_, g_, ACT.Tanh, scale=0.5).then_inc(m2_tanh, 1)
                    if v == 2:
                        act.wait_ge(rstd_turned, 2)
                        act.copy(small[:, RTOK:RTOK + TT], bank[5][:, 0:TT]).then_inc(rtok_ready, 1)
                        act.wait_ge(rtok_ready, 2)
                if has_out(v - 5) and v - 5 >= 8:
                    map_root((v - 5 - 9) // 2)
                if has_out(v - 4):
                    map_copies(v - 4)
                if v == MIX2_UNITS - 2:
                    act.wait_ge(ya_copied, 8)
                    for c in range(4):
                        act.wait_ge(n_used, 2 * C + c + 1)
                        y2_hi_part(c)
                if 0 <= v - 3 < MAPS:
                    map_exps(v - 3)
                if v == MIX2_UNITS - 1:
                    for c in (4, 5, 6):
                        act.wait_ge(y2_steps, c - 3)
                        y2_hi_part(c)
                if v == MIX2_UNITS:
                    act.wait_ge(y2_steps, 4)
                    y2_hi_part(7)
                if v == MIX2_UNITS + 1:
                    for c in range(4):
                        act.wait_ge(br_sum, c + 1)
                        act.copy(mhi[:, c, :], tmp[c % 2][:, :]).then_inc(br_hi, 1)
            split_unit(U_OUT2)
            for c in range(4, C):
                act.wait_ge(br_sum, c + 1)
                act.copy(mhi[:, c, :], tmp[c % 2][:, :]).then_inc(br_hi, 1)
            split_unit(U_OUT2 + 1)
            for j in range(SQUARE_UNITS):
                split_unit(U_OUT2 + j + 2) if j < 3 else None
                for c in (2 * j, 2 * j + 1):
                    if c == C - 2:
                        act.wait_ge(n_used, 2 * C + 4 + 1)
                    else:
                        act.wait_ge(unit_done, U_OUT2 + j + 1)
                    src = bank[c % 4][:, :]
                    square(S_POST2, c, src, scale=0.5)
                    act.activation(ypost[:, c, :], src, ACT.Copy, scale=small[:, PG + c:PG + c + 1]).then_inc(ypost_ready, 1)
            inverse_root(S_POST2, R_POST2, 6)
            feed(N_FFN3, X_MIX2, "norm_ffn_pre_g_2", S_FFN3, U_FFN3 + 1, lag=3)
            inverse_root(S_FFN3, R_FFN3)
            ffn_steps(2, U_FFN3)

            act.preload_act_table_set("natural_log_exp_and_others")
            for i in range(TT):
                if i < TT - 1:
                    act.wait_ge(ffn[2]["down_done"], i + 1)
                else:
                    act.wait_ge(unit_done, UNITS)
                for half in range(2):
                    if i:
                        act.wait_ge(y3_sq, 2 * i - 1 + half)
                    act.activation(sq[half][:, :], bank[2 * i + half][:, :], ACT.Square,
                                   accum_out=small[:, SS + 2 * i + half:SS + 2 * i + half + 1]).then_inc(y3_sq, 1)
                act.wait_ge(y3_sum, i + 1)
                root = small[:, RT3 + i:RT3 + i + 1]
                act.activation(root, root, ACT.Ln, scale=1.0 / D, bias=EPS).then_inc(y3_root, 1)
                act.wait_ge(y3_root, 2 * i + 1)
                act.activation(root, root, ACT.Exp, scale=-0.5).then_inc(y3_root, 1)

        @block.vector
        def _(dve):
            def split(par, half):
                dve.wait_ge(w_hi_ready, 2 * half + (par + 1))
                dve.tensor_tensor(wlo[par][:, :], raw[par][:, :], whi[par][:, :].bitcast(F32), ALU.subtract).then_inc(w_lo_ready, 1)

            def split_unit(u):
                if u < UNITS:
                    split(u % 2, u // 2)

            def lo(use, gain_at, c):
                dve.wait_ge(n_hi_ready, C * use + c + 1)
                dve.scalar_tensor_tensor(nlo[:, c, :], x[:, c, :], gain_at(c), nhi[:, c, :].bitcast(F32),
                                         ALU.mult, ALU.subtract).then_inc(n_ready, 1)

            def named(name):
                return lambda c: gain(name, c)

            def add_down(f, base, use, gain_at):
                for c in range(C):
                    if c < C - 1:
                        dve.wait_ge(ffn[f]["down_done"], c + 1)
                    else:
                        dve.wait_ge(unit_done, base + FFN_UNITS)
                    dve.scalar_tensor_tensor(x[:, c, :], bank[c][:, :], 0.5, x[:, c, :], ALU.mult, ALU.add).then_inc(x_ready, 1)
                    if c:
                        lo(use, gain_at, c - 1)
                lo(use, gain_at, C - 1)

            def add_square(base, stage, use, name):
                for j in range(SQUARE_UNITS):
                    if j < 3:
                        split_unit(base + j + 2)
                    for c in (2 * j, 2 * j + 1):
                        if c == C - 2:
                            dve.wait_ge(n_used, C * stage + 1)
                        else:
                            dve.wait_ge(unit_done, base + j + 1)
                        dve.tensor_tensor(x[:, c, :], bank[c % 4][:, :], x[:, c, :], ALU.add).then_inc(x_ready, 1)
                        if c == C - 2:
                            for done in range(C - 2):
                                lo(use, named(name), done)
                for c in (C - 2, C - 1):
                    lo(use, named(name), c)

            def ffn_steps(f, base, root):
                s_ = ffn[f]

                def gate_up(par, half, j, jj, first):
                    split(par, half)
                    dve.wait_ge(unit_done, 2 * half + (par - 1))
                    if not first:
                        dve.wait_ge(s_["h_ready"], j - 1)
                    dve.tensor_tensor(sq[jj][:, :], bank[2 * jj][:, :], rstd[:, :], ALU.mult).then_inc(s_["gu_scaled"], 1)
                    dve.tensor_tensor(tmp[jj][:, :], bank[2 * jj + 1][:, :], rstd[:, :], ALU.mult).then_inc(s_["gu_scaled"], 1)
                    dve.wait_ge(s_["silu_ready"], j + 1)
                    dve.wait_ge(s_["gu_scaled"], 2 * j + 2)
                    dve.tensor_tensor(tmp[jj][:, :], sq[jj][:, :], tmp[jj][:, :], ALU.mult).then_inc(s_["h_product"], 1)
                    dve.wait_ge(s_["h_hi_ready"], j + 1)
                    if isinstance(j, int):
                        dst, hi = hlo[:, j, :], hhi[:, j, :].bitcast(F32)
                    else:
                        dst = hlo[:, bass.ds(j, 1), :].rearrange("p o t -> p (o t)")
                        hi = hhi[:, :, :].bitcast(F32)[:, bass.ds(j, 1), :].rearrange("p o t -> p (o t)")
                    dve.tensor_tensor(dst, tmp[jj][:, :], hi, ALU.subtract).then_inc(s_["h_ready"], 1)

                b = base + 2
                dve.wait_ge(rstd_ready, root + 1)
                for j in range(2):
                    gate_up((b + j) % 2, (b + j) // 2, j, j, True)
                with dve.Fori(1, GATE_UNITS // 2) as i:
                    for j in range(2):
                        gate_up((b + j) % 2, i + (b + j) // 2, 2 * i + j, j, False)
                b = base + GATE_UNITS + 2
                with dve.Fori(0, (DOWN_UNITS - 3) // 2) as i:
                    for j in range(2):
                        split((b + j) % 2, i + (b + j) // 2)
                for n in (DOWN_UNITS - 3, DOWN_UNITS - 2):
                    split_unit(b + n)

            dve.wait_ge(mask_iota, 2)
            dve.tensor_scalar(maskt[:, 0, :], maskt[:, 0, :], 31, None, ALU.bitwise_and).then_inc(mask_steps, 1)
            dve.wait_ge(mask_steps, 1)
            dve.tensor_tensor(maskt[:, 2, :], maskt[:, 1, :], maskt[:, 0, :], ALU.is_gt).then_inc(mask_steps, 1)
            dve.tensor_tensor(masks[:, 0, :], maskt[:, 1, :], maskt[:, 0, :], ALU.bitwise_xor).then_inc(mask_steps, 1)
            dve.wait_ge(mask_steps, 3)
            for l in range(5):
                dve.scalar_tensor_tensor(masks[:, 1 + l, :], masks[:, 0, :], float(1 << l), maskt[:, 2, :],
                                         ALU.is_ge, ALU.mult).then_inc(mask_steps, 1)
            dve.wait_ge(mask_steps, 8)
            dve.tensor_scalar(masks[:, 0, :], masks[:, 0, :], 0.0, None, ALU.is_equal).then_inc(mask_steps, 1)
            dve.wait_ge(gain1_t, 1)
            dve.tensor_copy(gains[:, 0:C], bank[7][:, 0:C]).then_inc(gain1_ready, 1)
            dve.wait_ge(gain1_ready, 1)
            dve.wait_ge(first_hi, 1)
            dve.tensor_tensor(wlo[0][:, 0:W // 2], raw[0][:, 0:W // 2], whi[0][:, 0:W // 2].bitcast(F32),
                              ALU.subtract).then_inc(first_lo, 1)
            for c in range(C):
                dve.wait_ge(n_hi_ready, c + 1)
                dve.scalar_tensor_tensor(nlo[:, c, :], bank[c][:, :], gain("ffn1_norm", c), nhi[:, c, :].bitcast(F32),
                                         ALU.mult, ALU.subtract).then_inc(n_ready, 1)
                if c < 2:
                    dve.tensor_copy(x[:, c, :], bank[c][:, :]).then_inc(x_ready, 1)
            dve.wait_ge(w_hi_ready, 1)
            dve.tensor_tensor(wlo[0][:, W // 2:W], raw[0][:, W // 2:W], whi[0][:, W // 2:W].bitcast(F32),
                              ALU.subtract).then_inc(w_lo_ready, 1)
            for c in range(2, C):
                dve.tensor_copy(x[:, c, :], bank[c][:, :]).then_inc(x_ready, 1)
            split_unit(1)
            dve.wait_ge(gains_t, 1)
            dve.tensor_copy(gains[:, C:GAINS], bank[6][:, C:GAINS]).then_inc(gains_ready, 1)
            dve.wait_ge(gains_ready, 1)
            g0 = GAIN_AT["lb_param"]
            r0, r1 = gains[:, g0:g0 + 4], gains[:, g0 + 4:g0 + 8]
            dve.tensor_tensor(small[:, LB:LB + 4], r0, r1, ALU.max).then_inc(small_steps, 1)
            dve.wait_ge(small_steps, 1)
            dve.tensor_tensor(small[:, LBE:LBE + 4], r0, small[:, LB:LB + 4], ALU.subtract).then_inc(small_steps, 1)
            dve.tensor_tensor(small[:, LBE + 4:LBE + 8], r1, small[:, LB:LB + 4], ALU.subtract).then_inc(small_steps, 1)
            dve.tensor_scalar(small[:, SUBG:SUBG + 1], gain("diff_subln_g_2", 0), 1.0 - LAM_INIT, None, ALU.mult).then_inc(small_steps, 1)
            dve.tensor_tensor(small[:, GG:GG + C], gains[:, GAIN_AT["final_norm"]:GAIN_AT["final_norm"] + C],
                              gains[:, GAIN_AT["norm_mix_pre_g_2"]:GAIN_AT["norm_mix_pre_g_2"] + C], ALU.mult).then_inc(small_steps, 1)
            dve.tensor_scalar(small[:, PG:PG + C], gains[:, GAIN_AT["norm_mix_post_g_2"]:GAIN_AT["norm_mix_post_g_2"] + C],
                              0.5, None, ALU.mult).then_inc(small_steps, 1)
            dve.wait_ge(lb_exp, 1)
            dve.tensor_tensor(small[:, LB:LB + 4], small[:, LBE:LBE + 4], small[:, LBE + 4:LBE + 8], ALU.add).then_inc(small_steps, 1)
            dve.wait_ge(small_steps, 7)
            dve.reciprocal(small[:, LB + 4:LB + 8], small[:, LB:LB + 4]).then_inc(small_steps, 1)
            dve.wait_ge(small_steps, 8)
            dve.tensor_tensor(small[:, LB:LB + 4], small[:, LBE:LBE + 4], small[:, LB + 4:LB + 8], ALU.mult).then_inc(small_steps, 1)
            dve.wait_ge(small_steps, 9)
            dve.tensor_scalar(small[:, OMLB:OMLB + 4], small[:, LB:LB + 4], -1.0, 1.0, ALU.mult, ALU.add).then_inc(small_steps, 1)
            dve.wait_ge(small_steps, 10)
            ffn_steps(0, U_FFN1, R_FFN1)
            add_down(0, U_FFN1, N_MIX1, named("mix_norm"))
            split_unit(U_MIX1 + 1)

            def hgrn_levels(h, levels):
                for l in levels:
                    g, L = LEVELS * h + l, 1 << l
                    dve.wait_ge(decay_ready, 2 * g + 2)
                    z = qk[g % 2][:, :]
                    dve.tensor_tensor(pairs(z, L, 1), pairs(z, L, 1), pairs(hq[:, h, :], L, 1), ALU.mult).then_inc(qk_ready, 1)
                    dve.tensor_tensor(pairs(z, L, 0), pairs(z, L, 0), pairs(hk[:, h, :], L, 0), ALU.mult).then_inc(qk_ready, 1)

            def near_scores(h):
                dve.wait_ge(diag_done, h + 1)
                dve.wait_ge(qk_used, LEVELS * h + 6)
                if h:
                    dve.wait_ge(scores_dve, 6 * h)
                dve.memset(s32[:, :, :], 0.0).then_inc(s32_steps, 1)
                for l in range(6):
                    dve.wait_ge(s32_steps, 7 * h + l + 1)
                    b, slot = (bank[4], l) if l < 4 else (bank[5], l - 4)
                    dve.copy_predicated(s32[:, :, :], masks[:, l:l + 1, :].to_broadcast([P, TT, 32]),
                                        b[:, slot * P:slot * P + P].rearrange("p (j t) -> p j t", j=TT)).then_inc(s32_steps, 1)
                dve.wait_ge(s32_steps, 7 * h + 7)
                if h:
                    dve.wait_ge(o_done, h)
                else:
                    dve.wait_ge(pt_zero, 1)
                tile = pt[:, :].rearrange("p (j c) -> p j c", c=640)
                for m in range(4):
                    r = slice(32 * m, 32 * m + 32)
                    dve.tensor_copy(tile[r, :, 32 * m:32 * m + 32], s32[r, :, :]).then_inc(scores_dve, 1)
                for m in range(2):
                    r = slice(64 * m, 64 * m + 32)
                    dve.tensor_copy(tile[r, :, 64 * m + 32:64 * m + 64],
                                    bank[5][r, 256:384].rearrange("p (j c) -> p j c", j=TT)).then_inc(scores_dve, 1)

            for v in range(MIX1_UNITS + SQUARE_UNITS):
                u, pair = U_MIX1 + v, 2 * (v % 2)
                split_unit(u + 2)
                if v < 4 or v in (6, 7):
                    dve.wait_ge(rstd_ready, R_MIX1 + 1)
                    dve.wait_ge(unit_done, u + 1)
                    for b in range(2):
                        dve.tensor_tensor((hq, hf, None, hg)[v // 2][:, 2 * (v % 2) + b, :], bank[pair + b][:, :], rstd[:, :],
                                          ALU.mult).then_inc(m1_dve, 1)
                if v == 2:
                    dve.tensor_tensor(tmp[0][:, :], rstd[:, :], rstd[:, :], ALU.mult).then_inc(conv_pad, 1)
                if v < 2:
                    for h in (2 * v, 2 * v + 1):
                        dve.wait_ge(m1_fn, h + 1)
                        dve.tensor_scalar(hq[:, h, :], hq[:, h, :], 128.0 ** -0.5, None, ALU.mult).then_inc(q_scaled, 1)
                if v in (2, 3):
                    for h in (2 * (v - 2), 2 * (v - 2) + 1):
                        dve.wait_ge(m1_fn, 4 + h + 1)
                        dve.tensor_scalar(hf[:, h, :], hf[:, h, :], small[:, OMLB + h:OMLB + h + 1],
                                          small[:, LB + h:LB + h + 1], ALU.mult, ALU.add).then_inc(f_steps, 1)
                        dve.wait_ge(f_steps, 2 * h + 1)
                        dve.tensor_scalar(hk[:, h, :], hf[:, h, :], -1.0, 1.0, ALU.mult, ALU.add).then_inc(f_steps, 1)
                if v == 4:
                    dve.wait_ge(mem_rstd, 2)
                    for c in range(C):
                        dve.scalar_tensor_tensor(memt[:, c, :], memt[:, c, :], gain("mem_norm", c), orstd[:, 0:MEM],
                                                 ALU.mult, ALU.mult).then_inc(mem_scaled, 1)
                if v == 5:
                    dve.wait_ge(mem_hi_ready, 1)
                    dve.tensor_tensor(mnlo[:, :, :], memt[:, :, :], mnhi[:, :, :].bitcast(F32), ALU.subtract).then_inc(mem_ready, 1)
                    dve.memset(pt[:, :], 0.0).then_inc(pt_zero, 1)
                if v == 8:
                    dve.wait_ge(mem_ready, 1)
                    dve.memset(cu[:, :, 0:2], 0.0).then_inc(conv_pad, 1)
                    dve.wait_ge(conv_pad, 2)
                    dve.wait_ge(taps_loaded, 16)
                if v in (8, 9):
                    dve.wait_ge(unit_done, u + 1)
                    for b in range(2):
                        dve.tensor_tensor(cu[:, 2 * (v % 2) + b, 2:T + 2], bank[pair + b][:, :], tmp[0][:, :],
                                          ALU.mult).then_inc(m1_dve, 1)
                if v in (10, 11):
                    for b in range(2):
                        c = 2 * (v % 2) + b
                        dve.wait_ge(unit_done, u + 1)
                        dve.wait_ge(m1_dve, 12 + c + 1)
                        dve.tensor_tensor(cu[:, c, 2:T + 2], cu[:, c, 2:T + 2], bank[pair + b][:, :], ALU.mult).then_inc(m1_dve, 1)
                if v in (12, 13):
                    for b in range(2):
                        c = 2 * (v % 2) + b
                        dve.wait_ge(unit_done, u + 1)
                        dve.wait_ge(conv_steps, 4 * c + 4)
                        dve.tensor_tensor(cv[:, c, :], cv[:, c, :], bank[pair + b][:, :], ALU.mult).then_inc(m1_dve, 1)
                for h in range(HEADS):
                    if v == 4 + 2 * h:
                        hgrn_levels(h, range(5))
                    if v == 5 + 2 * h:
                        hgrn_levels(h, range(5, LEVELS))
                        near_scores(h)
                for h in range(HEADS):
                    if v == 8 + 2 * h:
                        dve.wait_ge(m1_fn, 8 + h + 1)
                        dve.wait_ge(o_rstd, 2 * h + 2)
                        dve.scalar_tensor_tensor(osb[:, :], osb[:, :], gain("hgrn_out_norm", h), orstd[:, :],
                                                 ALU.mult, ALU.mult).then_inc(y_steps, 1)
                        dve.wait_ge(y_steps, 2 * h + 1)
                        dve.tensor_tensor(hq[:, h, :], osb[:, :], hg[:, h, :], ALU.mult).then_inc(y_steps, 1)
                if v in (10, 11):
                    for c in (2 * (v % 2), 2 * (v % 2) + 1):
                        dve.wait_ge(m1_dve, 16 + c + 1)
                        dve.tensor_scalar(cv[:, c, :], cu[:, c, 0:T], convw[:, c, 0:1], None, ALU.mult).then_inc(conv_steps, 1)
                        for j in (1, 2):
                            dve.wait_ge(conv_steps, 4 * c + j)
                            dve.scalar_tensor_tensor(cv[:, c, :], cu[:, c, j:T + j], convw[:, c, j:j + 1], cv[:, c, :],
                                                     ALU.mult, ALU.add).then_inc(conv_steps, 1)
                        dve.wait_ge(conv_steps, 4 * c + 3)
                        dve.tensor_tensor(cv[:, c, :], cv[:, c, :], rstd[:, :], ALU.mult).then_inc(conv_steps, 1)
                for n, c in y1_order(v):
                    dve.wait_ge(y1_hi, n + 1)
                    src = hq[:, c, :] if c < 4 else cv[:, c - 4, :]
                    dve.tensor_tensor(nlo[:, c, :], src, nhi[:, c, :].bitcast(F32), ALU.subtract).then_inc(y1_ready, 1)
            add_square(U_OUT1, 0, N_ATT, "xattn_norm")
            split_unit(U_ATT + 1)

            def att_max(h):
                for b in range(2):
                    dve.wait_ge(sx_done, 2 * h + b + 1)
                    if h and b == 0:
                        dve.wait_ge(px_ready, TT * h)
                    dve.tensor_reduce(small[:, 32 + 2 * b:34 + 2 * b], bank[4 + b][:, :].rearrange("p (i m) -> p i m", i=2),
                                      AX_X, ALU.max, negate=True).then_inc(mx_ready, 1)

            def att_norm(h):
                dve.wait_ge(px_ready, TT * h + TT)
                dve.reciprocal(small[:, 40:44], small[:, 36:40]).then_inc(px_inv, 1)
                dve.wait_ge(px_inv, h + 1)
                for i in range(TT):
                    dve.tensor_scalar(px[:, i, :], px[:, i, :], small[:, 40 + i:41 + i], None, ALU.mult).then_inc(px_norm, 1)

            def att_lo(c, source):
                dve.wait_ge(ax_hi, c + 1)
                return dve.tensor_tensor(nlo[:, c, :], source, nhi[:, c, :].bitcast(F32), ALU.subtract).then_inc(ax_ready, 1)

            for p, (what, h) in enumerate(ATT_ORDER):
                if what == "q":
                    if p == 0:
                        dve.wait_ge(rstd_ready, R_ATT + 1)
                    dve.wait_ge(unit_done, U_ATT + p + 1)
                    for b in range(2):
                        dve.scalar_tensor_tensor(qx[:, 2 * h + b, :], bank[2 * (p % 2) + b][:, :], 256.0 ** -0.5, rstd[:, :],
                                                 ALU.mult, ALU.mult).then_inc(qx_ready, 1)
                head = {1: 0, 3: 1, 4: 2, 6: 3}.get(p)
                if p == 6:
                    att_max(3)
                split_unit(U_ATT + p + 2)
                if head is not None:
                    if p != 6:
                        att_max(head)
                    att_norm(head)
                if p == 5:
                    for c in range(4):
                        att_lo(c, qx[:, c, :])
                if p in (6, 7):
                    for c in range(2 * p - 8, 2 * p - 6):
                        att_lo(c, bank[6 + c % 2][:, :])
            add_square(U_O, 1, N_FFN2, "ffn2_norm")
            split_unit(U_FFN2 + 1)
            ffn_steps(1, U_FFN2, R_FFN2)
            add_down(1, U_FFN2, N_MIX2, lambda c: small[:, GG + c:GG + c + 1])
            split_unit(U_MIX2 + 1)
            split_unit(U_MIX2 + 2)
            dve.wait_ge(sq_summed, SUMS_BEFORE[S_FINAL] + 2)
            dve.wait_ge(rstd_ready, R_FINAL + 1)
            dve.tensor_tensor(rstd[:, :], sumsq[:, :], sumsq[:, :], ALU.mult).then_inc(final_steps, 1)
            dve.wait_ge(final_steps, 1)
            dve.tensor_tensor(rstd[:, :], rstd[:, :], bank[7][:, :], ALU.mult).then_inc(final_steps, 1)
            dve.wait_ge(rstd_ready, R_MIX2 + 1)
            dve.tensor_tensor(rstd[:, :], rstd[:, :], sumsq[:, :], ALU.mult).then_inc(final_steps, 1)
            dve.wait_ge(final_steps, 3)

            dve.wait_ge(lam_loaded, 64)
            for n in range(2):
                dve.tensor_tensor_reduce(lams[:, :], lamv[:, 2 * n, :], lamv[:, 2 * n + 1, :], 1.0, 0.0, ALU.mult, ALU.add,
                                         small[:, LSUM + n:LSUM + n + 1]).then_inc(lam_steps, 1)
                dve.wait_ge(lam_steps, n + 1)
            dve.wait_ge(lam_exp, 1)
            dve.tensor_tensor(small[:, NLAM:NLAM + 1], small[:, LEXP + 1:LEXP + 2], small[:, LEXP:LEXP + 1], ALU.subtract).then_inc(lam_steps, 1)
            dve.wait_ge(lam_steps, 3)
            dve.tensor_scalar(small[:, NLAM:NLAM + 1], small[:, NLAM:NLAM + 1], -LAM_INIT, None, ALU.add).then_inc(lam_steps, 1)
            dve.wait_ge(lam_steps, 4)

            def map_maxima(m):
                st = stat[:, m % 2]
                dve.wait_ge(bias_ready, m + 1)
                if m >= 2:
                    dve.wait_ge(map_norm, 4 * (m - 1))
                    outs = m - 1 if m <= 9 else 8 + (m - 1 - 8) // 2
                    if m - 2 < 8 or (m - 2) % 2:
                        dve.wait_ge(map_turned, 3 * outs)
                for n, i in enumerate((3, 2, 0, 1)):
                    w = P * (i + 1)
                    b = bank[{3: 4, 2: 5, 0: 5, 1: 6}[i]]
                    col = 384 if i == 0 else 0
                    dve.wait_ge(map_scores, 4 * m + (1, 3, 3, 4)[n])
                    dve.tensor_tensor_reduce(pm[m % 2][:, TILE_AT[i]:TILE_AT[i] + w], b[:, col:col + w],
                                             bias[m % 2][:, (3 - i) * P:T], 1.0, -3.0e38, ALU.add, ALU.max,
                                             st[:, 0, i:i + 1]).then_inc(map_max, 1)
                dve.wait_ge(map_max, 4 * m + 4)
                dve.tensor_scalar(st[:, 1, :], st[:, 0, :], -1.0, None, ALU.mult).then_inc(map_neg, 1)

            def map_softmax(m):
                st = stat[:, m % 2]
                dve.wait_ge(map_exp, 4 * m + 4)
                dve.reciprocal(st[:, 3, :], st[:, 2, :]).then_inc(map_inv, 1)
                inv = m + 1 + max(0, (m - 8 + 0) // 2 if m >= 8 else 0)
                dve.wait_ge(map_inv, inv)
                if m >= 8 and m % 2:
                    dve.tensor_scalar(st[:, 3, :], st[:, 3, :], small[:, NLAM:NLAM + 1], None, ALU.mult).then_inc(map_inv, 1)
                    dve.wait_ge(map_inv, inv + 1)
                for n, i in enumerate((3, 2, 0, 1)):
                    w = P * (i + 1)
                    p_ = pm[m % 2][:, TILE_AT[i]:TILE_AT[i] + w]
                    if m >= 8 and m % 2:
                        dve.scalar_tensor_tensor(p_, p_, st[:, 3, i:i + 1], pm[0][:, TILE_AT[i]:TILE_AT[i] + w],
                                                 ALU.mult, ALU.add).then_inc(map_norm, 1)
                    else:
                        dve.tensor_scalar(p_, p_, st[:, 3, i:i + 1], None, ALU.mult).then_inc(map_norm, 1)
                dve.wait_ge(map_norm, 4 * m + 4)

            def branch(j):
                for m in range(4):
                    c = 4 * (j % 2) + m
                    if m < 3:
                        dve.wait_ge(br_done, 3 * j + m + 1)
                    else:
                        dve.wait_ge(unit_done, U_BRANCH + j + 1)
                    dve.wait_ge(m2_tanh, C * (j // 2) + c + 1)
                    if j < 2:
                        dve.scalar_tensor_tensor(ga[:, c, :], ga[:, c, :], 1.0, bank[m][:, :], ALU.add, ALU.mult).then_inc(br_a, 1)
                    else:
                        dve.scalar_tensor_tensor(gb[:, c, :], gb[:, c, :], 1.0, bank[(4 if j == 2 else 0) + m][:, :],
                                                 ALU.add, ALU.mult).then_inc(br_b, 1)
                        dve.wait_ge(br_b, c + 1)
                        dve.wait_ge(br_a, c + 1)
                        if c >= 2:
                            dve.wait_ge(br_ready, c - 1)
                        dve.tensor_tensor(tmp[c % 2][:, :], ga[:, c, :], gb[:, c, :], ALU.add).then_inc(br_sum, 1)
                        if m:
                            merged_lo(c - 1)
                if j >= 2:
                    merged_lo(c)

            def merged_lo(c):
                dve.wait_ge(br_hi, c + 1)
                dve.tensor_tensor(mlo[:, c, :], tmp[c % 2][:, :], mhi[:, c, :].bitcast(F32), ALU.subtract).then_inc(br_ready, 1)

            def y2_lo_part(c):
                dve.wait_ge(y2_hi, c + 1)
                dve.tensor_tensor(nlo[:, c, :], (mq[:, c, :] if c < 4 else dq[:, c - 4, :]), nhi[:, c, :].bitcast(F32),
                                  ALU.subtract).then_inc(y2_ready, 1)

            for v in range(MIX2_UNITS + 2):
                if v not in (0, MIX2_UNITS - 1):
                    split_unit(U_MIX2 + v + 2)
                if v < MIX2_UNITS:
                    dve.wait_ge(unit_done, U_MIX2 + v + 1)
                    for b in range(2):
                        src, ch = bank[2 * (v % 2) + b][:, :], 2 * (v % 2) + b
                        if v in (0, 1, 6, 7):
                            dve.scalar_tensor_tensor((mq if v < 2 else dq)[:, ch, :], src, 64.0 ** -0.5, rstd[:, :],
                                                     ALU.mult, ALU.mult).then_inc(m2_dve, 1)
                        elif v in (2, 3, 8, 9):
                            dve.tensor_tensor((mk if v < 4 else dk)[:, ch, :], src, rstd[:, :], ALU.mult).then_inc(m2_dve, 1)
                        elif v >= 12:
                            if v == 16 and b == 0:
                                dve.wait_ge(av_done, 8)
                            dve.tensor_tensor((ga if v < 16 else gb)[:, 2 * (v % 4) + b, :], src, rstd[:, :],
                                              ALU.mult).then_inc(m2_dve, 1)
                if v == MIX2_UNITS - 1:
                    map_softmax(MAPS - 1)
                    split_unit(U_MIX2 + v + 2)
                if v < 4:
                    for c in (2 * v, 2 * v + 1):
                        dve.scalar_tensor_tensor(x[:, c, :], x[:, c, :], gain("final_norm", c), sumsq[:, :],
                                                 ALU.mult, ALU.mult).then_inc(x_ready, 1)
                if 0 <= v - 3 < MAPS:
                    map_maxima(v - 3)
                if v == MIX2_UNITS - 2:
                    for c in range(4):
                        y2_lo_part(c)
                if 0 <= v - 3 < MAPS - 1:
                    map_softmax(v - 3)
                if v - 5 >= 9 and (v - 5) % 2:
                    h = (v - 5 - 9) // 2
                    dve.wait_ge(yb_rstd, 2 * h + 2)
                    dve.wait_ge(yb_copied, h + 1)
                    dve.scalar_tensor_tensor(dq[:, h, :], dq[:, h, :], small[:, SUBG:SUBG + 1], yrstd[:, :],
                                             ALU.mult, ALU.mult).then_inc(y2_steps, 1)
                if v == MIX2_UNITS - 1:
                    for c in (4, 5, 6):
                        y2_lo_part(c)
                    branch(0)
                if v == MIX2_UNITS:
                    y2_lo_part(7)
                    branch(1)
            branch(2)
            split_unit(U_OUT2)
            branch(3)
            split_unit(U_OUT2 + 1)
            for j in range(SQUARE_UNITS):
                if j < 3:
                    split_unit(U_OUT2 + j + 2)
                for c in range(max(1, 2 * j), min(2 * j + 2, C - 1)):
                    n = add_count(S_POST2, c)
                    dve.wait_ge(sq_ready, square_count(S_POST2, c))
                    dve.wait_ge(sq_added, n - 1)
                    dve.tensor_tensor(sumsq[:, :], sumsq[:, :], sq[n % 2][:, :], ALU.add).then_inc(sq_added, 1)
            dve.wait_ge(rstd_ready, R_POST2 + 1)
            for c in range(C):
                if c % 2 == 0:
                    dve.tensor_tensor(tmp[0][:, :], ypost[:, c, :], rstd[:, :], ALU.mult).then_inc(scaled, 1)
                    dve.wait_ge(scaled, c // 2 + 1)
                else:
                    dve.wait_ge(scaled_pool, c // 2 + 1)
                dve.tensor_tensor(x[:, c, :], tmp[c % 2][:, :], x[:, c, :], ALU.add).then_inc(x_ready, 1)
                if c:
                    lo(N_FFN3, named("norm_ffn_pre_g_2"), c - 1)
            lo(N_FFN3, named("norm_ffn_pre_g_2"), C - 1)
            split_unit(U_FFN3 + 1)
            ffn_steps(2, U_FFN3, R_FFN3)

            dve.wait_ge(post_loaded, 16)
            for i in range(TT):
                root = small[:, RT3 + i:RT3 + i + 1]
                dve.wait_ge(y3_sq, 2 * i + 2)
                dve.tensor_tensor(root, small[:, SS + 2 * i:SS + 2 * i + 1], small[:, SS + 2 * i + 1:SS + 2 * i + 2],
                                  ALU.add).then_inc(y3_sum, 1)
                dve.wait_ge(y3_root, 2 * i + 2)
                for half in range(2):
                    cols = slice(T * half, T * half + T)
                    dve.scalar_tensor_tensor(out_tok[:, i, cols], bank[2 * i + half][:, :], root, post_gain[:, cols],
                                             ALU.mult, ALU.mult).then_inc(y3_scaled, 1)
                for half in range(2):
                    cols = slice(T * half, T * half + T)
                    xt = (x_tok_a if i < 2 else x_tok_b)[:, i % 2, cols]
                    dve.wait_ge(y3_scaled, 2 * i + half + 1)
                    dve.tensor_tensor(out_tok[:, i, cols], out_tok[:, i, cols], xt, ALU.add).then_inc(out_ready, 1)


INPUTS = ["x", "mem", "ffn1_norm", "ffn1_gate", "ffn1_up", "ffn1_down", "mix_norm", "w_in", "lb_param",
          "hgrn_out_norm", "conv_w", "w_out", "xattn_norm", "mem_norm", "w_q_mem", "w_kv_mem", "w_o_mem",
          "ffn2_norm", "ffn2_gate", "ffn2_up", "ffn2_down", "final_norm", "norm_mix_pre_g_2", "w_in_2",
          "w_branch_a_2", "w_branch_b_2", "lam_q1_2", "lam_k1_2", "lam_q2_2", "lam_k2_2", "diff_subln_g_2",
          "w_out_2", "norm_mix_post_g_2", "norm_ffn_pre_g_2", "w_gate_2", "w_up_2", "w_down_2",
          "norm_ffn_post_g_2"]


def kernel(**inputs):
    import numpy as np
    import concourse.bacc as bacc
    from concourse.bass_utils import run_bass_kernel_spmd

    nc = bacc.Bacc("TRN2", target_bir_lowering=False, num_devices=1)
    arrays, aps = {}, {}
    for name in INPUTS:
        v = np.ascontiguousarray(inputs[name])
        arrays[f"in_{name}"] = v
        aps[name] = nc.dram_tensor(f"in_{name}", v.shape, mybir.dt.from_np(v.dtype), kind="ExternalInput").ap()
    out = nc.dram_tensor("out_dram", (1, T, D), F32, kind="ExternalOutput").ap()
    two_blocks(nc, aps, out)
    r = run_bass_kernel_spmd(nc, [arrays], core_ids=[0])
    return r.results[0]["out_dram"]
```
